# Optimizing a Trainium2 kernel written in Bass

```python
import jax, jax.numpy as jnp
from jax import lax
import numpy as np
import math
import jax
import jax.numpy as jnp

D_MODEL = 1024
BATCH = 1
SEQ = 256
DEPTH = 2

N_EVEN = (DEPTH + 1) // 2
N_ODD = DEPTH // 2
D_FF = 2816
NORM_EPS = 1e-6

ATTN_HEADS = 8
HEAD_DIM = 64
ATTN_WIDTH = ATTN_HEADS * HEAD_DIM
ROT_DIM = HEAD_DIM // 4
ROPE_THETA = 500000.0
MOBA_BLOCK = 256
MOBA_TOPK = 3
MOBA_Q_CHUNK = 32

LRU_WIDTH = 512
LRU_HEADS = 8
LRU_HEAD_DIM = LRU_WIDTH // LRU_HEADS
LRU_CONV = 4
LRU_C = 8.0

AB_IN = 3 * ATTN_WIDTH + 2 * LRU_WIDTH
AB_OUT = ATTN_WIDTH + LRU_WIDTH

SC_WIDTH = D_MODEL
SC_CONV = 3


def rms_norm(x, g):
    xf = x.astype(jnp.float32)
    y = xf * lax.rsqrt(jnp.mean(xf * xf, axis=-1, keepdims=True) + NORM_EPS) * g.astype(jnp.float32)
    return y.astype(x.dtype)

def swiglu(h, w_gate, w_up, w_down):
    return (jax.nn.silu(h @ w_gate) * (h @ w_up)) @ w_down

def causal_depthwise_conv(x, w):
    k, c = w.shape
    return lax.conv_general_dilated(
        x, w[:, None, :].astype(x.dtype), window_strides=(1,), padding=[(k - 1, 0)],
        dimension_numbers=("NWC", "WIO", "NWC"), feature_group_count=c)

def partial_rope(x, pos):
    half = ROT_DIM // 2
    inv_freq = ROPE_THETA ** (-jnp.arange(0, ROT_DIM, 2, dtype=jnp.float32) / ROT_DIM)
    ang = pos[:, None] * inv_freq[None, :]
    cos = jnp.cos(ang)[None, :, None, :]
    sin = jnp.sin(ang)[None, :, None, :]
    xf = x.astype(jnp.float32)
    x1, x2, rest = xf[..., :half], xf[..., half:ROT_DIM], xf[..., ROT_DIM:]
    out = jnp.concatenate([x1 * cos - x2 * sin, x2 * cos + x1 * sin, rest], axis=-1)
    return out.astype(x.dtype)

def moba_attention(q, k, v):
    b, s, h, hd = q.shape
    n_blk = -(-s // MOBA_BLOCK)
    sp = n_blk * MOBA_BLOCK
    pad = ((0, 0), (0, sp - s), (0, 0), (0, 0))
    qt = jnp.pad(q, pad).transpose(0, 2, 1, 3)
    kt = jnp.pad(k, pad).transpose(0, 2, 1, 3)
    vt = jnp.pad(v, pad).transpose(0, 2, 1, 3)
    kb = kt.reshape(b, h, n_blk, MOBA_BLOCK, hd)
    vb = vt.reshape(b, h, n_blk, MOBA_BLOCK, hd)
    kmean = jnp.mean(kb.astype(jnp.float32), axis=3)
    n_sel = min(MOBA_TOPK, n_blk - 1)
    scale = hd ** -0.5
    blk_ids = jnp.arange(n_blk)
    bi = jnp.arange(b)[:, None, None]
    hi = jnp.arange(h)[None, :, None]
    neg = jnp.float32(-1e30)

    def chunk(c):
        start = c * MOBA_Q_CHUNK
        own = start // MOBA_BLOCK
        qc = lax.dynamic_slice_in_dim(qt, start, MOBA_Q_CHUNK, axis=2)
        qpos = start + jnp.arange(MOBA_Q_CHUNK)
        k_own = lax.dynamic_index_in_dim(kb, own, axis=2, keepdims=False)
        v_own = lax.dynamic_index_in_dim(vb, own, axis=2, keepdims=False)
        kpos = own * MOBA_BLOCK + jnp.arange(MOBA_BLOCK)
        s_own = jnp.einsum("bhqd,bhkd->bhqk", qc, k_own).astype(jnp.float32) * scale
        s_own = jnp.where(kpos[None, :] <= qpos[:, None], s_own, neg)
        logits = [s_own]
        vals = [v_own]
        if n_sel > 0:
            g = jnp.einsum("bhqd,bhnd->bhqn", qc.astype(jnp.float32), kmean)
            g = jnp.where(blk_ids < own, g, neg)
            _, idx = lax.top_k(g, n_sel)
            valid = idx < own
            for j in range(n_sel):
                ks = kb[bi, hi, idx[..., j]]
                vs = vb[bi, hi, idx[..., j]]
                sj = jnp.einsum("bhqd,bhqkd->bhqk", qc, ks).astype(jnp.float32) * scale
                logits.append(jnp.where(valid[..., j][..., None], sj, neg))
                vals.append(vs)
        p = jax.nn.softmax(jnp.concatenate(logits, axis=-1), axis=-1)
        p = p.astype(v.dtype)
        out = jnp.einsum("bhqk,bhkd->bhqd", p[..., :MOBA_BLOCK], vals[0])
        for j in range(1, n_sel + 1):
            pj = p[..., j * MOBA_BLOCK:(j + 1) * MOBA_BLOCK]
            out = out + jnp.einsum("bhqk,bhqkd->bhqd", pj, vals[j])
        return out

    outs = lax.map(chunk, jnp.arange(sp // MOBA_Q_CHUNK))
    outs = outs.transpose(1, 0, 3, 2, 4).reshape(b, sp, h, hd)[:, :s]
    return outs.reshape(b, s, h * hd)

def rg_lru(xc, wa, ba, wx, bx, lam):
    b, s, w = xc.shape
    xf = xc.astype(jnp.float32).reshape(b, s, LRU_HEADS, LRU_HEAD_DIM)
    r = jax.nn.sigmoid(jnp.einsum("bshi,hij->bshj", xf, wa.astype(jnp.float32)) + ba.astype(jnp.float32))
    i = jax.nn.sigmoid(jnp.einsum("bshi,hij->bshj", xf, wx.astype(jnp.float32)) + bx.astype(jnp.float32))
    log_a = -LRU_C * r * jax.nn.softplus(-lam.astype(jnp.float32)).reshape(LRU_HEADS, LRU_HEAD_DIM)
    a = jnp.exp(log_a)
    u = jnp.sqrt(-jnp.expm1(2.0 * log_a)) * (i * xf)
    a = a.reshape(b, s, w)
    u = u.reshape(b, s, w)

    def combine(e1, e2):
        a1, u1 = e1
        a2, u2 = e2
        return a1 * a2, a2 * u1 + u2

    _, hseq = lax.associative_scan(combine, (a, u), axis=1)
    return hseq.astype(xc.dtype)

def first_inputs(seed: int = 0) -> dict:
    key = jax.random.key(seed)
    ks = jax.random.split(key, 24)
    f32 = jnp.float32

    def nrm(k, shape, fan_in):
        return jax.random.normal(k, shape, f32) * (fan_in ** -0.5)

    x = jax.random.normal(ks[0], (BATCH, SEQ, D_MODEL), f32)
    ffn1_w_gate = nrm(ks[1], (DEPTH, D_MODEL, D_FF), D_MODEL)
    ffn1_w_up = nrm(ks[2], (DEPTH, D_MODEL, D_FF), D_MODEL)
    ffn1_w_down = nrm(ks[3], (DEPTH, D_FF, D_MODEL), D_FF)
    ffn2_w_gate = nrm(ks[4], (DEPTH, D_MODEL, D_FF), D_MODEL)
    ffn2_w_up = nrm(ks[5], (DEPTH, D_MODEL, D_FF), D_MODEL)
    ffn2_w_down = nrm(ks[6], (DEPTH, D_FF, D_MODEL), D_FF)
    norm_pre = 1.0 + 0.05 * jax.random.normal(ks[7], (DEPTH, 3, D_MODEL), f32)
    norm_post = 1.0 + 0.05 * jax.random.normal(ks[8], (DEPTH, 3, D_MODEL), f32)
    ab_w_in = nrm(ks[9], (N_EVEN, D_MODEL, AB_IN), D_MODEL)
    ab_w_out = nrm(ks[10], (N_EVEN, AB_OUT, D_MODEL), AB_OUT)
    lru_conv_w = nrm(ks[11], (N_EVEN, LRU_CONV, LRU_WIDTH), LRU_CONV)
    lru_conv_b = 0.01 * jax.random.normal(ks[12], (N_EVEN, LRU_WIDTH), f32)
    lru_gate_a_w = nrm(ks[13], (N_EVEN, LRU_HEADS, LRU_HEAD_DIM, LRU_HEAD_DIM), LRU_HEAD_DIM)
    lru_gate_a_b = 0.01 * jax.random.normal(ks[14], (N_EVEN, LRU_HEADS, LRU_HEAD_DIM), f32)
    lru_gate_x_w = nrm(ks[15], (N_EVEN, LRU_HEADS, LRU_HEAD_DIM, LRU_HEAD_DIM), LRU_HEAD_DIM)
    lru_gate_x_b = 0.01 * jax.random.normal(ks[16], (N_EVEN, LRU_HEADS, LRU_HEAD_DIM), f32)
    a_c = jax.random.uniform(ks[17], (N_EVEN, LRU_WIDTH), f32, 0.9, 0.999)
    a0 = a_c ** (1.0 / LRU_C)
    lru_lambda = jnp.log(a0) - jnp.log1p(-a0)
    c_w_in = nrm(ks[18], (N_ODD, D_MODEL, 3 * SC_WIDTH), D_MODEL)
    c_conv_w = nrm(ks[19], (N_ODD, SC_CONV, SC_WIDTH), SC_CONV)
    c_w_out = nrm(ks[20], (N_ODD, SC_WIDTH, D_MODEL), SC_WIDTH)
    return {
        "x": x,
        "ffn1_w_gate": ffn1_w_gate, "ffn1_w_up": ffn1_w_up, "ffn1_w_down": ffn1_w_down,
        "ffn2_w_gate": ffn2_w_gate, "ffn2_w_up": ffn2_w_up, "ffn2_w_down": ffn2_w_down,
        "norm_pre": norm_pre, "norm_post": norm_post,
        "ab_w_in": ab_w_in, "ab_w_out": ab_w_out,
        "lru_conv_w": lru_conv_w, "lru_conv_b": lru_conv_b,
        "lru_gate_a_w": lru_gate_a_w, "lru_gate_a_b": lru_gate_a_b,
        "lru_gate_x_w": lru_gate_x_w, "lru_gate_x_b": lru_gate_x_b,
        "lru_lambda": lru_lambda,
        "c_w_in": c_w_in, "c_conv_w": c_conv_w, "c_w_out": c_w_out,
    }

def first_block(x, ffn1_w_gate, ffn1_w_up, ffn1_w_down, ffn2_w_gate, ffn2_w_up, ffn2_w_down,
              norm_pre, norm_post, ab_w_in, ab_w_out, lru_conv_w, lru_conv_b,
              lru_gate_a_w, lru_gate_a_b, lru_gate_x_w, lru_gate_x_b, lru_lambda,
              c_w_in, c_conv_w, c_w_out):
    b, s, d = x.shape
    pos = jnp.arange(s, dtype=jnp.float32)
    for l in range(DEPTH):
        hdn = swiglu(rms_norm(x, norm_pre[l, 0]), ffn1_w_gate[l], ffn1_w_up[l], ffn1_w_down[l])
        x = x + 0.5 * rms_norm(hdn, norm_post[l, 0])

        h = rms_norm(x, norm_pre[l, 1])
        if l % 2 == 0:
            e = l // 2
            p = h @ ab_w_in[e]
            q = p[..., :ATTN_WIDTH].reshape(b, s, ATTN_HEADS, HEAD_DIM)
            k = p[..., ATTN_WIDTH:2 * ATTN_WIDTH].reshape(b, s, ATTN_HEADS, HEAD_DIM)
            v = p[..., 2 * ATTN_WIDTH:3 * ATTN_WIDTH].reshape(b, s, ATTN_HEADS, HEAD_DIM)
            lru_x = p[..., 3 * ATTN_WIDTH:3 * ATTN_WIDTH + LRU_WIDTH]
            lru_g = p[..., 3 * ATTN_WIDTH + LRU_WIDTH:]
            attn = moba_attention(partial_rope(q, pos), partial_rope(k, pos), v)
            xc = causal_depthwise_conv(lru_x, lru_conv_w[e]) + lru_conv_b[e]
            rec = rg_lru(xc, lru_gate_a_w[e], lru_gate_a_b[e], lru_gate_x_w[e], lru_gate_x_b[e],
                         lru_lambda[e]) * jax.nn.gelu(lru_g)
            mix = jnp.concatenate([attn, rec], axis=-1) @ ab_w_out[e]
        else:
            o = l // 2
            p = h @ c_w_in[o]
            gate_b = p[..., :SC_WIDTH]
            gate_c = p[..., SC_WIDTH:2 * SC_WIDTH]
            xt = p[..., 2 * SC_WIDTH:]
            mix = (gate_b * causal_depthwise_conv(gate_c * xt, c_conv_w[o])) @ c_w_out[o]
        x = x + rms_norm(mix, norm_post[l, 1])

        hdn = swiglu(rms_norm(x, norm_pre[l, 2]), ffn2_w_gate[l], ffn2_w_up[l], ffn2_w_down[l])
        x = x + 0.5 * rms_norm(hdn, norm_post[l, 2])
    return x


DEPTH_2 = 1

GRID_W = 64
CTX_LEN = 256
MIX_WIDTH = D_MODEL
FOURIER_HEAD_DIM = 64
FOURIER_WIDTH = MIX_WIDTH // 4
FOURIER_HEADS = FOURIER_WIDTH // FOURIER_HEAD_DIM
SSD_WIDTH = MIX_WIDTH - FOURIER_WIDTH
SSD_HEAD_DIM = 64
SSD_HEADS = SSD_WIDTH // SSD_HEAD_DIM
SSD_GROUPS = 4
SSD_STATE = 128
GROUP_STATE = SSD_GROUPS * SSD_STATE
CONV_WIDTH = 3
CHUNK = 128
N_MOD = 9
MACARON_WEIGHT = 0.5
EPS = 1e-6
CONV_DIM = GROUP_STATE + SSD_WIDTH + GROUP_STATE
PROJ_WIDTH = FOURIER_WIDTH + SSD_WIDTH + CONV_DIM + 2 * SSD_HEADS


def rms_norm_2(x, g):
    x32 = x.astype(jnp.float32)
    y = x32 * lax.rsqrt(jnp.mean(x32 * x32, axis=-1, keepdims=True) + EPS)
    return (y * g.astype(jnp.float32)).astype(x.dtype)

def modulate(h, shift, scale):
    return h * (1 + scale[:, None, :]) + shift[:, None, :]

def macaron_ffn(x, mod3, norm_pre, norm_post, w_gate, w_up, w_down):
    h = modulate(rms_norm_2(x, norm_pre), mod3[:, 0], mod3[:, 1])
    y = (jax.nn.silu(h @ w_gate) * (h @ w_up)) @ w_down
    return x + MACARON_WEIGHT * mod3[:, 2][:, None, :] * rms_norm_2(y, norm_post)

def centred_dwconv_silu(u, w, b):
    out = lax.conv_general_dilated(u, w[:, None, :], (1,), 'SAME',
                                   dimension_numbers=('NWC', 'WIO', 'NWC'),
                                   feature_group_count=u.shape[-1])
    return jax.nn.silu(out + b)

def softplus_dt(dt_raw, dt_bias):
    b, L = dt_raw.shape[:2]
    return jax.nn.softplus(dt_raw.astype(jnp.float32).reshape(b, L, 2, SSD_HEADS)
                           + dt_bias.astype(jnp.float32))

def flip(t):
    return jnp.flip(t, axis=1)

def fourier_mix(u, fourier_w):
    b, L, _ = u.shape
    uh = u.reshape(b, L, FOURIER_HEADS, FOURIER_HEAD_DIM).astype(jnp.float32)
    f = jnp.fft.fft2(uh, axes=(1, 3), norm='ortho').real.astype(u.dtype)
    return jnp.einsum('blhd,hde->blhe', f, fourier_w).reshape(b, L, FOURIER_WIDTH)

def ssd_chunked(xs, dt, a, bm, cm, h0):
    b, L = xs.shape[:2]
    nc = L // CHUNK
    R = SSD_HEADS // SSD_GROUPS
    xdt = (xs * dt[..., None]).reshape(b, nc, CHUNK, SSD_GROUPS, R, SSD_HEAD_DIM)
    a_cs = jnp.cumsum(jnp.transpose((dt * a).reshape(b, nc, CHUNK, SSD_GROUPS, R), (0, 1, 3, 4, 2)), axis=-1)
    bc = bm.reshape(b, nc, CHUNK, SSD_GROUPS, SSD_STATE)
    cc = cm.reshape(b, nc, CHUNK, SSD_GROUPS, SSD_STATE)
    lower = jnp.tril(jnp.ones((CHUNK, CHUNK), dtype=bool))
    seg = jnp.exp(jnp.where(lower, a_cs[..., :, None] - a_cs[..., None, :], -jnp.inf))
    cb = jnp.einsum('bclgn,bcsgn->bcgls', cc, bc)
    y_diag = jnp.einsum('bcgls,bcgrls,bcsgrp->bclgrp', cb, seg, xdt)
    states = jnp.einsum('bcsgn,bcgrs,bcsgrp->bcgrpn', bc, jnp.exp(a_cs[..., -1:] - a_cs), xdt)

    def step(h, inp):
        s, d = inp
        return h * d[..., None, None] + s, h

    h_last, h_prev = lax.scan(step, h0.reshape(b, SSD_GROUPS, R, SSD_HEAD_DIM, SSD_STATE),
                              (jnp.moveaxis(states, 1, 0), jnp.moveaxis(jnp.exp(a_cs[..., -1]), 1, 0)))
    y_off = jnp.einsum('bclgn,cbgrpn,bcgrl->bclgrp', cc, h_prev, jnp.exp(a_cs))
    y = (y_diag + y_off).reshape(b, L, SSD_HEADS, SSD_HEAD_DIM)
    return y, h_last.reshape(b, SSD_HEADS, SSD_HEAD_DIM, SSD_STATE)

def ssd_final_state(xs, dt, a, bm):
    b, L = xs.shape[:2]
    R = SSD_HEADS // SSD_GROUPS
    cs = jnp.cumsum(dt * a, axis=1)
    xdt = (xs * (dt * jnp.exp(cs[:, -1:] - cs))[..., None]).reshape(b, L, SSD_GROUPS, R, SSD_HEAD_DIM)
    return jnp.einsum('blgn,blgrp->bgrpn', bm, xdt).reshape(b, SSD_HEADS, SSD_HEAD_DIM, SSD_STATE)

def mix_sublayer(x, mod3, h0_f, h0_b, norm_pre, norm_post, w_in, fourier_w, conv_w, conv_b,
                 dt_bias, a_log, d_skip, ssd_norm, w_out):
    b, L, _ = x.shape
    h = modulate(rms_norm_2(x, norm_pre), mod3[:, 0], mod3[:, 1])
    u_f, z, xbc, dt_raw = jnp.split(h @ w_in, [FOURIER_WIDTH, FOURIER_WIDTH + SSD_WIDTH,
                                               FOURIER_WIDTH + SSD_WIDTH + CONV_DIM], axis=-1)
    xbc = centred_dwconv_silu(xbc, conv_w, conv_b)
    cm, xs, bm = jnp.split(xbc, [GROUP_STATE, GROUP_STATE + SSD_WIDTH], axis=-1)
    xs = xs.reshape(b, L, SSD_HEADS, SSD_HEAD_DIM)
    bm = bm.reshape(b, L, SSD_GROUPS, SSD_STATE)
    cm = cm.reshape(b, L, SSD_GROUPS, SSD_STATE)
    dt = softplus_dt(dt_raw, dt_bias)
    a = -jnp.exp(a_log.astype(jnp.float32))
    y_f, h_f = ssd_chunked(xs, dt[:, :, 0], a[0], bm, cm, h0_f)
    y_b, h_b = ssd_chunked(flip(xs), flip(dt[:, :, 1]), a[1], flip(bm), flip(cm), h0_b)
    y = y_f + flip(y_b) + d_skip.astype(jnp.float32)[:, None] * xs
    y = y.reshape(b, L, SSD_WIDTH).astype(x.dtype) * jax.nn.silu(z)
    y = rms_norm_2(y.reshape(b, L, SSD_GROUPS, SSD_WIDTH // SSD_GROUPS),
                 ssd_norm.reshape(SSD_GROUPS, SSD_WIDTH // SSD_GROUPS)).reshape(b, L, SSD_WIDTH)
    out = jnp.concatenate([fourier_mix(u_f, fourier_w), y], axis=-1) @ w_out
    return x + mod3[:, 2][:, None, :] * rms_norm_2(out, norm_post), h_f, h_b

def context_states(ctx, mod3, norm_pre, w_in, conv_w, conv_b, dt_bias, a_log):
    b, L, _ = ctx.shape
    h = modulate(rms_norm_2(ctx, norm_pre), mod3[:, 0], mod3[:, 1])
    xb, dt_raw = jnp.split(h @ w_in[:, FOURIER_WIDTH + SSD_WIDTH + GROUP_STATE:],
                           [SSD_WIDTH + GROUP_STATE], axis=-1)
    xb = centred_dwconv_silu(xb, conv_w[:, GROUP_STATE:], conv_b[GROUP_STATE:])
    xs, bm = jnp.split(xb, [SSD_WIDTH], axis=-1)
    xs = xs.reshape(b, L, SSD_HEADS, SSD_HEAD_DIM)
    bm = bm.reshape(b, L, SSD_GROUPS, SSD_STATE)
    dt = softplus_dt(dt_raw, dt_bias)
    a = -jnp.exp(a_log.astype(jnp.float32))
    h_f = ssd_final_state(xs, dt[:, :, 0], a[0], bm)
    h_b = ssd_final_state(flip(xs), flip(dt[:, :, 1]), a[1], flip(bm))
    return h_f, h_b

def second_inputs(seed: int = 0) -> dict:
    key = jax.random.key(seed)
    ks = iter(jax.random.split(key, 32))
    f32 = jnp.float32
    L = DEPTH_2

    def normal(shape, scale=1.0):
        return scale * jax.random.normal(next(ks), shape, f32)

    def gain(shape):
        return 1.0 + 0.1 * jax.random.normal(next(ks), shape, f32)

    d = {}
    d['x'] = normal((BATCH, SEQ, D_MODEL))
    d['c'] = normal((BATCH, D_MODEL))
    d['ctx'] = normal((BATCH, CTX_LEN, D_MODEL))
    d['c_ctx'] = normal((D_MODEL,))
    d['ada_w'] = normal((L, D_MODEL, N_MOD * D_MODEL), D_MODEL ** -0.5)
    d['ada_b'] = normal((L, N_MOD * D_MODEL), 0.02)
    d['ffn1_norm_pre'] = gain((L, D_MODEL))
    d['ffn1_norm_post'] = gain((L, D_MODEL))
    d['ffn1_w_gate'] = normal((L, D_MODEL, D_FF), D_MODEL ** -0.5)
    d['ffn1_w_up'] = normal((L, D_MODEL, D_FF), D_MODEL ** -0.5)
    d['ffn1_w_down'] = normal((L, D_FF, D_MODEL), D_FF ** -0.5)
    d['mix_norm_pre'] = gain((L, D_MODEL))
    d['mix_norm_post'] = gain((L, D_MODEL))
    d['w_in'] = normal((L, D_MODEL, PROJ_WIDTH), D_MODEL ** -0.5)
    d['fourier_w'] = normal((L, FOURIER_HEADS, FOURIER_HEAD_DIM, FOURIER_HEAD_DIM), FOURIER_HEAD_DIM ** -0.5)
    d['conv_w'] = normal((L, CONV_WIDTH, CONV_DIM), CONV_WIDTH ** -0.5)
    d['conv_b'] = normal((L, CONV_DIM), 0.02)
    dt_init = jnp.exp(jax.random.uniform(next(ks), (L, 2, SSD_HEADS), f32, math.log(1e-3), math.log(1e-1)))
    d['dt_bias'] = dt_init + jnp.log(-jnp.expm1(-dt_init))
    d['a_log'] = jnp.log(jax.random.uniform(next(ks), (L, 2, SSD_HEADS), f32, 1.0, 16.0))
    d['d_skip'] = gain((L, SSD_HEADS))
    d['ssd_norm'] = gain((L, SSD_WIDTH))
    d['w_out'] = normal((L, MIX_WIDTH, D_MODEL), MIX_WIDTH ** -0.5)
    d['ffn2_norm_pre'] = gain((L, D_MODEL))
    d['ffn2_norm_post'] = gain((L, D_MODEL))
    d['ffn2_w_gate'] = normal((L, D_MODEL, D_FF), D_MODEL ** -0.5)
    d['ffn2_w_up'] = normal((L, D_MODEL, D_FF), D_MODEL ** -0.5)
    d['ffn2_w_down'] = normal((L, D_FF, D_MODEL), D_FF ** -0.5)
    return d

def second_block(x, c, ctx, c_ctx, ada_w, ada_b, ffn1_norm_pre, ffn1_norm_post, ffn1_w_gate, ffn1_w_up,
              ffn1_w_down, mix_norm_pre, mix_norm_post, w_in, fourier_w, conv_w, conv_b, dt_bias, a_log,
              d_skip, ssd_norm, w_out, ffn2_norm_pre, ffn2_norm_post, ffn2_w_gate, ffn2_w_up, ffn2_w_down):
    b = x.shape[0]
    for layer in range(DEPTH_2):
        mod = (jax.nn.silu(c) @ ada_w[layer] + ada_b[layer]).reshape(b, N_MOD, D_MODEL)
        mod_ctx = (jax.nn.silu(c_ctx) @ ada_w[layer] + ada_b[layer]).reshape(1, N_MOD, D_MODEL)
        ffn1 = (ffn1_norm_pre[layer], ffn1_norm_post[layer], ffn1_w_gate[layer], ffn1_w_up[layer], ffn1_w_down[layer])
        ffn2 = (ffn2_norm_pre[layer], ffn2_norm_post[layer], ffn2_w_gate[layer], ffn2_w_up[layer], ffn2_w_down[layer])
        mix = (mix_norm_pre[layer], mix_norm_post[layer], w_in[layer], fourier_w[layer], conv_w[layer],
               conv_b[layer], dt_bias[layer], a_log[layer], d_skip[layer], ssd_norm[layer], w_out[layer])

        x = macaron_ffn(x, mod[:, 0:3], *ffn1)
        ctx = macaron_ffn(ctx, mod_ctx[:, 0:3], *ffn1)

        if layer + 1 < DEPTH_2:
            zeros = jnp.zeros((b, SSD_HEADS, SSD_HEAD_DIM, SSD_STATE), jnp.float32)
            ctx, h_ctx_f, h_ctx_b = mix_sublayer(ctx, mod_ctx[:, 3:6], zeros, zeros, *mix)
        else:
            h_ctx_f, h_ctx_b = context_states(ctx, mod_ctx[:, 3:6], mix_norm_pre[layer], w_in[layer],
                                              conv_w[layer], conv_b[layer], dt_bias[layer], a_log[layer])

        x, _, _ = mix_sublayer(x, mod[:, 3:6], h_ctx_f, h_ctx_b, *mix)

        x = macaron_ffn(x, mod[:, 6:9], *ffn2)
        if layer + 1 < DEPTH_2:
            ctx = macaron_ffn(ctx, mod_ctx[:, 6:9], *ffn2)
    return x


def setup_inputs(seed=0):
    out = dict(first_inputs(seed))
    for name, value in second_inputs(seed + 1).items():
        if name != "x":
            out[name + "_2"] = value
    return out


def reference(
    x, ffn1_w_gate, ffn1_w_up, ffn1_w_down, ffn2_w_gate, ffn2_w_up, ffn2_w_down, norm_pre,
    norm_post, ab_w_in, ab_w_out, lru_conv_w, lru_conv_b, lru_gate_a_w, lru_gate_a_b,
    lru_gate_x_w, lru_gate_x_b, lru_lambda, c_w_in, c_conv_w, c_w_out, c_2, ctx_2, c_ctx_2,
    ada_w_2, ada_b_2, ffn1_norm_pre_2, ffn1_norm_post_2, ffn1_w_gate_2, ffn1_w_up_2,
    ffn1_w_down_2, mix_norm_pre_2, mix_norm_post_2, w_in_2, fourier_w_2, conv_w_2, conv_b_2,
    dt_bias_2, a_log_2, d_skip_2, ssd_norm_2, w_out_2, ffn2_norm_pre_2, ffn2_norm_post_2,
    ffn2_w_gate_2, ffn2_w_up_2, ffn2_w_down_2,
):
    x = first_block(
        x, ffn1_w_gate, ffn1_w_up, ffn1_w_down, ffn2_w_gate, ffn2_w_up, ffn2_w_down, norm_pre,
        norm_post, ab_w_in, ab_w_out, lru_conv_w, lru_conv_b, lru_gate_a_w, lru_gate_a_b,
        lru_gate_x_w, lru_gate_x_b, lru_lambda, c_w_in, c_conv_w, c_w_out,
    )
    return second_block(
        x, c_2, ctx_2, c_ctx_2, ada_w_2, ada_b_2, ffn1_norm_pre_2, ffn1_norm_post_2,
        ffn1_w_gate_2, ffn1_w_up_2, ffn1_w_down_2, mix_norm_pre_2, mix_norm_post_2, w_in_2,
        fourier_w_2, conv_w_2, conv_b_2, dt_bias_2, a_log_2, d_skip_2, ssd_norm_2, w_out_2,
        ffn2_norm_pre_2, ffn2_norm_post_2, ffn2_w_gate_2, ffn2_w_up_2, ffn2_w_down_2,
    )


_drawn_inputs = setup_inputs


def setup_inputs(seed=0):
    import zlib

    import numpy as np

    out = dict(_drawn_inputs(seed))
    spreads = {}
    factors = {'lru_gate_a_b': 27.893,
     'lru_gate_x_b': 8.0,
     'ctx_2': 35.912,
     'ada_b_2': 3.429,
     'ffn1_norm_pre_2': 2.83,
     'ffn1_norm_post_2': 3.506,
     'conv_b_2': 8.0,
     'd_skip_2': 30.123,
     'ffn2_norm_pre_2': 3.141,
     'ffn2_norm_post_2': 3.976,
     'c_ctx_2': 4.283}
    for name, (base, spread) in spreads.items():
        noise = np.random.default_rng([zlib.crc32(name.encode()), seed]).standard_normal(out[name].shape)
        drawn = base * np.exp(spread * noise) if base else spread * noise
        out[name] = jnp.asarray(drawn.astype(out[name].dtype))
    for name, factor in factors.items():
        out[name] = (out[name] * factor).astype(out[name].dtype)
    return out
```

```python
from contextlib import ExitStack

import numpy as np

import concourse.bass as bass
from concourse import mybir

F32 = mybir.dt.float32
F32R = mybir.dt.float32r
ACT = mybir.ActivationFunctionType
ALU = mybir.AluOpType
AX = mybir.AxisListType

P = 128
D = 1024
KT = D // P
TOK = 256
TT = TOK // P
FF = 2816
FS = 256
STEPS = FF // FS
HEADS, HD = 8, 64
HALF_ROT = HD // 8
LRU_W = 512
LT = LRU_W // P
LRU_CONV = 4
LRU_C = 8.0
SC_CONV = 3
SSD_H, SSD_P = 12, 64
SSD_W = SSD_H * SSD_P
SSD_G = 4
GW = SSD_W // SSD_G
HPG = SSD_H // SSD_G
FOURIER = 256
XBC_T = (512 + SSD_W + 512) // P
CM_T, XS_T, BM_T = 0, 4, 10
NDT = 2 * SSD_H
N_MOD = 9
EPS = 1e-6
SLOT = 1024
RING = 6
SLOTS_FFN = 6 * STEPS
ADA_CH = N_MOD * D // 512

PHASES = [("ada", 4 * ADA_CH), ("ctx_ffn", SLOTS_FFN), ("ctx_mix", 11), ("ffn_0", SLOTS_FFN),
          ("ab", 28), ("ffn_1", SLOTS_FFN), ("ffn_2", SLOTS_FFN), ("sc", 32), ("ffn_3", SLOTS_FFN),
          ("ffn_4", SLOTS_FFN), ("ssd", 31), ("ffn_5", SLOTS_FFN)]
BASE, NSLOT = {}, 0
for _name, _n in PHASES:
    BASE[_name] = NSLOT
    NSLOT += _n
SUB = [name for name, _ in PHASES[1:]]
FFNS = [s for s, name in enumerate(SUB) if "ffn" in name]
WITH_POST = [s for s, name in enumerate(SUB) if name != "ctx_mix"]
MOD = {0: (1, 0, 1, 2), 1: (1, 3, 4, None), 8: (0, 0, 1, 2), 9: (0, 3, 4, 5), 10: (0, 6, 7, 8)}
NORMS = []
for _s in range(len(SUB)):
    NORMS += [("pre", _s, t) for t in range(TT)]
    if _s in WITH_POST:
        NORMS += [("post", _s, t) for t in range(TT)]
NORM_N = {k: i + 1 for i, k in enumerate(NORMS)}

FIRST_N = {}
for _s in range(len(SUB)):
    for _k in (["gu"] if _s in FFNS else []) + (["dn"] if _s in WITH_POST else []):
        FIRST_N[_k, _s] = len(FIRST_N) + 1
LAST = [BASE[name] + dict(PHASES)[name] for name in SUB]
MIX_AB, MIX_SC, MIX_SSD = 3, 2, 5
MIX0 = {"ab": 0, "sc": MIX_AB, "ssd": MIX_AB + MIX_SC}

PRE_DMA_N, POST_DMA_N, PRE_MOD_N, POST_MOD_N = {}, {}, {}, {}
for _s in range(len(SUB)):
    PRE_DMA_N[_s] = PRE_DMA_N.get(_s - 1, 0) + 16 * (3 if _s in MOD else 1)
    PRE_MOD_N[_s] = PRE_MOD_N.get(_s - 1, 0) + (_s in MOD)
    POST_DMA_N[_s] = POST_DMA_N.get(_s - 1, 0) + 16 * ((_s in WITH_POST) + (_s in WITH_POST and _s in MOD))
    POST_MOD_N[_s] = POST_MOD_N.get(_s - 1, 0) + (_s in WITH_POST and _s in MOD)


def build(nc, weights, x_in, ctx_in, pre_rows, post_rows, small, mod, out):
    with ExitStack() as stack:
        def sb(name, shape, dt=F32):
            return stack.enter_context(nc.sbuf_tensor(name, shape, dt))

        def sem(name):
            return stack.enter_context(nc.semaphore(name))

        raw = sb("raw", [P, RING, SLOT])
        w_hi = sb("w_hi", [P, RING, SLOT], F32R)
        w_lo = sb("w_lo", [P, RING, SLOT], F32R)
        hT_hi = sb("hT_hi", [P, KT, TOK], F32R)
        hT_lo = sb("hT_lo", [P, KT, TOK], F32R)
        actT_hi = sb("actT_hi", [P, 2, TOK], F32R)
        actT_lo = sb("actT_lo", [P, 2, TOK], F32R)
        silu = sb("silu", [P, TT, FS])
        act_tok = sb("act_tok", [P, TT, FS])
        x = sb("x", [P, TT, D])
        xn = sb("xn", [P, TT, D])
        pre_row = sb("pre_row", [P, D])
        shift_row = sb("shift_row", [P, D])
        post_row = sb("post_row", [P, D])
        mod_row = sb("mod_row", [P, D])
        ssq = sb("ssq", [P, 4])
        ms = sb("ms", [P, 4])
        rstd = sb("rstd", [P, 4])
        neg_half = sb("neg_half", [P, 8])
        state0 = sb("state0", [P, 2, SSD_G, GW])
        arena = sb("arena", [P, 13580])

        ident = sb("ident", [P, P])
        lru_cols = sb("lru_cols", [P, LT, 8])
        rope = sb("rope", [P, TT, 2, HALF_ROT])
        causal = sb("causal", [P, 3 * P])
        sc_cols = sb("sc_cols", [P, KT, SC_CONV])
        ssd_cols = sb("ssd_cols", [P, XBC_T, 4])
        ssd_rows = sb("ssd_rows", [P, 2 * NDT + SSD_H])
        ssd_norm = sb("ssd_norm", [P, SSD_W])
        tri = sb("tri", [P, 2, TT, TOK])
        dft_l = sb("dft_l", [P, 2, TT, TOK])
        dft_d = sb("dft_d", [P, 2, P])
        fourier_bd = sb("fourier_bd", [P, 2, P])
        c_cols = sb("c_cols", [P, 2, KT])
        silu_c = sb("silu_c", [P, 2, KT])
        dt_tmp = sb("dt_tmp", [P, 6, TT * NDT])
        dt = sb("dt", [P, TT, NDT])
        dta = sb("dta", [P, TT, NDT])
        neg_a = sb("neg_a", [P, NDT])
        pcol = sb("pcol", [P, TT + 1, NDT])
        exp_p = sb("exp_p", [P, TT, NDT])
        prow = sb("prow", [SSD_H, 2, TOK])
        lru_tmp = sb("lru_tmp", [P, 8, LT])
        soft = sb("soft", [P, 4, HEADS, TT])
        gstat = sb("gstat", [P, 3, TT * SSD_G])

        dn = stack.enter_context(nc.psum_tensor("dn", [P, TT, D], F32))
        gu = stack.enter_context(nc.psum_tensor("gu", [P, TT, 512], F32))
        tp = stack.enter_context(nc.psum_tensor("tp", [P, TT, 512], F32))

        def part(at, *shape):
            n = int(np.prod(shape))
            v = arena[:, at:at + n]
            if len(shape) == 2:
                v = v.rearrange("p (a b) -> p a b", a=shape[0])
            elif len(shape) == 3:
                v = v.rearrange("p (a b c) -> p a b c", a=shape[0], b=shape[1])
            return v

        mod_parts = arena[:, 0:3 * 512]
        mod_bias = arena[0:2, 3 * 512:3 * 512 + N_MOD * D]
        mod_out = arena[0:2, 3 * 512 + N_MOD * D:6 * 512 + N_MOD * D]
        comb = arena[:, 6 * 512 + N_MOD * D:6 * 512 + N_MOD * D + P]
        c_split = hT_lo[:, :, 0:P]

        lx = part(0, LT, TOK + LRU_CONV - 1)
        xc = part(1036, LT, TOK)
        gelu = part(2060, LT, TOK)
        rgate = part(3084, LT, TOK)
        igate = part(4108, LT, TOK)
        th = part(5132, LT, TOK)
        decay = part(6156, LT, TOK)
        vtok = part(7180, TT, HEADS * HD)
        qT = part(8204, HEADS // 2, TOK)
        kT = part(9228, HEADS // 2, TOK)
        masked = part(10252, 2, 3 * P)
        expo = part(11020, 2, 3 * P)
        expT = part(11788, 2, 3 * P)
        attn = part(12556, TT, HEADS * HD)
        qk = xn[:, :, :].rearrange("p t (h d) -> p t h d", h=2 * HEADS)
        rope_t = silu[:, :, :].rearrange("p a b -> p (a b)")
        rope_u = act_tok[:, :, :].rearrange("p a b -> p (a b)")

        gate_bd = shift_row[:].rearrange("p (g i c) -> p g i c", g=2, i=LT)

        cgate = part(0, 2, 2 * TOK)
        cx = part(1024, KT, TOK + SC_CONV - 1)
        conv_y = part(1024 + 2064, KT, TOK)

        xbc_in = part(0, XBC_T, TOK + 2)
        xbc = part(3612, XBC_T, TOK)
        y_acc = part(0, TT, SSD_W)
        y_sum = part(1536, TT, SSD_W)
        bm_tok = part(1536, TT, 512)
        f_mid = part(3612 + 1024, 2, 2, TOK)
        f_T = part(3612 + 2048, 2, TOK)
        decays = part(3612 + 1024, 2, 3 * TOK)
        xs_tok = part(7196, TT, SSD_W)
        x_dt = [part(8732, TT, SSD_W), part(10268, TT, SSD_W)]
        cb_m = part(11804, 3 * TOK)
        y_off = part(12572, 2, 3 * 2 * SSD_P)
        u_tok = xn[:, :, 0:FOURIER]
        z_tok = xn[:, :, FOURIER:D]

        landed = [sem(f"landed_{r}") for r in range(RING)]
        hi_ready, lo_ready, slot_used = sem("hi_ready"), sem("lo_ready"), sem("slot_used")
        consts, gate_loaded, ctx_loaded, x_loaded, stored = sem("consts"), sem("gate_loaded"), sem("ctx_loaded"), sem("x_loaded"), sem("stored")
        row_pre, row_post, pre_mod, post_mod = sem("row_pre"), sem("row_post"), sem("pre_mod"), sem("post_mod")
        halves = sem("halves")
        ssq_ready, rstd_ready, x_new, xn_ready = sem("ssq_ready"), sem("rstd_ready"), sem("x_new"), sem("xn_ready")
        hT_psum, hT_hi_ready, hT_lo_ready = sem("hT_psum"), sem("hT_hi_ready"), sem("hT_lo_ready")
        first_tok = sem("first_tok")
        silu_ready, act_ready = sem("silu_ready"), sem("act_ready")
        actT_psum, actT_hi_ready, actT_lo_ready = sem("actT_psum"), sem("actT_hi_ready"), sem("actT_lo_ready")
        dve_step, pool_step = sem("dve_step"), sem("pool_step")
        c_ready, c_split_ready = sem("c_ready"), sem("c_split_ready")
        ada_rows, ada_summed, ada_out, ada_stored = sem("ada_rows"), sem("ada_summed"), sem("ada_out"), sem("ada_stored")
        mixT_psum, mix_hi, mix_lo = sem("mixT_psum"), sem("mix_hi"), sem("mix_lo")
        ab_evac, xc_ready, gates_done, gates_ready = sem("ab_evac"), sem("xc_ready"), sem("gates_done"), sem("gates_ready")
        lam_z, lam_exp, lru_c_ready = sem("lam_z"), sem("lam_exp"), sem("lru_c_ready")
        lru_tanh, lru_decay, lru_ratio, lru_root, rec_ready = sem("lru_tanh"), sem("lru_decay"), sem("lru_ratio"), sem("lru_root"), sem("rec_ready")
        roped, qkT_psum, qkT_ready = sem("roped"), sem("qkT_psum"), sem("qkT_ready")
        scores_done, masked_ready, exp_ready = sem("scores_done"), sem("masked_ready"), sem("exp_ready")
        expT_psum, expT_ready, attn_psum, attn_ready = sem("expT_psum"), sem("expT_ready"), sem("attn_psum"), sem("attn_ready")
        sc_gate, sc_mixed = sem("sc_gate"), sem("sc_mixed")
        dt_z, dt_exp, dta_ready, a_exp = sem("dt_z"), sem("dt_exp"), sem("dta_ready"), sem("a_exp")
        p_psum, p_ready, p_arg, p_exp = sem("p_psum"), sem("p_ready"), sem("p_arg"), sem("p_exp")
        pads, xbc_evac, conv_done, xbc_ready = sem("pads"), sem("xbc_evac"), sem("conv_done"), sem("xbc_ready")
        tokT_psum, tok_ready, xdt_ready = sem("tokT_psum"), sem("tok_ready"), sem("xdt_ready")
        state_psum, state_ready, wide_ready = sem("state_psum"), sem("state_ready"), sem("wide_ready")
        four_psum, four_ready = sem("four_psum"), sem("four_ready")
        yoff_psum, yoff_used, cb_psum, cb_ready = sem("yoff_psum"), sem("yoff_used"), sem("cb_psum"), sem("cb_ready")
        rows_psum, arg_ready, dec_ready, g_ready = sem("rows_psum"), sem("arg_ready"), sem("dec_ready"), sem("g_ready")
        y_psum, gsq_ready, gr_ready, y_ready = sem("y_psum"), sem("gsq_ready"), sem("gr_ready"), sem("y_ready")

        small_tiles = {"ident": ident, "lru_cols": lru_cols, "rope": rope,
                       "causal": causal, "sc_cols": sc_cols, "ssd_cols": ssd_cols, "tri": tri,
                       "dft_l": dft_l, "dft_d": dft_d, "fourier_bd": fourier_bd, "c_cols": c_cols,
                       "comb": comb}
        ALL_CONSTS = 16 * (len(small_tiles) + 3)

        def dn_bank(b):
            return dn[:, b // 2, (b % 2) * 512:(b % 2) * 512 + 512]

        def any_bank(b):
            return dn_bank(b) if b < 4 else gu[:, b - 4, :] if b < 6 else tp[:, b - 6, :]

        block = stack.enter_context(nc.Block())

        @block.sync
        def _(sp):
            def load(n_first, r, it):
                n = n_first + r
                if n >= RING:
                    sp.wait_ge(lo_ready, n - RING + 1 + RING * it)
                sp.dma_start(raw[:, r, :], weights[bass.ts(n + RING * it, P), :]).then_inc(landed[r], 16)

            for r in range(RING):
                load(0, r, 0)
            with sp.Fori(0, NSLOT // RING - 1) as it:
                for r in range(RING):
                    load(RING, r, it)

        def slot_landed(eng, n, it=0):
            eng.wait_ge(landed[n % RING], 16 * (n // RING + 1) + 16 * it)


        @block.tensor
        def _(pe):
            def transposed(s, t):
                pe.wait_ge(xn_ready, TT * s + t + 1)
                if t:
                    pe.wait_ge(hT_lo_ready, 2 * (TT * s + t))
                for half in range(2):
                    for q in range(4):
                        k = 4 * half + q
                        m = pe.transpose(tp[:, half, q * P:(q + 1) * P], xn[:, t, k * P:(k + 1) * P], ident[:])
                    m.then_inc(hT_psum, 1)

            def hT_there(s, t):
                pe.wait_ge(hT_lo_ready, 2 * (TT * s + t) + 2)

            def wide_slot(n, si, tiles, bank, it=0, used=True):
                pe.wait_ge(lo_ready, n + 1 + RING * it)
                r = n % RING
                for kk in range(2):
                    k = 2 * si + kk
                    for t in tiles:
                        for q, (h, w) in enumerate(((hT_hi, w_hi), (hT_lo, w_hi), (hT_hi, w_lo))):
                            m = pe.matmul(bank[:, t, :], h[:, k, t * P:(t + 1) * P],
                                          w[:, r, kk * 512:(kk + 1) * 512],
                                          start=k == 0 and q == 0, stop=k == KT - 1 and q == 2)
                if used:
                    m.then_inc(slot_used, 1)
                return m

            def col_slot(n, o):
                pe.wait_ge(lo_ready, n + 1)
                r = n % RING
                for k in range(KT):
                    for q, (h, w) in enumerate(((hT_hi, w_hi), (hT_lo, w_hi), (hT_hi, w_lo))):
                        m = pe.matmul(o, w[:, r, k * P:(k + 1) * P], h[:, k, :],
                                      start=k == 0 and q == 0, stop=k == KT - 1 and q == 2)
                m.then_inc(slot_used, 1)

            def down_slot(n, a_hi, a_lo, k, tiles, start, stop, it=0, used=True):
                pe.wait_ge(lo_ready, n + 1 + RING * it)
                r = n % RING
                for t in tiles:
                    for half in range(2):
                        c = slice(512 * half, 512 * (half + 1))
                        for q, (a, w) in enumerate(((a_hi, w_hi), (a_lo, w_hi), (a_hi, w_lo))):
                            m = pe.matmul(dn[:, t, c], a[:, k, t * P:(t + 1) * P], w[:, r, c],
                                          start=start and q == 0, stop=stop and q == 2)
                if used:
                    m.then_inc(slot_used, 1)
                return m

            def out_proj(n, order, parts):
                for i, k in enumerate(order):
                    pe.wait_ge(mix_lo, parts[k])
                    if i < KT - 1:
                        down_slot(n + i, hT_hi, hT_lo, k, range(TT), i == 0, False)
                    else:
                        down_slot(n + i, hT_hi, hT_lo, k, [0], False, True, used=False).then_inc(first_tok, 1)
                        down_slot(n + i, hT_hi, hT_lo, k, [1], False, True)

            def ada():
                def chunks(first, it):
                    def product(m):
                        if not first:
                            pe.wait_ge(ada_rows, m + 1 + 3 * it)
                        for si in range(4):
                            n = 4 * m + si + (0 if first else 12)
                            pe.wait_ge(lo_ready, n + 1 + 12 * it)
                            for kk in range(2):
                                k = 2 * si + kk
                                for q, w in enumerate((w_hi, w_lo)):
                                    mm = pe.matmul(dn_bank(m), c_split[:, k, :],
                                                   w[:, n % RING, kk * 512:(kk + 1) * 512],
                                                   start=k == 0 and q == 0, stop=k == KT - 1 and q == 1)
                            mm.then_inc(slot_used, 1)

                    def summed(m):
                        c = m if first else m + 3
                        pe.wait_ge(ada_rows, c + 1 + 3 * it)
                        if not first:
                            pe.wait_ge(ada_out, m + 1 + 3 * it)
                        bank = gu[:, m, :] if m < 2 else tp[:, 0, :]
                        pe.matmul(bank, comb, mod_parts[:, m * 512:(m + 1) * 512],
                                  start=True, stop=True).then_inc(ada_summed, 1)

                    product(0)
                    product(1)
                    summed(0)
                    product(2)
                    summed(1)
                    summed(2)

                chunks(True, 0)
                with pe.Fori(0, ADA_CH // 3 - 1) as it:
                    chunks(False, it)

            def ffn(s, n0):
                c0 = FFNS.index(s) * STEPS

                def act_transposed(c, it=0):
                    pe.wait_ge(act_ready, TT * (c + 1) + TT * it)
                    for t in range(TT):
                        for kk in range(2):
                            m = pe.transpose(tp[:, 0, kk * TOK + t * P:kk * TOK + (t + 1) * P],
                                             act_tok[:, t, kk * P:(kk + 1) * P], ident[:])
                    m.then_inc(actT_psum, 1)

                def step(j, it):
                    n = n0 + 4 + 6 * (j - 1)
                    act_transposed(c0 + j - 1, it)
                    for si in range(4):
                        wide_slot(n + si, si, range(TT), gu, it=it)
                    pe.wait_ge(actT_lo_ready, c0 + j + it)
                    for kk in range(2):
                        down_slot(n + 4 + kk, actT_hi, actT_lo, kk, range(TT), j == 1 and kk == 0, False, it=it)

                transposed(s, 0)
                hT_there(s, 0)
                wide_slot(n0, 0, [0], gu, used=False)
                wide_slot(n0 + 1, 1, [0], gu, used=False)
                transposed(s, 1)
                wide_slot(n0 + 2, 2, [0], gu, used=False)
                wide_slot(n0 + 3, 3, [0], gu, used=False).then_inc(first_tok, 1)
                hT_there(s, 1)
                for si in range(4):
                    wide_slot(n0 + si, si, [1], gu)
                step(1, 0)
                with pe.Fori(0, STEPS - 3) as it:
                    step(2, it)
                step(STEPS - 1, 0)
                act_transposed(c0 + STEPS - 1)
                pe.wait_ge(actT_lo_ready, c0 + STEPS)
                n = n0 + 4 + 6 * (STEPS - 1)
                down_slot(n, actT_hi, actT_lo, 0, [0], False, False, used=False)
                down_slot(n + 1, actT_hi, actT_lo, 1, [0], False, True, used=False).then_inc(first_tok, 1)
                down_slot(n, actT_hi, actT_lo, 0, [1], False, False)
                down_slot(n + 1, actT_hi, actT_lo, 1, [1], False, True)

            def ab(s, n0):
                for t in range(TT):
                    transposed(s, t)
                hT_there(s, 1)
                for i in range(LT):
                    col_slot(n0 + i, dn[:, 0, i * TOK:(i + 1) * TOK])
                for i in range(LT):
                    col_slot(n0 + LT + i, dn[:, 1, i * TOK:(i + 1) * TOK])
                for si in range(4):
                    wide_slot(n0 + 8 + si, si, range(TT), gu)
                for si in range(4):
                    wide_slot(n0 + 12 + si, si, range(TT), tp)
                pe.wait_ge(xc_ready, 1)
                pe.wait_ge(gate_loaded, 16)
                pe.wait_ge(ab_evac, 4)
                for gate in range(2):
                    for i in range(LT):
                        m = pe.matmul(dn[:, gate, i * TOK:(i + 1) * TOK], gate_bd[:, gate, i, :], xc[:, i, :],
                                      start=True, stop=True)
                    m.then_inc(gates_done, 1)
                pe.wait_ge(ab_evac, 6)
                for si in range(4):
                    wide_slot(n0 + 16 + si, si, range(TT), gu)
                pe.wait_ge(roped, 1)
                for which, bank in ((0, tp), (1, gu)):
                    if which:
                        pe.wait_ge(ab_evac, 10)
                    for half in range(2):
                        for pair in range(2):
                            for t in range(TT):
                                h = 8 * which + 2 * (2 * half + pair)
                                m = pe.transpose(bank[:, half, pair * TOK + t * P:pair * TOK + (t + 1) * P],
                                                 qk[:, t, h:h + 2, :].rearrange("p h d -> p (h d)"), ident[:])
                        m.then_inc(qkT_psum, 1)

                def scores(h):
                    bank = (gu, tp)[(h // 2) % 2][:, h % 2, :]
                    rows = slice(HD * (h % 2), HD * (h % 2) + HD)
                    pe.wait_ge(masked_ready, 3 * (h - 4) + 2) if h >= 4 else pe.wait_ge(qkT_ready, 4)
                    pe.matmul(bank[:, 0:P], qT[rows, h // 2, 0:P], kT[rows, h // 2, 0:P], start=True, stop=True)
                    pe.matmul(bank[:, P:P + TOK], qT[rows, h // 2, P:TOK], kT[rows, h // 2, :],
                              start=True, stop=True).then_inc(scores_done, 1)

                def weighted(h):
                    pe.wait_ge(expT_ready, h + 1)
                    eT, v = expT[:, h % 2, :], slice(h * HD, (h + 1) * HD)
                    pe.matmul(dn[:, 1, v], eT[:, 0:P], vtok[:, 0, v], start=True, stop=True)
                    pe.matmul(dn[:, 1, 512 + h * HD:512 + (h + 1) * HD], eT[:, P:2 * P], vtok[:, 0, v],
                              start=True, stop=False)
                    m = pe.matmul(dn[:, 1, 512 + h * HD:512 + (h + 1) * HD], eT[:, 2 * P:3 * P], vtok[:, 1, v],
                                  start=False, stop=True)
                    if h == HEADS - 1:
                        m.then_inc(attn_psum, 1)

                for h in range(4):
                    scores(h)
                pe.wait_ge(gates_ready, 2 * LT)
                for h in range(HEADS):
                    pe.wait_ge(exp_ready, h + 1)
                    if h >= 2:
                        pe.wait_ge(expT_ready, h - 1)
                    for q in range(3):
                        m = pe.transpose(dn[:, 0, (h % 2) * 512 + q * P:(h % 2) * 512 + (q + 1) * P],
                                         expo[:, h % 2, q * P:(q + 1) * P], ident[:])
                    m.then_inc(expT_psum, 1)
                    if h + 4 < HEADS:
                        scores(h + 4)
                    if h:
                        weighted(h - 1)
                weighted(HEADS - 1)
                pe.wait_ge(attn_ready, 1)
                for t in range(TT):
                    for k in range(4):
                        m = pe.transpose(tp[:, t, k * P:(k + 1) * P], attn[:, t, k * P:(k + 1) * P], ident[:])
                    m.then_inc(mixT_psum, 1)
                out_proj(n0 + 20, [4, 5, 6, 7, 0, 1, 2, 3], [MIX0["ab"] + MIX_AB] * 4 + [MIX0["ab"] + MIX_AB] * 4)

            def sc(s, n0):
                for t in range(TT):
                    transposed(s, t)
                hT_there(s, 1)
                for q in range(3 * KT):
                    if q >= 8:
                        i, kind = (q - 8) // 3, (q - 8) % 3
                        if kind == 0:
                            pe.wait_ge(sc_gate, i + 1)
                        else:
                            pe.wait_ge(sc_mixed, 2 * i + kind)
                    col_slot(n0 + q, any_bank(q % 8)[:, 0:TOK])
                out_proj(n0 + 3 * KT, range(KT), [MIX0["sc"] + 1] * 4 + [MIX0["sc"] + 2] * 4)

            def dt_slot(n):
                pe.wait_ge(lo_ready, n + 1)
                r = n % RING
                for t in range(TT):
                    for k in range(KT):
                        for q, (h, w) in enumerate(((hT_hi, w_hi), (hT_lo, w_hi), (hT_hi, w_lo))):
                            m = pe.matmul(tp[:, 0, t * NDT:(t + 1) * NDT], h[:, k, t * P:(t + 1) * P],
                                          w[:, r, k * NDT:(k + 1) * NDT],
                                          start=k == 0 and q == 0, stop=k == KT - 1 and q == 2)
                m.then_inc(slot_used, 1)

            def log_decays(turn):
                pe.wait_ge(dta_ready, turn + 1)
                for t in range(TT):
                    for d in range(2):
                        for st in range(TT):
                            m = pe.matmul(tp[:, 1, t * NDT + d * SSD_H:t * NDT + (d + 1) * SSD_H],
                                          tri[:, d, st, t * P:(t + 1) * P], dta[:, st, d * SSD_H:(d + 1) * SSD_H],
                                          start=st == 0, stop=st == 1)
                if turn == 0:
                    for st in range(TT):
                        m = pe.matmul(tp[:, 1, 2 * NDT:3 * NDT], tri[:, 0, 0, P:TOK], dta[:, st, :],
                                      start=st == 0, stop=st == 1)
                else:
                    for d in range(2):
                        for st in range(TT):
                            m = pe.matmul(gu[0:SSD_H, d, 0:TOK], dta[:, st, d * SSD_H:(d + 1) * SSD_H],
                                          tri[:, d, st, :], start=st == 0, stop=st == 1)
                m.then_inc(p_psum, 1)

            def xbc_slots(n, pairs, pair0, after):
                for p in range(pairs):
                    if p >= 4:
                        pe.wait_ge(xbc_evac, pair0 + p - 3)
                    for q in range(2):
                        col_slot(n + 2 * p + q, dn_bank(p % 4)[:, q * TOK:(q + 1) * TOK])
                    if p == 1:
                        after()

            def tokens(first_tile, count, bank):
                for t in range(TT):
                    for i in range(count):
                        m = pe.transpose(bank[:, t, i * P:(i + 1) * P], xbc[:, first_tile + i, t * P:(t + 1) * P], ident[:])
                m.then_inc(tokT_psum, 1)

            def ctx_mix(s, n0):
                for t in range(TT):
                    transposed(s, t)
                hT_there(s, 1)
                dt_slot(n0)
                xbc_slots(n0 + 1, 5, 0, lambda: log_decays(0))
                pe.wait_ge(xbc_evac, 5)
                pe.wait_ge(xbc_ready, 3)
                tokens(XS_T, 6, dn)
                pe.wait_ge(xbc_ready, 5)
                tokens(BM_T, 4, gu)
                pe.wait_ge(tok_ready, 4)
                pe.wait_ge(xdt_ready, 2)
                for d in range(2):
                    for g in range(SSD_G):
                        for t in range(TT):
                            m = pe.matmul(dn[:, d, g * 256:g * 256 + GW], bm_tok[:, t, g * P:(g + 1) * P],
                                          x_dt[d][:, t, g * GW:(g + 1) * GW], start=t == 0, stop=t == 1)
                    m.then_inc(state_psum, 1)

            def ssd(s, n0):
                for t in range(TT):
                    transposed(s, t)
                hT_there(s, 1)
                dt_slot(n0)
                pe.wait_ge(state_ready, 2)
                xbc_slots(n0 + 1, 7, 5, lambda: log_decays(1))
                pe.wait_ge(p_ready, 2)
                for si in range(4):
                    wide_slot(n0 + 15 + si, si, range(TT), gu)
                for si in range(4):
                    wide_slot(n0 + 19 + si, si, range(TT), tp)
                pe.wait_ge(xbc_evac, 12)
                pe.wait_ge(xbc_ready, 12)
                tokens(XS_T, 6, dn)
                pe.wait_ge(wide_ready, 4)
                for m_ in range(2):
                    for ft in range(2):
                        for st in range(TT):
                            m = pe.matmul(gu[:, m_, ft * TOK:(ft + 1) * TOK], u_tok[:, st, ft * P:(ft + 1) * P],
                                          dft_l[:, m_, st, :], start=st == 0, stop=st == 1)
                m.then_inc(four_psum, 1)
                pe.wait_ge(four_ready, 1)
                for ft in range(2):
                    for m_ in range(2):
                        m = pe.matmul(tp[:, 0, ft * TOK:(ft + 1) * TOK], dft_d[:, m_, :], f_mid[:, m_, ft, :],
                                      start=m_ == 0, stop=m_ == 1)
                m.then_inc(four_psum, 1)
                pe.wait_ge(four_ready, 2)
                for ft in range(2):
                    m = pe.matmul(tp[:, 1, ft * TOK:(ft + 1) * TOK], fourier_bd[:, ft, :], f_T[:, ft, :],
                                  start=True, stop=True)
                m.then_inc(four_psum, 1)
                pe.wait_ge(mix_lo, MIX0["ssd"] + 1)
                for g in range(SSD_G):
                    if g:
                        pe.wait_ge(yoff_used, TT * g)
                    for t in range(TT):
                        for d in range(2):
                            m = pe.matmul(tp[:, t, d * GW:(d + 1) * GW], xbc[:, CM_T + g, t * P:(t + 1) * P],
                                          state0[:, d, g, :], start=True, stop=True)
                    m.then_inc(yoff_psum, 1)
                pe.wait_ge(yoff_used, TT * SSD_G)
                pe.wait_ge(tok_ready, 6)

                def outputs(h):
                    pe.wait_ge(g_ready, h + 1)
                    w, c = decays[:, h % 2, :], slice(h * SSD_P, (h + 1) * SSD_P)
                    sums = [[(0, 0, 0), (384, 1, 0), (512, 1, 1)], [(128, 0, 0), (256, 0, 1), (640, 1, 1)]]
                    for t in range(TT):
                        for q, (at, d, st) in enumerate(sums[t]):
                            m = pe.matmul(dn[:, t, c], w[:, at:at + P], x_dt[d][:, st, c], start=q == 0, stop=q == 2)
                    m.then_inc(y_psum, 1)

                pe.wait_ge(xdt_ready, 4)
                for h in range(SSD_H):
                    g = h // HPG
                    if h % HPG == 0:
                        if g >= 2:
                            pe.wait_ge(cb_ready, g - 1)
                        for st in range(TT):
                            m = pe.matmul(tp[:, g % 2, st * TOK:(st + 1) * TOK], xbc[:, BM_T + g, st * P:(st + 1) * P],
                                          xbc[:, CM_T + g, :], start=True, stop=True)
                        m.then_inc(cb_psum, 1)
                    if h >= 2:
                        pe.wait_ge(arg_ready, h - 1)
                    for d in range(2):
                        m = pe.matmul(gu[:, h % 2, d * TOK:(d + 1) * TOK], ident[0:SSD_H, h:h + 1].broadcast_to([SSD_H, P]),
                                      prow[:, d, :], start=True, stop=True)
                    m.then_inc(rows_psum, 1)
                    if h:
                        outputs(h - 1)
                outputs(SSD_H - 1)
                for t in range(TT):
                    pe.wait_ge(y_ready, t + 1)
                    for i in range(SSD_W // P):
                        o = tp[:, t, i * P:(i + 1) * P] if i < 4 else gu[:, t, (i - 4) * P:(i - 3) * P]
                        m = pe.transpose(o, y_sum[:, t, i * P:(i + 1) * P], ident[:])
                        if i in (3, 5):
                            m.then_inc(mixT_psum, 1)
                out_proj(n0 + 23, range(KT), [MIX0["ssd"] + MIX_SSD] * KT)

            pe.wait_ge(consts, ALL_CONSTS)
            pe.wait_ge(c_split_ready, 1)
            ada()
            for s, name in enumerate(SUB):
                {"ctx_mix": ctx_mix, "ab": ab, "sc": sc, "ssd": ssd}.get(name, ffn)(s, BASE[name])

        @block.scalar
        def _(act):
            def copy(o, i, done, **kw):
                act.activation(o, i, ACT.Copy, **kw).then_inc(done, 1)

            def upper(n, it=0):
                if n >= NSLOT:
                    return
                slot_landed(act, n, it)
                if n >= RING:
                    act.wait_ge(slot_used, n - RING + 1 + RING * it)
                copy(w_hi[:, n % RING, :], raw[:, n % RING, :], hi_ready)

            def after_slots(n, count, it=0):
                for q in range(count):
                    upper(n + q + RING, it)

            def out_squares(s, factor):
                for t in range(TT):
                    if t == 0:
                        act.wait_ge(first_tok, FIRST_N["dn", s])
                    else:
                        act.wait_ge(slot_used, LAST[s])
                    act.activation(xn[:, t, :], dn[:, t, :], ACT.Square, scale=1.0 / (factor * D ** 0.5),
                                   accum_out=ssq[:, 2 + t:3 + t]).then_inc(ssq_ready, 1)

            def in_squares(s):
                for t in range(TT):
                    if SUB[s] == "ctx_ffn":
                        act.wait_ge(ctx_loaded, 16)
                    elif s == 2:
                        act.wait_ge(x_loaded, 16)
                    else:
                        act.wait_ge(x_new, TT * WITH_POST.index(s - 1) + t + 1)
                    act.activation(xn[:, t, :], x[:, t, :], ACT.Square, scale=1.0 / D ** 0.5,
                                   accum_out=ssq[:, t:t + 1]).then_inc(ssq_ready, 1)

            def in_upper(s):
                for t in range(TT):
                    for half in range(2):
                        act.wait_ge(hT_psum, 2 * (TT * s + t) + half + 1)
                        copy(hT_hi[:, 4 * half:4 * half + 4, t * P:(t + 1) * P],
                             tp[:, half, :].rearrange("p (k c) -> p k c", k=4), hT_hi_ready)

            def ada():
                act.wait_ge(consts, ALL_CONSTS)
                act.activation(silu_c[:], c_cols[:], ACT.Silu).then_inc(c_ready, 1)
                for n in range(RING):
                    upper(n)

                def chunks(first, it):
                    for m in range(3):
                        n = 4 * m + (0 if first else 12)
                        for si in range(4):
                            slot_landed(act, n + si + RING, 2 * it)
                            act.wait_ge(slot_used, n + si + 1 + 2 * RING * it)
                            copy(w_hi[:, (n + si) % RING, :], raw[:, (n + si) % RING, :], hi_ready)
                        act.wait_ge(slot_used, n + 4 + 12 * it)
                        if not first:
                            act.wait_ge(ada_summed, m + 1 + 3 * it)
                        copy(mod_parts[:, m * 512:(m + 1) * 512], dn_bank(m), ada_rows)

                chunks(True, 0)
                with act.Fori(0, ADA_CH // 3 - 1) as it:
                    chunks(False, it)

            def ffn(s, n0):
                c0 = FFNS.index(s) * STEPS

                def act_upper(c, it=0):
                    act.wait_ge(actT_psum, c + 1 + it)
                    copy(actT_hi[:], tp[:, 0, :].rearrange("p (k c) -> p k c", k=2), actT_hi_ready)

                def gate(t):
                    act.activation(silu[:, t, :], gu[:, t, 0:FS], ACT.Silu).then_inc(silu_ready, 1)

                def step(j, it):
                    n = n0 + 4 + 6 * (j - 1)
                    act_upper(c0 + j - 1, it)
                    after_slots(n, 3, it)
                    act.wait_ge(slot_used, n + 4 + RING * it)
                    gate(0)
                    gate(1)
                    after_slots(n + 3, 3, it)

                act.wait_ge(first_tok, FIRST_N["gu", s])
                gate(0)
                after_slots(n0, 3)
                act.wait_ge(slot_used, n0 + 4)
                gate(1)
                after_slots(n0 + 3, 1)
                step(1, 0)
                with act.Fori(0, STEPS - 3) as it:
                    step(2, it)
                step(STEPS - 1, 0)
                act_upper(c0 + STEPS - 1)
                out_squares(s, 0.5)
                after_slots(n0 + 4 + 6 * (STEPS - 1), 2)

            def ab(s, n0):
                act.wait_ge(lam_z, 1)
                act.activation(lru_tmp[:, 1, :], lru_tmp[:, 1, :], ACT.Exp).then_inc(lam_exp, 1)
                for pair in range(2):
                    after_slots(n0 + 2 * pair, 2)
                    act.wait_ge(slot_used, n0 + 2 * pair + 2)
                    copy(lx[:, 2 * pair:2 * pair + 2, LRU_CONV - 1:],
                         dn[:, 0, pair * 512:(pair + 1) * 512].rearrange("p (i c) -> p i c", i=2), ab_evac)
                for pair in range(2):
                    after_slots(n0 + 4 + 2 * pair, 2)
                    act.wait_ge(slot_used, n0 + 4 + 2 * pair + 2)
                    act.activation(gelu[:, 2 * pair:2 * pair + 2, :],
                                   dn[:, 1, pair * 512:(pair + 1) * 512].rearrange("p (i c) -> p i c", i=2),
                                   ACT.Gelu_apprx_tanh).then_inc(ab_evac, 1)
                after_slots(n0 + 8, 4)
                act.wait_ge(slot_used, n0 + 12)
                for t in range(TT):
                    copy(qk[:, t, 0:HEADS, :], gu[:, t, :].rearrange("p (h d) -> p h d", h=HEADS), ab_evac, scale=HD ** -0.5)
                after_slots(n0 + 12, 4)
                act.wait_ge(slot_used, n0 + 16)
                for t in range(TT):
                    copy(qk[:, t, HEADS:2 * HEADS, :], tp[:, t, :].rearrange("p (h d) -> p h d", h=HEADS), ab_evac)
                for g, o in enumerate((rgate, igate)):
                    act.wait_ge(gates_done, g + 1)
                    for i in range(LT):
                        act.activation(o[:, i, :], dn[:, g, i * TOK:(i + 1) * TOK], ACT.Sigmoid,
                                       bias=lru_cols[:, i, 5 + g:6 + g]).then_inc(gates_ready, 1)
                act.wait_ge(lru_c_ready, 1)
                act.wait_ge(gates_ready, LT)
                for i in range(LT):
                    act.activation(th[:, i, :], rgate[:, i, :], ACT.Tanh, scale=lru_tmp[:, 6, i:i + 1]).then_inc(lru_tanh, 1)
                for i in range(LT):
                    act.activation(decay[:, i, :], rgate[:, i, :], ACT.Exp, scale=lru_tmp[:, 7, i:i + 1]).then_inc(lru_decay, 1)
                after_slots(n0 + 16, 4)
                act.wait_ge(slot_used, n0 + 20)
                for t in range(TT):
                    copy(vtok[:, t, :], gu[:, t, :], ab_evac)
                for which, (o, bank) in enumerate(((qT, tp), (kT, gu))):
                    for half in range(2):
                        act.wait_ge(qkT_psum, 2 * which + half + 1)
                        copy(o[:, 2 * half:2 * half + 2, :], bank[:, half, :].rearrange("p (a c) -> p a c", a=2), qkT_ready)
                act.wait_ge(lru_ratio, 1)
                act.activation(th[:, :, :], th[:, :, :], ACT.Sqrt, scale=2.0).then_inc(lru_root, 1)

                def turned(h):
                    act.wait_ge(expT_psum, h + 1)
                    copy(expT[:, h % 2, :], dn[:, 0, (h % 2) * 512:(h % 2) * 512 + 3 * P], expT_ready)

                for h in range(HEADS):
                    act.wait_ge(masked_ready, 3 * h + 3)
                    act.activation(expo[:, h % 2, 0:P], masked[:, h % 2, 0:P], ACT.Exp,
                                   bias=soft[:, 1, h, 0:1], accum_out=soft[:, 2, h, 0:1])
                    act.activation(expo[:, h % 2, P:3 * P], masked[:, h % 2, P:3 * P], ACT.Exp,
                                   bias=soft[:, 1, h, 1:2], accum_out=soft[:, 2, h, 1:2]).then_inc(exp_ready, 1)
                    if h:
                        turned(h - 1)
                turned(HEADS - 1)
                act.wait_ge(rec_ready, 1)
                copy(hT_hi[:, 4:8, :], gelu[:, :, :], mix_hi)
                for t in range(TT):
                    act.wait_ge(mixT_psum, t + 1)
                    copy(hT_hi[:, 0:4, t * P:(t + 1) * P], tp[:, t, :].rearrange("p (k c) -> p k c", k=4), mix_hi)
                after_slots(n0 + 20, 7)
                out_squares(s, 1.0)
                after_slots(n0 + 27, 1)

            def sc(s, n0):
                for i in range(KT):
                    act.wait_ge(slot_used, n0 + 3 * i + 1)
                    if i >= 2:
                        act.wait_ge(sc_mixed, 2 * (i - 2) + 1)
                    copy(cgate[:, i % 2, 0:TOK], any_bank(3 * i % 8)[:, 0:TOK], sc_gate)
                    after_slots(n0 + 3 * i, 3)
                act.wait_ge(slot_used, n0 + 3 * KT)
                for half in range(2):
                    act.wait_ge(sc_mixed, 8 * half + 8)
                    copy(hT_hi[:, 4 * half:4 * half + 4, :], conv_y[:, 4 * half:4 * half + 4, :], mix_hi)
                after_slots(n0 + 3 * KT, KT - 1)
                out_squares(s, 1.0)
                after_slots(n0 + 3 * KT + KT - 1, 1)

            def dt_and_conv(turn, n0, pairs, pair0, tile0):
                if turn == 0:
                    act.activation(neg_a[:], ssd_rows[:, NDT:2 * NDT], ACT.Exp).then_inc(a_exp, 1)
                after_slots(n0, 1)
                act.wait_ge(dt_z, turn + 1)
                act.activation(dt_tmp[:, 1, :], dt_tmp[:, 1, :], ACT.Exp).then_inc(dt_exp, 1)

                def convolved(p):
                    act.wait_ge(conv_done, pair0 + p + 1)
                    for q in range(2):
                        i = tile0 + 2 * p + q
                        m = act.activation(xbc[:, i, :], xbc[:, i, :], ACT.Silu, bias=ssd_cols[:, i, 3:4])
                    m.then_inc(xbc_ready, 1)

                for p in range(pairs):
                    n = n0 + 1 + 2 * p
                    after_slots(n, 2)
                    act.wait_ge(slot_used, n + 2)
                    i = tile0 + 2 * p
                    copy(xbc_in[:, i:i + 2, 1:1 + TOK], dn_bank(p % 4).rearrange("p (i c) -> p i c", i=2), xbc_evac)
                    if p:
                        convolved(p - 1)
                    if p == 2:
                        act.wait_ge(p_psum, turn + 1)
                        if turn == 0:
                            copy(pcol[:, :, :], tp[:, 1, 0:3 * NDT].rearrange("p (t h) -> p t h", t=3), p_ready)
                        else:
                            act.activation(pcol[:, 0:2, :], tp[:, 1, 0:2 * NDT].rearrange("p (t h) -> p t h", t=2), ACT.Copy)
                            copy(prow[:, :, :], gu[0:SSD_H, :, 0:TOK], p_ready)
                convolved(pairs - 1)

            def x_tokens(turn):
                act.wait_ge(tokT_psum, 2 * turn + 1)
                for t in range(TT):
                    copy(xs_tok[:, t, :], dn[:, t, 0:SSD_W], tok_ready)

            def ctx_mix(s, n0):
                dt_and_conv(0, n0, 5, 0, XS_T)
                act.wait_ge(p_arg, 1)
                act.activation(exp_p[:, :, :], exp_p[:, :, :], ACT.Exp).then_inc(p_exp, 1)
                x_tokens(0)
                act.wait_ge(tokT_psum, 2)
                for t in range(TT):
                    copy(bm_tok[:, t, :], gu[:, t, :], tok_ready)
                for d in range(2):
                    act.wait_ge(state_psum, d + 1)
                    copy(state0[:, d, :, :], dn[:, d, :].rearrange("p (g c) -> p g c", g=SSD_G)[:, :, 0:GW], state_ready)

            def ssd(s, n0):
                dt_and_conv(1, n0, 7, 5, 0)
                act.wait_ge(p_ready, 2)
                act.activation(exp_p[:, :, :], pcol[:, 0:2, :], ACT.Exp).then_inc(p_exp, 1)
                after_slots(n0 + 15, 4)
                act.wait_ge(slot_used, n0 + 19)
                for t in range(TT):
                    act.activation(u_tok[:, t, :], gu[:, t, 0:FOURIER], ACT.Copy)
                for t in range(TT):
                    act.activation(z_tok[:, t, 0:256], gu[:, t, FOURIER:512], ACT.Silu).then_inc(wide_ready, 1)
                after_slots(n0 + 19, 4)
                act.wait_ge(slot_used, n0 + 23)
                for t in range(TT):
                    act.activation(z_tok[:, t, 256:SSD_W], tp[:, t, :], ACT.Silu).then_inc(wide_ready, 1)
                x_tokens(1)
                act.wait_ge(four_psum, 1)
                copy(f_mid[:, :, :, :], gu[:, :, :].rearrange("p m (f c) -> p m f c", f=2), four_ready)
                act.wait_ge(four_psum, 2)
                copy(f_T[:, :, :], tp[:, 0, :].rearrange("p (f c) -> p f c", f=2), four_ready)
                act.wait_ge(four_psum, 3)
                copy(hT_hi[:, 0:2, :], tp[:, 1, :].rearrange("p (f c) -> p f c", f=2), mix_hi)
                for h in range(SSD_H):
                    act.wait_ge(arg_ready, h + 1)
                    act.activation(decays[:, h % 2, :], decays[:, h % 2, :], ACT.Exp).then_inc(dec_ready, 1)
                for t in range(TT):
                    c = slice(t * P, (t + 1) * P)
                    act.wait_ge(mixT_psum, 2 + 2 * t + 1)
                    copy(hT_hi[:, 2:6, c], tp[:, t, :].rearrange("p (k c) -> p k c", k=4), mix_hi)
                    act.wait_ge(mixT_psum, 2 + 2 * t + 2)
                    copy(hT_hi[:, 6:8, c], gu[:, t, 0:TOK].rearrange("p (k c) -> p k c", k=2), mix_hi)
                after_slots(n0 + 23, 7)
                out_squares(s, 1.0)
                after_slots(n0 + 30, 1)

            for name, tile in small_tiles.items():
                act.dma_start(tile if name == "comb" else tile[:], small[name]).then_inc(consts, 16)
            act.dma_start(ssd_rows[:], small["ssd_rows"][0, :].partition_broadcast(P)).then_inc(consts, 16)
            act.dma_start(ssd_norm[:], small["ssd_norm"][0, :].partition_broadcast(P)).then_inc(consts, 16)
            act.dma_start(mod_bias, small["ada_b"][0, :].partition_broadcast(2)).then_inc(consts, 16)
            act.dma_start(x[:], ctx_in.rearrange("(t p) d -> p t d", p=P)).then_inc(ctx_loaded, 16)
            ada()
            for s, name in enumerate(SUB):
                in_squares(s)
                in_upper(s)
                {"ctx_mix": ctx_mix, "ab": ab, "sc": sc, "ssd": ssd}.get(name, ffn)(s, BASE[name])

        @block.vector
        def _(dve):
            steps = [0]

            def then(ins):
                steps[0] += 1
                ins.then_inc(dve_step, 1)
                dve.wait_ge(dve_step, steps[0])

            def rest(n, it=0):
                if n >= NSLOT:
                    return
                dve.wait_ge(hi_ready, n + 1 + RING * it)
                r = n % RING
                dve.tensor_tensor(w_lo[:, r, :], raw[:, r, :], w_hi[:, r, :].bitcast(F32),
                                  ALU.subtract).then_inc(lo_ready, 1)

            def after_slots(n, count, it=0):
                for q in range(count):
                    rest(n + q + RING, it)

            def lower(o, i, hi, done):
                dve.tensor_tensor(o, i, hi.bitcast(F32), ALU.subtract).then_inc(done, 1)

            def residual(s):
                for t in range(TT):
                    dve.wait_ge(rstd_ready, NORM_N["post", s, t])
                    if s in MOD:
                        dve.wait_ge(post_mod, POST_MOD_N[s])
                    else:
                        dve.wait_ge(row_post, POST_DMA_N[s])
                    then(dve.scalar_tensor_tensor(xn[:, t, :], dn[:, t, :], rstd[:, 2 + t:3 + t], post_row[:],
                                                  ALU.mult, ALU.mult))
                    dve.tensor_tensor(x[:, t, :], x[:, t, :], xn[:, t, :], ALU.add).then_inc(x_new, 1)

            def normalised(s):
                for t in range(TT):
                    dve.wait_ge(rstd_ready, NORM_N["pre", s, t])
                    if s in MOD:
                        dve.wait_ge(pre_mod, PRE_MOD_N[s])
                    else:
                        dve.wait_ge(row_pre, PRE_DMA_N[s])
                    m = dve.scalar_tensor_tensor(xn[:, t, :], x[:, t, :], rstd[:, t:t + 1], pre_row[:], ALU.mult, ALU.mult)
                    if s in MOD:
                        then(m)
                        m = dve.tensor_tensor(xn[:, t, :], xn[:, t, :], shift_row[:], ALU.add)
                    m.then_inc(xn_ready, 1)

            def in_lower(s):
                for t in range(TT):
                    for half in range(2):
                        c = (slice(None), slice(4 * half, 4 * half + 4), slice(t * P, (t + 1) * P))
                        dve.wait_ge(hT_hi_ready, 2 * (TT * s + t) + half + 1)
                        lower(hT_lo[c], tp[:, half, :].rearrange("p (k c) -> p k c", k=4), hT_hi[c], hT_lo_ready)

            def log1p(tiles):
                u, s1, s2, acc = tiles
                then(dve.tensor_scalar(s1, u, 2.0, None, ALU.add))
                then(dve.reciprocal(s2, s1))
                then(dve.tensor_tensor(s1, u, s2, ALU.mult))
                then(dve.tensor_tensor(s2, s1, s1, ALU.mult))
                then(dve.tensor_scalar(acc, s2, 1.0 / 17, None, ALU.mult))
                for k in range(15, 2, -2):
                    then(dve.scalar_tensor_tensor(acc, acc, 1.0 / k, s2, ALU.add, ALU.mult))
                then(dve.scalar_tensor_tensor(acc, acc, 1.0, s1, ALU.add, ALU.mult))

            def ada():
                dve.memset(c_split.bitcast(F32), 0.0).then_inc(halves, 1)
                dve.wait_ge(c_ready, 1)
                dve.wait_ge(halves, 2)
                for v in range(2):
                    then(dve.tensor_copy(c_split[:, :, 2 * v], silu_c[:, v, :]))
                    m = dve.tensor_tensor(c_split[:, :, 2 * v + 1], silu_c[:, v, :], c_split[:, :, 2 * v].bitcast(F32), ALU.subtract)
                m.then_inc(c_split_ready, 1)
                for n in range(RING):
                    rest(n)

                def chunks(first, it):
                    def rests(m):
                        n = 4 * m + (0 if first else 12)
                        for si in range(4):
                            r = (n + si) % RING
                            dve.wait_ge(hi_ready, n + si + RING + 1 + 2 * RING * it)
                            dve.tensor_tensor(w_lo[:, r, :], raw[:, r, :], w_hi[:, r, :].bitcast(F32),
                                              ALU.subtract).then_inc(lo_ready, 1)

                    def summed(m):
                        dve.wait_ge(ada_summed, (m if first else m + 3) + 1 + 3 * it)
                        if not first:
                            dve.wait_ge(ada_stored, 16 + 16 * it)
                        bank = gu[0:2, m, :] if m < 2 else tp[0:2, 0, :]
                        bias = mod_bias[:, m * 512:(m + 1) * 512] if first else mod_bias[:, bass.ds(m * 512 + 1536 + 1536 * it, 512)]
                        dve.tensor_tensor(mod_out[:, m * 512:(m + 1) * 512], bank, bias, ALU.add).then_inc(ada_out, 1)

                    rests(0)
                    rests(1)
                    summed(0)
                    rests(2)
                    summed(1)
                    summed(2)

                chunks(True, 0)
                with dve.Fori(0, ADA_CH // 3 - 1) as it:
                    chunks(False, it)

            def ffn(s, n0):
                c0 = FFNS.index(s) * STEPS

                def act_lower(c, it=0):
                    dve.wait_ge(actT_hi_ready, c + 1 + it)
                    lower(actT_lo[:], tp[:, 0, :].rearrange("p (k c) -> p k c", k=2), actT_hi[:], actT_lo_ready)

                def gated(c, t, it=0):
                    dve.wait_ge(silu_ready, TT * c + t + 1 + TT * it)
                    dve.tensor_tensor(act_tok[:, t, :], silu[:, t, :], gu[:, t, FS:512], ALU.mult).then_inc(act_ready, 1)

                def step(j, it):
                    n = n0 + 4 + 6 * (j - 1)
                    act_lower(c0 + j - 1, it)
                    after_slots(n, 3, it)
                    gated(c0 + j, 0, it)
                    gated(c0 + j, 1, it)
                    after_slots(n + 3, 3, it)

                gated(c0, 0)
                after_slots(n0, 3)
                gated(c0, 1)
                after_slots(n0 + 3, 1)
                step(1, 0)
                with dve.Fori(0, STEPS - 3) as it:
                    step(2, it)
                step(STEPS - 1, 0)
                act_lower(c0 + STEPS - 1)

            def ab(s, n0):
                then(dve.memset(lx[:, :, 0:LRU_CONV - 1], 0.0))
                lam = lru_cols[:, :, 7]
                then(dve.tensor_scalar(lru_tmp[:, 0, :], lam, -1.0, None, ALU.mult))
                dve.tensor_tensor(lru_tmp[:, 1, :], lam, lru_tmp[:, 0, :], ALU.min).then_inc(lam_z, 1)
                dve.wait_ge(lam_exp, 1)
                log1p([lru_tmp[:, q, :] for q in (1, 2, 3, 4)])
                then(dve.tensor_scalar(lru_tmp[:, 5, :], lru_tmp[:, 0, :], 0.0, None, ALU.max))
                then(dve.scalar_tensor_tensor(lru_tmp[:, 5, :], lru_tmp[:, 4, :], 2.0, lru_tmp[:, 5, :], ALU.mult, ALU.add))
                dve.tensor_scalar(lru_tmp[:, 6, :], lru_tmp[:, 5, :], LRU_C, None, ALU.mult)
                dve.tensor_scalar(lru_tmp[:, 7, :], lru_tmp[:, 5, :], -LRU_C, None, ALU.mult).then_inc(lru_c_ready, 1)
                after_slots(n0, 4)
                dve.wait_ge(ab_evac, 2)
                for j in range(LRU_CONV):
                    for i in range(LT):
                        src, w = lx[:, i, j:j + TOK], lru_cols[:, i, j:j + 1]
                        if j == 0:
                            m = dve.tensor_scalar(xc[:, i, :], src, w, lru_cols[:, i, 4:5], ALU.mult, ALU.add)
                        else:
                            m = dve.scalar_tensor_tensor(xc[:, i, :], src, w, xc[:, i, :], ALU.mult, ALU.add)
                    if j < LRU_CONV - 1:
                        then(m)
                    else:
                        m.then_inc(xc_ready, 1)
                after_slots(n0 + 4, 12)
                dve.wait_ge(ab_evac, 8)
                half = [qk[:, :, :, q * HALF_ROT:(q + 1) * HALF_ROT] for q in range(2)]
                turn = [rope[:, :, q, :].unsqueeze(2).broadcast_to([P, TT, 2 * HEADS, HALF_ROT]) for q in range(2)]
                tmp = [v.rearrange("p (n t h d) -> p n t h d", n=2, t=TT, h=2 * HEADS) for v in (rope_t, rope_u)]
                for q in range(2):
                    for c in range(2):
                        m = dve.tensor_tensor(tmp[q][:, c], half[q], turn[c], ALU.mult)
                then(m)
                dve.tensor_tensor(half[0], tmp[0][:, 0], tmp[1][:, 1], ALU.subtract)
                dve.tensor_tensor(half[1], tmp[1][:, 0], tmp[0][:, 1], ALU.add).then_inc(roped, 1)
                dve.wait_ge(lru_decay, LT)
                then(dve.tensor_scalar(rgate[:, :, :], th[:, :, :], 1.0, None, ALU.add))
                then(dve.reciprocal(rgate[:, :, :], rgate[:, :, :]))
                dve.tensor_tensor(th[:, :, :], th[:, :, :], rgate[:, :, :], ALU.mult).then_inc(lru_ratio, 1)
                after_slots(n0 + 16, 4)
                then(dve.tensor_tensor(igate[:, :, :], igate[:, :, :], xc[:, :, :], ALU.mult))
                dve.wait_ge(lru_root, 1)
                then(dve.tensor_tensor(igate[:, :, :], igate[:, :, :], th[:, :, :], ALU.mult))
                for i in range(LT):
                    m = dve.tensor_tensor_scan(rgate[:, i, :], decay[:, i, :], igate[:, i, :], 0.0, ALU.mult, ALU.add)
                then(m)
                dve.tensor_tensor(gelu[:, :, :], gelu[:, :, :], rgate[:, :, :], ALU.mult).then_inc(rec_ready, 1)
                for h in range(HEADS):
                    bank = (gu, tp)[(h // 2) % 2][:, h % 2, :]
                    dve.wait_ge(scores_done, h + 1)
                    if h >= 2:
                        dve.wait_ge(exp_ready, h - 1)
                    for t, c in enumerate((slice(0, P), slice(P, 3 * P))):
                        dve.tensor_tensor_reduce(masked[:, h % 2, c], bank[:, c], causal[:, c], 1.0, -3.0e38,
                                                 ALU.add, ALU.max, soft[:, 0, h, t:t + 1]).then_inc(masked_ready, 1)
                    dve.wait_ge(masked_ready, 3 * h + 2)
                    dve.tensor_scalar(soft[:, 1, h, :], soft[:, 0, h, :], -1.0, None, ALU.mult).then_inc(masked_ready, 1)
                dve.wait_ge(mix_hi, 1)
                lower(hT_lo[:, 4:8, :], gelu[:, :, :], hT_hi[:, 4:8, :], mix_lo)
                dve.wait_ge(exp_ready, HEADS)
                then(dve.reciprocal(soft[:, 3, :, :], soft[:, 2, :, :]))
                dve.wait_ge(attn_psum, 1)
                for t in range(TT):
                    m = dve.tensor_tensor(attn[:, t, :].rearrange("p (h d) -> p h d", h=HEADS),
                                          dn[:, 1, t * 512:(t + 1) * 512].rearrange("p (h d) -> p h d", h=HEADS),
                                          soft[:, 3, :, t].unsqueeze(2).broadcast_to([P, HEADS, HD]), ALU.mult)
                m.then_inc(attn_ready, 1)
                for t in range(TT):
                    c = (slice(None), slice(0, 4), slice(t * P, (t + 1) * P))
                    dve.wait_ge(mix_hi, 2 + t)
                    lower(hT_lo[c], tp[:, t, :].rearrange("p (k c) -> p k c", k=4), hT_hi[c], mix_lo)
                after_slots(n0 + 20, 7)

            def sc(s, n0):
                then(dve.memset(cx[:, :, 0:SC_CONV - 1], 0.0))
                for i in range(KT):
                    dve.wait_ge(sc_gate, i + 1)
                    dve.wait_ge(slot_used, n0 + 3 * i + 2)
                    dve.tensor_tensor(cx[:, i, SC_CONV - 1:], cgate[:, i % 2, 0:TOK], any_bank((3 * i + 1) % 8)[:, 0:TOK],
                                      ALU.mult).then_inc(sc_mixed, 1)
                    dve.wait_ge(sc_mixed, 2 * i + 1)
                    for j in range(SC_CONV):
                        src, w = cx[:, i, j:j + TOK], sc_cols[:, i, j:j + 1]
                        if j == 0:
                            then(dve.tensor_scalar(conv_y[:, i, :], src, w, None, ALU.mult))
                        else:
                            then(dve.scalar_tensor_tensor(conv_y[:, i, :], src, w, conv_y[:, i, :], ALU.mult, ALU.add))
                    dve.wait_ge(slot_used, n0 + 3 * i + 3)
                    dve.tensor_tensor(conv_y[:, i, :], conv_y[:, i, :], any_bank((3 * i + 2) % 8)[:, 0:TOK],
                                      ALU.mult).then_inc(sc_mixed, 1)
                    after_slots(n0 + 3 * i, 3)
                for half in range(2):
                    c = (slice(None), slice(4 * half, 4 * half + 4))
                    dve.wait_ge(mix_hi, MIX0["sc"] + half + 1)
                    lower(hT_lo[c], conv_y[c], hT_hi[c], mix_lo)
                after_slots(n0 + 3 * KT, KT - 1)

            def dt_and_conv(turn, n0, pairs, pair0, tile0, after):
                for edge in (0, TOK + 1):
                    m = dve.memset(xbc_in[:, :, edge:edge + 1], 0.0)
                then(m)
                if turn == 0:
                    dve.wait_ge(a_exp, 1)
                    then(dve.tensor_scalar(neg_a[:], neg_a[:], -1.0, None, ALU.mult))
                after_slots(n0, 1)
                z, u, s1, s2, acc, mz = (dt_tmp[:, q, :] for q in range(6))

                def both(v):
                    return v.rearrange("p (t h) -> p t h", t=TT)

                dve.wait_ge(slot_used, n0 + 1)
                then(dve.tensor_tensor(both(z), both(tp[:, 0, 0:TT * NDT]),
                                       ssd_rows[:, 0:NDT].unsqueeze(1).broadcast_to([P, TT, NDT]), ALU.add))
                then(dve.tensor_scalar(u, z, -1.0, None, ALU.mult))
                dve.tensor_tensor(u, z, u, ALU.min).then_inc(dt_z, 1)
                then(dve.tensor_scalar(mz, z, 0.0, None, ALU.max))
                dve.wait_ge(dt_exp, turn + 1)
                log1p([u, s1, s2, acc])
                then(dve.scalar_tensor_tensor(both(dt[:, :, :].rearrange("p t h -> p (t h)")), both(acc), 2.0, both(mz), ALU.mult, ALU.add))
                dve.tensor_tensor(dta[:, :, :], dt[:, :, :], neg_a[:].unsqueeze(1).broadcast_to([P, TT, NDT]),
                                  ALU.mult).then_inc(dta_ready, 1)
                for p in range(pairs):
                    after_slots(n0 + 1 + 2 * p, 2)
                    dve.wait_ge(xbc_evac, pair0 + p + 1)
                    for j in range(3):
                        for q in range(2):
                            i = tile0 + 2 * p + q
                            src, w = xbc_in[:, i, j:j + TOK], ssd_cols[:, i, j:j + 1]
                            if j == 0:
                                m = dve.tensor_scalar(xbc[:, i, :], src, w, None, ALU.mult)
                            else:
                                m = dve.scalar_tensor_tensor(xbc[:, i, :], src, w, xbc[:, i, :], ALU.mult, ALU.add)
                        if j < 2:
                            then(m)
                        else:
                            m.then_inc(conv_done, 1)
                    if p == 3:
                        after()

            def heads_of(v):
                return v.rearrange("p (h d) -> p h d", d=SSD_P)

            def x_times(w):
                for d in range(2):
                    for t in range(TT):
                        m = dve.tensor_tensor(heads_of(x_dt[d][:, t, :]), heads_of(xs_tok[:, t, :]),
                                              w[:, t, d * SSD_H:(d + 1) * SSD_H].unsqueeze(2).broadcast_to([P, SSD_H, SSD_P]), ALU.mult)
                    m.then_inc(xdt_ready, 1)

            def ctx_mix(s, n0):
                def decay_arguments():
                    dve.wait_ge(p_ready, 1)
                    dve.tensor_tensor(exp_p[:, :, :], pcol[:, 2, :].unsqueeze(1).broadcast_to([P, TT, NDT]),
                                      pcol[:, 0:2, :], ALU.subtract).then_inc(p_arg, 1)

                dt_and_conv(0, n0, 5, 0, XS_T, decay_arguments)
                dve.wait_ge(p_exp, 1)
                then(dve.tensor_tensor(exp_p[:, :, :], exp_p[:, :, :], dt[:, :, :], ALU.mult))
                dve.wait_ge(tok_ready, 2)
                x_times(exp_p)

            def ssd(s, n0):
                dt_and_conv(1, n0, 7, 5, 0, lambda: None)
                after_slots(n0 + 15, 8)
                dve.wait_ge(tok_ready, 6)
                for t in range(TT):
                    m = dve.tensor_tensor(heads_of(y_acc[:, t, :]), heads_of(xs_tok[:, t, :]),
                                          ssd_rows[:, 2 * NDT:].unsqueeze(2).broadcast_to([P, SSD_H, SSD_P]), ALU.mult)
                then(m)
                x_times(dt)
                dve.wait_ge(mix_hi, MIX0["ssd"] + 1)
                lower(hT_lo[:, 0:2, :], tp[:, 1, :].rearrange("p (f c) -> p f c", f=2), hT_hi[:, 0:2, :], mix_lo)
                dve.wait_ge(p_exp, 2)
                for g in range(SSD_G):
                    dve.wait_ge(yoff_psum, g + 1)
                    for t in range(TT):
                        w = exp_p[:, t, :].rearrange("p (d h) -> p d h", d=2)[:, :, g * HPG:(g + 1) * HPG]
                        for d in range(2):
                            m = dve.tensor_tensor(heads_of(y_off[:, t, d * GW:(d + 1) * GW]), heads_of(tp[:, t, d * GW:(d + 1) * GW]),
                                                  w[:, d, :].unsqueeze(2).broadcast_to([P, HPG, SSD_P]), ALU.mult)
                        m.then_inc(yoff_used, 1)
                    dve.wait_ge(yoff_used, TT * (g + 1))
                    for d in range(2):
                        for t in range(TT):
                            acc = y_acc[:, t, g * GW:(g + 1) * GW]
                            m = dve.tensor_tensor(acc, acc, y_off[:, t, d * GW:(d + 1) * GW], ALU.add)
                        then(m)

                def masked_cb(g):
                    dve.wait_ge(cb_psum, g + 1)
                    cb = tp[:, g % 2, :]
                    dve.tensor_tensor(cb_m[:, 0:256], cb[:, 0:256], tri[:, 0, 0, :], ALU.mult)
                    dve.tensor_tensor(cb_m[:, 256:384], cb[:, 384:512], tri[:, 0, 1, P:], ALU.mult)
                    dve.tensor_tensor(cb_m[:, 384:512], cb[:, 0:128], tri[:, 1, 0, 0:P], ALU.mult)
                    dve.tensor_tensor(cb_m[:, 512:768], cb[:, 256:512], tri[:, 1, 1, :], ALU.mult).then_inc(cb_ready, 1)

                def arguments(h):
                    dve.wait_ge(rows_psum, h + 1)
                    if h >= 2:
                        dve.wait_ge(y_psum, h - 1)
                    w, b = decays[:, h % 2, :], gu[:, h % 2, :]
                    for at, c, d, st in ((0, slice(0, 256), 0, 0), (256, slice(128, 256), 0, 1),
                                         (384, slice(256, 384), 1, 0), (512, slice(256, 512), 1, 1)):
                        m = dve.tensor_scalar(w[:, at:at + c.stop - c.start], b[:, c], pcol[:, st, d * SSD_H + h:d * SSD_H + h + 1],
                                              0.0, ALU.subtract, ALU.min)
                    m.then_inc(arg_ready, 1)

                arguments(0)
                for h in range(SSD_H):
                    if h + 1 < SSD_H:
                        arguments(h + 1)
                    if h % HPG == 0:
                        masked_cb(h // HPG)
                    dve.wait_ge(cb_ready, h // HPG + 1)
                    dve.wait_ge(dec_ready, h + 1)
                    dve.tensor_tensor(decays[:, h % 2, :], decays[:, h % 2, :], cb_m[:, :], ALU.mult).then_inc(g_ready, 1)
                dve.wait_ge(y_psum, SSD_H)
                dve.wait_ge(wide_ready, 4)
                for t in range(TT):
                    m = dve.tensor_tensor(y_sum[:, t, :], dn[:, t, 0:SSD_W], y_acc[:, t, :], ALU.add)
                then(m)
                then(dve.tensor_tensor(y_sum[:, :, :], y_sum[:, :, :], z_tok, ALU.mult))
                then(dve.tensor_tensor(y_acc[:, :, :], y_sum[:, :, :], y_sum[:, :, :], ALU.mult))
                then(dve.tensor_reduce(gstat[:, 0, :], y_acc[:, :, :].rearrange("p t (g c) -> p (t g) c", g=SSD_G), AX.X, ALU.add))
                dve.tensor_scalar(gstat[:, 1, :], gstat[:, 0, :], 1.0 / GW, EPS, ALU.mult, ALU.add).then_inc(gsq_ready, 1)
                dve.wait_ge(gr_ready, 1)
                for t in range(TT):
                    v = y_sum[:, t, :].rearrange("p (g c) -> p g c", g=SSD_G)
                    then(dve.tensor_tensor(v, v, gstat[:, 2, t * SSD_G:(t + 1) * SSD_G].unsqueeze(2).broadcast_to([P, SSD_G, GW]), ALU.mult))
                    dve.tensor_tensor(y_sum[:, t, :], y_sum[:, t, :], ssd_norm[:], ALU.mult).then_inc(y_ready, 1)
                for t in range(TT):
                    c = slice(t * P, (t + 1) * P)
                    dve.wait_ge(mix_hi, MIX0["ssd"] + 2 + 2 * t)
                    lower(hT_lo[:, 2:6, c], tp[:, t, :].rearrange("p (k c) -> p k c", k=4), hT_hi[:, 2:6, c], mix_lo)
                    dve.wait_ge(mix_hi, MIX0["ssd"] + 3 + 2 * t)
                    lower(hT_lo[:, 6:8, c], gu[:, t, 0:TOK].rearrange("p (k c) -> p k c", k=2), hT_hi[:, 6:8, c], mix_lo)
                after_slots(n0 + 23, 7)

            dve.memset(neg_half[:], -0.5).then_inc(halves, 1)
            ada()
            for s, name in enumerate(SUB):
                normalised(s)
                in_lower(s)
                {"ctx_mix": ctx_mix, "ab": ab, "sc": sc, "ssd": ssd}.get(name, ffn)(s, BASE[name])
                if s in WITH_POST:
                    residual(s)
                    left = 2 if s in FFNS else 1
                    after_slots(LAST[s] - left, left)

        @block.gpsimd
        def _(pool):
            steps = [0]

            def then(ins):
                steps[0] += 1
                ins.then_inc(pool_step, 1)
                pool.wait_ge(pool_step, steps[0])

            def inverse_root(kind, s, t):
                eps = EPS / 0.25 if kind == "post" and s in FFNS else EPS
                c = slice(t + (2 if kind == "post" else 0), t + (2 if kind == "post" else 0) + 1)
                pool.wait_ge(ssq_ready, NORM_N[kind, s, t])
                then(pool.tensor_scalar(ms[:, c], ssq[:, c], eps, None, ALU.add))
                pool.tensor_tensor(rstd[:, c], ms[:, c], neg_half[:, 0:1], ALU.pow).then_inc(rstd_ready, 1)

            def mod_vector(v, q):
                return mod[v, q * D:(q + 1) * D].partition_broadcast(P)

            def rows_in(s):
                pool.dma_start(pre_row[:], pre_rows[s, :].partition_broadcast(P)).then_inc(row_pre, 16)
                if s in MOD:
                    v, shift, scale, _ = MOD[s]
                    pool.dma_start(shift_row[:], mod_vector(v, shift)).then_inc(row_pre, 16)
                    pool.dma_start(mod_row[:], mod_vector(v, scale)).then_inc(row_pre, 16)
                    pool.wait_ge(row_pre, PRE_DMA_N[s])
                    then(pool.tensor_scalar(mod_row[:], mod_row[:], 1.0, None, ALU.add))
                    pool.tensor_tensor(pre_row[:], pre_row[:], mod_row[:], ALU.mult).then_inc(pre_mod, 1)
                    pool.wait_ge(pre_mod, PRE_MOD_N[s])

            def rows_out(s):
                pool.dma_start(post_row[:], post_rows[s, :].partition_broadcast(P)).then_inc(row_post, 16)
                if s in MOD:
                    v, _, _, gate = MOD[s]
                    pool.dma_start(mod_row[:], mod_vector(v, gate)).then_inc(row_post, 16)
                    pool.wait_ge(row_post, POST_DMA_N[s])
                    pool.tensor_tensor(post_row[:], post_row[:], mod_row[:], ALU.mult).then_inc(post_mod, 1)
                    pool.wait_ge(post_mod, POST_MOD_N[s])

            pool.wait_ge(halves, 1)
            for it in range(ADA_CH // 3):
                pool.wait_ge(ada_out, 3 * it + 3)
                pool.dma_start(mod[:, it * 1536:(it + 1) * 1536], mod_out).then_inc(ada_stored, 16)
            pool.wait_ge(ada_stored, 16 * (ADA_CH // 3))
            rows_in(0)
            for s, name in enumerate(SUB):
                for t in range(TT):
                    inverse_root("pre", s, t)
                if s in WITH_POST:
                    rows_out(s)
                pool.wait_ge(xn_ready, TT * (s + 1))
                if name == "ctx_mix":
                    pool.dma_start(x[:], x_in.rearrange("(t p) d -> p t d", p=P)).then_inc(x_loaded, 16)
                    pool.dma_start(gate_bd, small["gate_bd"]).then_inc(gate_loaded, 16)
                if s + 1 < len(SUB):
                    rows_in(s + 1)
                if name == "ssd":
                    pool.wait_ge(gsq_ready, 1)
                    pool.tensor_tensor(gstat[:, 2, :], gstat[:, 1, :], neg_half[:], ALU.pow).then_inc(gr_ready, 1)
                if s in WITH_POST:
                    for t in range(TT):
                        inverse_root("post", s, t)
            for t in range(TT):
                pool.wait_ge(x_new, TT * (len(WITH_POST) - 1) + t + 1)
                pool.dma_start(out[t * P:(t + 1) * P, :], x[:, t, :]).then_inc(stored, 16)
            pool.wait_ge(stored, 16 * TT)

def wide(w):
    return w.reshape(KT // 2, 2, P, 512).transpose(0, 2, 1, 3).reshape(KT // 2 * P, SLOT)


def columns(w):
    return w.reshape(KT, P, -1, P).transpose(2, 1, 0, 3).reshape(-1, SLOT)


def narrow(w):
    slot = np.zeros((P, SLOT), np.float32)
    slot[:, :KT * NDT] = w.reshape(KT, P, NDT).transpose(1, 0, 2).reshape(P, KT * NDT)
    return slot


def swiglu_slots(w_gate, w_up, w_down):
    slots = []
    for j in range(STEPS):
        c = slice(j * FS, (j + 1) * FS)
        slots.append(wide(np.concatenate([w_gate[:, c], w_up[:, c]], axis=1)))
        if j:
            slots.append(w_down[(j - 1) * FS:j * FS])
    slots.append(w_down[(STEPS - 1) * FS:])
    return slots


def mixed_columns(w, which):
    return np.concatenate([columns(w[:, c:c + P]) for c in which])


def kernel(x, ffn1_w_gate, ffn1_w_up, ffn1_w_down, ffn2_w_gate, ffn2_w_up, ffn2_w_down, norm_pre,
           norm_post, ab_w_in, ab_w_out, lru_conv_w, lru_conv_b, lru_gate_a_w, lru_gate_a_b,
           lru_gate_x_w, lru_gate_x_b, lru_lambda, c_w_in, c_conv_w, c_w_out, c_2, ctx_2, c_ctx_2,
           ada_w_2, ada_b_2, ffn1_norm_pre_2, ffn1_norm_post_2, ffn1_w_gate_2, ffn1_w_up_2,
           ffn1_w_down_2, mix_norm_pre_2, mix_norm_post_2, w_in_2, fourier_w_2, conv_w_2, conv_b_2,
           dt_bias_2, a_log_2, d_skip_2, ssd_norm_2, w_out_2, ffn2_norm_pre_2, ffn2_norm_post_2,
           ffn2_w_gate_2, ffn2_w_up_2, ffn2_w_down_2):
    first = swiglu_slots(ffn1_w_gate_2[0], ffn1_w_up_2[0], ffn1_w_down_2[0])
    w_in, dt_at = w_in_2[0], 4 * 256 + 512 + SSD_W + 512
    ab, c_in = ab_w_in[0], c_w_in[0]
    phases = {
        "ada": [wide(ada_w_2[0][:, 512 * i:512 * (i + 1)]) for i in range(ADA_CH)],
        "ctx_ffn": first,
        "ctx_mix": [narrow(w_in[:, dt_at:]), columns(w_in[:, 1024 + 512:dt_at])],
        "ffn_0": swiglu_slots(ffn1_w_gate[0], ffn1_w_up[0], ffn1_w_down[0]),
        "ab": [columns(ab[:, 1536:2560])] + [wide(ab[:, 512 * i:512 * (i + 1)]) for i in range(3)]
        + [ab_w_out[0][512:], ab_w_out[0][:512]],
        "ffn_1": swiglu_slots(ffn2_w_gate[0], ffn2_w_up[0], ffn2_w_down[0]),
        "ffn_2": swiglu_slots(ffn1_w_gate[1], ffn1_w_up[1], ffn1_w_down[1]),
        "sc": [mixed_columns(c_in, [k * D + i * P for i in range(KT) for k in (1, 2, 0)]), c_w_out[0]],
        "ffn_3": swiglu_slots(ffn2_w_gate[1], ffn2_w_up[1], ffn2_w_down[1]),
        "ffn_4": first,
        "ssd": [narrow(w_in[:, dt_at:]), columns(w_in[:, 1024:dt_at]), wide(w_in[:, :512]), wide(w_in[:, 512:1024]),
                w_out_2[0]],
        "ffn_5": swiglu_slots(ffn2_w_gate_2[0], ffn2_w_up_2[0], ffn2_w_down_2[0]),
    }
    stream = np.concatenate([w for name, _ in PHASES for w in phases[name]])
    assert stream.shape == (NSLOT * P, SLOT)
    pre = np.stack([ffn1_norm_pre_2[0], mix_norm_pre_2[0], norm_pre[0, 0], norm_pre[0, 1], norm_pre[0, 2],
                    norm_pre[1, 0], norm_pre[1, 1], norm_pre[1, 2], ffn1_norm_pre_2[0], mix_norm_pre_2[0],
                    ffn2_norm_pre_2[0]])
    post = np.stack([ffn1_norm_post_2[0], np.zeros(D, np.float32), norm_post[0, 0], norm_post[0, 1], norm_post[0, 2],
                     norm_post[1, 0], norm_post[1, 1], norm_post[1, 2], ffn1_norm_post_2[0], mix_norm_post_2[0],
                     ffn2_norm_post_2[0]])

    def pairs(w):
        bd = np.zeros((P, len(w) // 2, P), np.float32)
        for h in range(len(w)):
            at = slice(HD * (h % 2), HD * (h % 2) + HD)
            bd[at, h // 2, at] = w[h]
        return bd

    def tiles(v):
        return np.moveaxis(v.reshape(*v.shape[:-1], -1, P), (-1, -2), (0, 1))

    lru_cols = np.concatenate([tiles(lru_conv_w[0])] + [tiles(v.reshape(1, LRU_W)) for v in
                              (lru_conv_b[0], lru_gate_a_b[0], lru_gate_x_b[0], lru_lambda[0])], axis=2)
    i = np.arange(P)
    pos = np.arange(TOK)
    angle = pos[:, None] * 500000.0 ** (-np.arange(0, 2 * HALF_ROT, 2) / (2 * HALF_ROT))[None, :]
    diag = np.where(i[None, :] <= i[:, None], 0.0, -1e30)
    turn_l = 2 * np.pi * (np.outer(pos, pos) % TOK) / TOK
    turn_d = 2 * np.pi * (np.outer(np.arange(HD), np.arange(HD)) % HD) / HD
    by_tile = lambda m: m.reshape(TT, P, TOK).transpose(1, 0, 2)
    small_arrays = {
        "ident": np.eye(P),
        "lru_cols": lru_cols,
        "gate_bd": np.stack([pairs(lru_gate_a_w[0]), pairs(lru_gate_x_w[0])], axis=1),
        "rope": np.stack([np.cos(angle), np.sin(angle)], axis=1).reshape(TT, P, 2, HALF_ROT).transpose(1, 0, 2, 3),
        "causal": np.concatenate([diag, np.zeros((P, P)), diag], axis=1),
        "sc_cols": tiles(c_conv_w[0]),
        "ssd_cols": np.concatenate([tiles(conv_w_2[0]), tiles(conv_b_2)], axis=2),
        "tri": np.stack([by_tile(pos[:, None] <= pos[None, :]), by_tile(pos[:, None] >= pos[None, :])], axis=1),
        "dft_l": np.stack([by_tile(np.cos(turn_l) / 16), by_tile(np.sin(turn_l) / 16)], axis=1),
        "dft_d": np.stack([np.kron(np.eye(2), np.cos(turn_d) / 8), np.kron(np.eye(2), -np.sin(turn_d) / 8)], axis=1),
        "fourier_bd": pairs(fourier_w_2[0]),
        "c_cols": np.concatenate([tiles(c_2), tiles(c_ctx_2[None, :])], axis=2).transpose(0, 2, 1),
        "comb": np.pad([[1, 0], [1, 0], [0, 1], [0, 1]], ((0, P - 4), (0, P - 2))),
        "ssd_rows": np.concatenate([dt_bias_2.reshape(1, NDT), a_log_2.reshape(1, NDT), d_skip_2.reshape(1, SSD_H)], axis=1),
        "ssd_norm": ssd_norm_2,
        "ada_b": ada_b_2,
    }

    import concourse.bacc as bacc
    from concourse.bass_utils import run_bass_kernel_spmd

    nc = bacc.Bacc("TRN2", target_bir_lowering=False, num_devices=1)
    arrays = {"weights": stream, "x_in": x[0], "ctx_in": ctx_2[0], "pre_rows": pre, "post_rows": post}
    arrays.update(small_arrays)
    arrays = {name: np.ascontiguousarray(v, dtype=np.float32) for name, v in arrays.items()}
    aps = {name: nc.dram_tensor("in_" + name, v.shape, F32, kind="ExternalInput").ap() for name, v in arrays.items()}
    mod = nc.dram_tensor("mod", [2, N_MOD * D], F32, kind="Internal").ap()
    out = nc.dram_tensor("out", [TOK, D], F32, kind="ExternalOutput").ap()
    build(nc, aps["weights"], aps["x_in"], aps["ctx_in"], aps["pre_rows"], aps["post_rows"],
          {name: aps[name] for name in small_arrays}, mod, out)
    nc.compile()
    results = run_bass_kernel_spmd(nc, [{"in_" + name: v for name, v in arrays.items()}], core_ids=[0])
    return results.results[0]["out"].reshape(1, TOK, D)
```

```python
from contextlib import ExitStack

import numpy as np

import concourse.bass as bass
from concourse import mybir

F32 = mybir.dt.float32
F32R = mybir.dt.float32r
ACT = mybir.ActivationFunctionType
ALU = mybir.AluOpType
AX = mybir.AxisListType

P = 128
D = 1024
KT = D // P
TOK = 256
TT = TOK // P
LOW = 32
FF = 2816
FS = 256
STEPS = FF // FS
HEADS, HD = 8, 64
HALF_ROT = HD // 8
LRU_W = 512
LT = LRU_W // P
LRU_CONV = 4
LRU_C = 8.0
SC_CONV = 3
SSD_H, SSD_P = 12, 64
SSD_W = SSD_H * SSD_P
SSD_G = 4
GW = SSD_W // SSD_G
HPG = SSD_H // SSD_G
FOURIER = 256
XBC_T = (512 + SSD_W + 512) // P
CM_T, XS_T, BM_T = 0, 4, 10
NDT = 2 * SSD_H
N_MOD = 9
EPS = 1e-6
SLOT = 1024
RING = 6
SLOTS_FFN = 6 * STEPS
ADA_CH = N_MOD * D // 512

ADA_FIRST = 3
PHASES = [("ffn_0", SLOTS_FFN + 4 * ADA_CH), ("ab", 28), ("ffn_1", SLOTS_FFN),
          ("ctx_ffn", SLOTS_FFN), ("ffn_2", SLOTS_FFN), ("sc", 32), ("ctx_mix", 11), ("ffn_3", SLOTS_FFN),
          ("ffn_4", SLOTS_FFN), ("ssd", 31), ("ffn_5", SLOTS_FFN)]
BASE, NSLOT = {}, 0
for _name, _n in PHASES:
    BASE[_name] = NSLOT
    NSLOT += _n
SUB = [name for name, _ in PHASES]
FFNS = [s for s, name in enumerate(SUB) if "ffn" in name]
CTX = [SUB.index("ctx_ffn"), SUB.index("ctx_mix")]
TAIL = CTX[1] + 1
WITH_POST = [s for s, name in enumerate(SUB) if name != "ctx_mix"]
MOD = {CTX[0]: (1, 0, 1, 2), CTX[1]: (1, 3, 4, None), SUB.index("ffn_4"): (0, 0, 1, 2), SUB.index("ssd"): (0, 3, 4, 5),
       SUB.index("ffn_5"): (0, 6, 7, 8)}
SOURCE = {s: max([q for q in range(s) if (q in CTX) == (s in CTX)], default=None) for s in range(len(SUB))}
EARLY = [s for s in range(1, len(SUB)) if SOURCE[s] != s - 1]
READY = [s for s in EARLY if s in FFNS and s - 1 in FFNS]
LEFT = {s: 2 if s in FFNS else 1 if s in WITH_POST else 0 for s in range(len(SUB))}
NORMS = [("pre", 0, t) for t in range(TT)]
for _s in range(len(SUB)):
    _posts = [("post", _s, t) for t in range(TT)] if _s in WITH_POST else []
    _pres = [("pre", _s + 1, t) for t in range(TT)] if _s + 1 < len(SUB) else []
    NORMS += _pres + _posts if _s + 1 in EARLY else _posts + _pres
NORM_N = {k: i + 1 for i, k in enumerate(NORMS)}
PRE_DMA_N, POST_DMA_N, PRE_MOD_N, POST_MOD_N = {}, {}, {}, {}
for _s in range(len(SUB)):
    PRE_DMA_N[_s] = PRE_DMA_N.get(_s - 1, 0) + 16 * (3 if _s in MOD else 1)
    PRE_MOD_N[_s] = PRE_MOD_N.get(_s - 1, 0) + (_s in MOD)
    POST_DMA_N[_s] = POST_DMA_N.get(_s - 1, 0) + 16 * ((_s in WITH_POST) + (_s in WITH_POST and _s in MOD))
    POST_MOD_N[_s] = POST_MOD_N.get(_s - 1, 0) + (_s in WITH_POST and _s in MOD)
X_NEW_N = {s: TT * (i + 1) for i, s in enumerate(WITH_POST)}

FIRST_N = {}
for _s in range(len(SUB)):
    for _k in (["gu"] if _s in FFNS and _s not in READY else []) + (["dn"] if _s in WITH_POST else []):
        FIRST_N[_k, _s] = len(FIRST_N) + 1
LAST = [BASE[name] + dict(PHASES)[name] for name in SUB]
MIX_AB, MIX_SC, MIX_SSD = 3, 2, 5
MIX0 = {"ab": 0, "sc": MIX_AB, "ssd": MIX_AB + MIX_SC}


def build(nc, weights, x_in, ctx_in, pre_rows, post_rows, small, mod, out):
    with ExitStack() as stack:
        def sb(name, shape, dt=F32):
            return stack.enter_context(nc.sbuf_tensor(name, shape, dt))

        def sem(name):
            return stack.enter_context(nc.semaphore(name))

        raw = sb("raw", [P, RING, SLOT])
        w_hi = sb("w_hi", [P, RING, SLOT], F32R)
        w_lo = sb("w_lo", [P, RING, SLOT], F32R)
        hT_hi = sb("hT_hi", [P, KT, TOK], F32R)
        hT_lo = sb("hT_lo", [P, KT, TOK], F32R)
        actT_hi = sb("actT_hi", [P, 2, TOK], F32R)
        actT_lo = sb("actT_lo", [P, 2, TOK], F32R)
        silu = sb("silu", [P, TT, FS])
        act_tok = sb("act_tok", [P, TT, FS])
        x = sb("x", [P, TT, D])
        xn = sb("xn", [P, TT, D])
        pre_row = sb("pre_row", [P, D])
        shift_row = sb("shift_row", [P, D])
        post_row = sb("post_row", [P, D])
        mod_row = sb("mod_row", [P, D])
        ssq = sb("ssq", [P, 4])
        ms = sb("ms", [P, 4])
        rstd = sb("rstd", [P, 4])
        neg_half = sb("neg_half", [P, 8])
        state0 = sb("state0", [P, 2, SSD_G, GW])
        arena = sb("arena", [P, 13580])

        ident = sb("ident", [P, P])
        lru_cols = sb("lru_cols", [P, LT, 8])
        rope = sb("rope", [P, TT, 2, HALF_ROT])
        sc_cols = sb("sc_cols", [P, KT, SC_CONV])
        ssd_cols = sb("ssd_cols", [P, XBC_T, 4])
        ssd_rows = sb("ssd_rows", [P, 2 * NDT + SSD_H])
        ssd_norm = sb("ssd_norm", [P, SSD_W])
        tri = sb("tri", [P, 2, TT, TOK])
        dft_l = sb("dft_l", [P, 2, TT, TOK])
        dft_d = sb("dft_d", [P, 2, P])
        fourier_bd = sb("fourier_bd", [P, 2, P])
        c_cols = sb("c_cols", [P, 2, KT])
        silu_c = sb("silu_c", [P, 2, KT])
        c_split = sb("c_split", [P, KT, 64], F32R)
        dt_tmp = sb("dt_tmp", [P, 6, TT * NDT])
        dt = sb("dt", [P, TT, NDT])
        dta = sb("dta", [P, TT, NDT])
        neg_a = sb("neg_a", [P, NDT])
        pcol = sb("pcol", [P, TT + 1, NDT])
        exp_p = sb("exp_p", [P, TT, NDT])
        prow = sb("prow", [SSD_H, 2, TOK])
        gstat = sb("gstat", [P, 3, TT * SSD_G])

        dn = stack.enter_context(nc.psum_tensor("dn", [P, TT, D], F32))
        gu = stack.enter_context(nc.psum_tensor("gu", [P, TT, 512], F32))
        tp = stack.enter_context(nc.psum_tensor("tp", [P, TT, 512], F32))

        def part(at, *shape):
            n = int(np.prod(shape))
            v = arena[:, at:at + n]
            if len(shape) == 2:
                v = v.rearrange("p (a b) -> p a b", a=shape[0])
            elif len(shape) == 3:
                v = v.rearrange("p (a b c) -> p a b c", a=shape[0], b=shape[1])
            return v

        mod_bias = arena[0:2, 0:N_MOD * D]
        mod_sum = arena[0:2, N_MOD * D:N_MOD * D + 1536]
        mod_out = arena[0:2, N_MOD * D + 1536:N_MOD * D + 3072]
        mod_low = mod_row[0:2, 480:992]

        ctx_x = arena[:, 11532:11532 + TT * D].rearrange("p (t d) -> p t d", t=TT)

        lx = part(0, LT, TOK + LRU_CONV - 1)
        xc = part(1036, LT, TOK)
        gelu = part(2060, LT, TOK)
        rgate = part(3084, LT, TOK)
        igate = part(4108, LT, TOK)
        th = part(5132, LT, TOK)
        decay = part(6156, LT, TOK)
        vtok = part(7180, TT, HEADS * HD)
        qT = part(8204, HEADS // 2, TOK)
        kT = part(9228, HEADS // 2, TOK)
        masked = part(10252, 2, 3 * P)
        expo = part(11020, 2, 3 * P)
        expT = part(11788, 2, 3 * P)
        attn = part(12556, TT, HEADS * HD)
        qk = xn[:, :, :].rearrange("p t (h d) -> p t h d", h=2 * HEADS)
        rope_t = silu[:, :, :].rearrange("p a b -> p (a b)")
        rope_u = act_tok[:, :, :].rearrange("p a b -> p (a b)")

        causal = mod_row[:, 0:3 * P]
        lru_tmp = mod_row[:, 384:416].rearrange("p (q i) -> p q i", q=8)
        soft = mod_row[:, 416:480].rearrange("p (q h t) -> p q h t", q=4, h=HEADS)
        gate_bd = shift_row[:].rearrange("p (g i c) -> p g i c", g=2, i=LT)

        cgate = part(0, 2, 2 * TOK)
        cx = part(1024, KT, TOK + SC_CONV - 1)
        conv_y = part(1024 + 2064, KT, TOK)

        row_one = hT_hi[0:SSD_H, 5, 0:SSD_H]
        row_hi, row_lo = (v[0:SSD_H, 6:8, :] for v in (hT_hi, hT_lo))
        xbc_in = part(0, XBC_T, TOK + 2)
        xbc = part(3612, XBC_T, TOK)
        y_acc = part(0, TT, SSD_W)
        y_sum = part(1536, TT, SSD_W)
        bm_tok = part(1536, TT, 512)
        f_mid = part(3612 + 1024, 2, 2, TOK)
        f_T = part(3612 + 2048, 2, TOK)
        decays = [part(at, 3 * TOK) for at in (1536, 3612 + 1024, 3612 + 1792)]
        xs_tok = part(7196, TT, SSD_W)
        x_dt = [part(8732, TT, SSD_W), part(10268, TT, SSD_W)]
        cb_m = part(11804, 3 * TOK)
        y_off = part(12572, 2, 3 * 2 * SSD_P)
        u_tok = xn[:, :, 0:FOURIER]
        z_tok = xn[:, :, FOURIER:D]

        landed = [sem(f"landed_{r}") for r in range(RING)]
        hi_ready, lo_ready, slot_used = sem("hi_ready"), sem("lo_ready"), sem("slot_used")
        consts, late_consts, c_loaded, ctx_loaded, x_loaded, stored = sem("consts"), sem("late_consts"), sem("c_loaded"), sem("ctx_loaded"), sem("x_loaded"), sem("stored")
        row_pre, row_post, pre_mod, post_mod = sem("row_pre"), sem("row_post"), sem("pre_mod"), sem("post_mod")
        halves = sem("halves")
        ssq_ready, rstd_ready, x_new, xn_ready = sem("ssq_ready"), sem("rstd_ready"), sem("x_new"), sem("xn_ready")
        hT_psum, hT_hi_ready, hT_lo_ready = sem("hT_psum"), sem("hT_hi_ready"), sem("hT_lo_ready")
        first_tok = sem("first_tok")
        silu_ready, act_ready = sem("silu_ready"), sem("act_ready")
        actT_psum, actT_hi_ready, actT_lo_ready = sem("actT_psum"), sem("actT_hi_ready"), sem("actT_lo_ready")
        dve_step, pool_step = sem("dve_step"), sem("pool_step")
        c_ready, c_split_ready = sem("c_ready"), sem("c_split_ready")
        ada_low, ada_out, ada_biased, ada_stored = sem("ada_low"), sem("ada_out"), sem("ada_biased"), sem("ada_stored")
        mixT_psum, mix_hi, mix_lo = sem("mixT_psum"), sem("mix_hi"), sem("mix_lo")
        ab_evac, xc_ready, gates_done, gates_ready = sem("ab_evac"), sem("xc_ready"), sem("gates_done"), sem("gates_ready")
        lam_z, lam_exp, lru_c_ready = sem("lam_z"), sem("lam_exp"), sem("lru_c_ready")
        lru_tanh, lru_decay, lru_ratio, lru_root, rec_ready = sem("lru_tanh"), sem("lru_decay"), sem("lru_ratio"), sem("lru_root"), sem("rec_ready")
        roped, qkT_psum, qkT_ready = sem("roped"), sem("qkT_psum"), sem("qkT_ready")
        scores_done, masked_ready, exp_ready = sem("scores_done"), sem("masked_ready"), sem("exp_ready")
        expT_psum, expT_ready, attn_psum, attn_ready = sem("expT_psum"), sem("expT_ready"), sem("attn_psum"), sem("attn_ready")
        sc_gate, sc_mixed = sem("sc_gate"), sem("sc_mixed")
        dt_z, dt_exp, dta_ready, a_exp = sem("dt_z"), sem("dt_exp"), sem("dta_ready"), sem("a_exp")
        p_psum, p_ready, p_arg, p_exp = sem("p_psum"), sem("p_ready"), sem("p_arg"), sem("p_exp")
        pads, xbc_evac, conv_done, xbc_ready = sem("pads"), sem("xbc_evac"), sem("conv_done"), sem("xbc_ready")
        tokT_psum, tok_ready, xdt_ready = sem("tokT_psum"), sem("tok_ready"), sem("xdt_ready")
        state_psum, state_ready, wide_ready = sem("state_psum"), sem("state_ready"), sem("wide_ready")
        four_psum, four_ready = sem("four_psum"), sem("four_ready")
        yoff_psum, yoff_used, cb_psum, cb_ready = sem("yoff_psum"), sem("yoff_used"), sem("cb_psum"), sem("cb_ready")
        rows_psum, arg_ready, dec_ready, g_ready = sem("rows_psum"), sem("arg_ready"), sem("dec_ready"), sem("g_ready")
        row_split_hi, row_split, y_taken, y_gated = sem("row_split_hi"), sem("row_split"), sem("y_taken"), sem("y_gated")
        y_psum, gsq_ready, gr_ready, y_ready = sem("y_psum"), sem("gsq_ready"), sem("gr_ready"), sem("y_ready")

        late_tiles = {"ada_b": mod_bias, "lru_cols": lru_cols, "rope": rope, "causal": causal, "sc_cols": sc_cols, "ssd_cols": ssd_cols,
                      "tri": tri, "dft_l": dft_l, "dft_d": dft_d, "fourier_bd": fourier_bd, "gate_bd": gate_bd}
        ALL_LATE = 16 * (len(late_tiles) + 2)

        def stream_of(s):
            return ctx_x if s in CTX else x

        def dn_bank(b):
            return dn[:, b // 2, (b % 2) * 512:(b % 2) * 512 + 512]

        def any_bank(b):
            return dn_bank(b) if b < 4 else gu[:, b - 4, :] if b < 6 else tp[:, b - 6, :]

        def ada_bank(m):
            return dn_bank(m) if m < ADA_FIRST else tp[:, 1, :]

        def last_act(s):
            return (actT_hi, actT_lo) if s == 0 or s + 1 in READY else (hT_hi, hT_lo)

        def xbc_bank(turn, p):
            return dn_bank(p % 4) if turn else any_bank([4, 5, 0, 1, 2][p])

        def in_bank(s, t, half):
            return gu[:, half, :] if t and s not in FFNS else tp[:, half, :]

        x_cols = dn[:, :, :].rearrange("p t d -> p (t d)")

        block = stack.enter_context(nc.Block())

        @block.sync
        def _(sp):
            def load(n_first, r, it):
                n = n_first + r
                if n >= RING:
                    sp.wait_ge(lo_ready, n - RING + 1 + RING * it)
                sp.dma_start(raw[:, r, :], weights[bass.ts(n + RING * it, P), :]).then_inc(landed[r], 16)

            sp.dma_start(x[:], x_in.rearrange("(t p) d -> p t d", p=P)).then_inc(x_loaded, 16)
            for r in range(RING):
                load(0, r, 0)
            with sp.Fori(0, NSLOT // RING - 1) as it:
                for r in range(RING):
                    load(RING, r, it)

        def slot_landed(eng, n, it=0):
            eng.wait_ge(landed[n % RING], 16 * (n // RING + 1) + 16 * it)

        @block.tensor
        def _(pe):
            def transposed(s, t):
                pe.wait_ge(xn_ready, TT * s + t + 1)
                if t and s in FFNS:
                    pe.wait_ge(hT_lo_ready, 2 * (TT * s + t))
                for half in range(2):
                    for q in range(4):
                        k = 4 * half + q
                        m = pe.transpose(in_bank(s, t, half)[:, q * P:(q + 1) * P], xn[:, t, k * P:(k + 1) * P], ident[:])
                    m.then_inc(hT_psum, 1)

            def hT_there(s, t):
                pe.wait_ge(hT_lo_ready, 2 * (TT * s + t) + 2)

            def half_there(s, t):
                pe.wait_ge(hT_lo_ready, 2 * (TT * s + t) + 1)

            def wide_slot(n, si, tiles, bank, it=0, used=True):
                pe.wait_ge(lo_ready, n + 1 + RING * it)
                r = n % RING
                for kk in range(2):
                    k = 2 * si + kk
                    for t in tiles:
                        for q, (h, w) in enumerate(((hT_hi, w_hi), (hT_lo, w_hi), (hT_hi, w_lo))):
                            m = pe.matmul(bank[:, t, :], h[:, k, t * P:(t + 1) * P],
                                          w[:, r, kk * 512:(kk + 1) * 512],
                                          start=k == 0 and q == 0, stop=k == KT - 1 and q == 2)
                if used:
                    m.then_inc(slot_used, 1)
                return m

            def col_slot(n, o):
                pe.wait_ge(lo_ready, n + 1)
                r = n % RING
                for k in range(KT):
                    for q, (h, w) in enumerate(((hT_hi, w_hi), (hT_lo, w_hi), (hT_hi, w_lo))):
                        m = pe.matmul(o, w[:, r, k * P:(k + 1) * P], h[:, k, :],
                                      start=k == 0 and q == 0, stop=k == KT - 1 and q == 2)
                m.then_inc(slot_used, 1)

            def down_slot(n, a_hi, a_lo, k, tiles, start, stop, it=0, used=True):
                pe.wait_ge(lo_ready, n + 1 + RING * it)
                r = n % RING
                for t in tiles:
                    for half in range(2):
                        c = slice(512 * half, 512 * (half + 1))
                        for q, (a, w) in enumerate(((a_hi, w_hi), (a_lo, w_hi), (a_hi, w_lo))):
                            m = pe.matmul(dn[:, t, c], a[:, k, t * P:(t + 1) * P], w[:, r, c],
                                          start=start and q == 0, stop=stop and q == 2)
                if used:
                    m.then_inc(slot_used, 1)
                return m

            def out_proj(n, order, parts, first=True):
                for i, k in enumerate(order):
                    pe.wait_ge(mix_lo, parts[k])
                    if i < len(order) - 1:
                        down_slot(n + i, hT_hi, hT_lo, k, range(TT), first and i == 0, False)
                    else:
                        down_slot(n + i, hT_hi, hT_lo, k, [0], False, True, used=False).then_inc(first_tok, 1)
                        down_slot(n + i, hT_hi, hT_lo, k, [1], False, True)

            def ada_chunk(n, m, it=0, r=0):
                if m >= ADA_FIRST:
                    pe.wait_ge(ada_out, m + ADA_FIRST * it)
                for si in range(4):
                    pe.wait_ge(lo_ready, n + si + 1 + RING * r)
                    for kk in range(2):
                        k = 2 * si + kk
                        for q, w in enumerate((w_hi, w_lo)):
                            mm = pe.matmul(ada_bank(m)[0:64, :], c_split[:, k, :],
                                           w[:, (n + si) % RING, kk * 512:(kk + 1) * 512],
                                           start=k == 0 and q == 0, stop=k == KT - 1 and q == 1)
                    mm.then_inc(slot_used, 1)

            def ffn(s, n0):
                c0 = FFNS.index(s) * STEPS
                end = LAST[s] - 2

                def act_transposed(c, it=0, bank=tp[:, 0, :]):
                    pe.wait_ge(act_ready, TT * (c + 1) + TT * it)
                    for t in range(TT):
                        for kk in range(2):
                            m = pe.transpose(bank[:, kk * TOK + t * P:kk * TOK + (t + 1) * P],
                                             act_tok[:, t, kk * P:(kk + 1) * P], ident[:])
                    m.then_inc(actT_psum, 1)

                def gate_up(n, r=0):
                    for si in range(4):
                        wide_slot(n + si, si, range(TT), gu, it=r)

                def down(n, c, first=False, r=0, it=0):
                    pe.wait_ge(actT_lo_ready, c + 1 + it)
                    for kk in range(2):
                        down_slot(n + kk, actT_hi, actT_lo, kk, range(TT), first and kk == 0, False, it=r)

                def step(j, it=0):
                    n = n0 + 4 + 6 * (j - 1)
                    act_transposed(c0 + j - 1, it)
                    gate_up(n, it)
                    if j == 1:
                        if s == TAIL:
                            context_states()
                        if s in EARLY:
                            pe.wait_ge(x_new, X_NEW_N[max(WITH_POST[:WITH_POST.index(s)])])
                    down(n + 4, c0 + j - 1, j == 1, it, it)

                def steps_with_ada(n, j, m, first=False, it=0):
                    r, i2 = 4 * it, 2 * it
                    act_transposed(c0 + j - 1, i2)
                    gate_up(n, r)
                    ada_chunk(n + 4, m, it, r)
                    down(n + 8, c0 + j - 1, first, r, i2)
                    act_transposed(c0 + j, i2)
                    gate_up(n + 10, r)
                    ada_chunk(n + 14, m + 1, it, r)
                    down(n + 18, c0 + j, False, r, i2)
                    ada_chunk(n + 20, m + 2, it, r)

                if s in READY:
                    gate_up(n0)
                else:
                    transposed(s, 0)
                    if s == TAIL:
                        context_x_tokens()
                    half_there(s, 0)
                    wide_slot(n0, 0, [0], gu, used=False)
                    wide_slot(n0 + 1, 1, [0], gu, used=False)
                    hT_there(s, 0)
                    transposed(s, 1)
                    wide_slot(n0 + 2, 2, [0], gu, used=False)
                    wide_slot(n0 + 3, 3, [0], gu, used=False).then_inc(first_tok, 1)
                    hT_there(s, 1)
                    for si in range(4):
                        wide_slot(n0 + si, si, [1], gu)
                    if s == TAIL:
                        context_b_tokens()
                if s == 0:
                    pe.wait_ge(c_split_ready, 1)
                    for m in range(ADA_FIRST):
                        ada_chunk(n0 + 4 + 4 * m, m)
                    steps_with_ada(n0 + 16, 1, ADA_FIRST, first=True)
                    with pe.Fori(0, STEPS // 2 - 1) as it:
                        steps_with_ada(n0 + 40, 3, 2 * ADA_FIRST, it=it)
                    act_transposed(c0 + STEPS - 1)
                else:
                    step(1)
                    with pe.Fori(0, STEPS - 3) as it:
                        step(2, it)
                    act_transposed(c0 + STEPS - 2)
                    gate_up(end - 6)
                    pe.wait_ge(actT_lo_ready, c0 + STEPS - 1)
                    if s + 1 in READY:
                        transposed(s + 1, 0)
                        down(end - 2, c0 + STEPS - 2)
                        act_transposed(c0 + STEPS - 1, bank=gu[:, 0, :])
                        transposed(s + 1, 1)
                    else:
                        down_slot(end - 2, actT_hi, actT_lo, 0, range(TT), False, False)
                        act_transposed(c0 + STEPS - 1)
                        down_slot(end - 1, actT_hi, actT_lo, 1, range(TT), False, False)
                pe.wait_ge(actT_lo_ready, c0 + STEPS)
                a_hi, a_lo = last_act(s)
                down_slot(end, a_hi, a_lo, 0, [0], False, False, used=False)
                down_slot(end + 1, a_hi, a_lo, 1, [0], False, True, used=False).then_inc(first_tok, 1)
                down_slot(end, a_hi, a_lo, 0, [1], False, False)
                down_slot(end + 1, a_hi, a_lo, 1, [1], False, True)
                if s + 1 in READY:
                    hT_there(s + 1, 1)

            def ab(s, n0):
                pe.wait_ge(late_consts, ALL_LATE)
                for t in range(TT):
                    transposed(s, t)
                hT_there(s, 1)
                for i in range(LT):
                    col_slot(n0 + i, dn[:, 0, i * TOK:(i + 1) * TOK])
                for i in range(LT):
                    col_slot(n0 + LT + i, dn[:, 1, i * TOK:(i + 1) * TOK])
                for si in range(4):
                    wide_slot(n0 + 8 + si, si, range(TT), gu)
                pe.wait_ge(xc_ready, 1)
                pe.wait_ge(ab_evac, 4)
                for gate in range(2):
                    for i in range(LT):
                        m = pe.matmul(dn[:, gate, i * TOK:(i + 1) * TOK], gate_bd[:, gate, i, :], xc[:, i, :],
                                      start=True, stop=True)
                    m.then_inc(gates_done, 1)
                for si in range(4):
                    wide_slot(n0 + 12 + si, si, range(TT), tp)
                pe.wait_ge(ab_evac, 6)
                for si in range(4):
                    wide_slot(n0 + 16 + si, si, range(TT), gu)
                pe.wait_ge(roped, 1)
                for which, bank in ((0, tp), (1, gu)):
                    if which:
                        pe.wait_ge(ab_evac, 10)
                    for half in range(2):
                        for pair in range(2):
                            for t in range(TT):
                                h = 8 * which + 2 * (2 * half + pair)
                                m = pe.transpose(bank[:, half, pair * TOK + t * P:pair * TOK + (t + 1) * P],
                                                 qk[:, t, h:h + 2, :].rearrange("p h d -> p (h d)"), ident[:])
                        m.then_inc(qkT_psum, 1)

                def scores(h):
                    bank = (gu, tp)[(h // 2) % 2][:, h % 2, :]
                    rows = slice(HD * (h % 2), HD * (h % 2) + HD)
                    pe.wait_ge(masked_ready, 3 * (h - 4) + 2) if h >= 4 else pe.wait_ge(qkT_ready, 4)
                    pe.matmul(bank[:, 0:P], qT[rows, h // 2, 0:P], kT[rows, h // 2, 0:P], start=True, stop=True)
                    pe.matmul(bank[:, P:P + TOK], qT[rows, h // 2, P:TOK], kT[rows, h // 2, :],
                              start=True, stop=True).then_inc(scores_done, 1)

                def weighted(h):
                    pe.wait_ge(expT_ready, h + 1)
                    eT, v = expT[:, h % 2, :], slice(h * HD, (h + 1) * HD)
                    pe.matmul(dn[:, 1, v], eT[:, 0:P], vtok[:, 0, v], start=True, stop=True)
                    pe.matmul(dn[:, 1, 512 + h * HD:512 + (h + 1) * HD], eT[:, P:2 * P], vtok[:, 0, v],
                              start=True, stop=False)
                    m = pe.matmul(dn[:, 1, 512 + h * HD:512 + (h + 1) * HD], eT[:, 2 * P:3 * P], vtok[:, 1, v],
                                  start=False, stop=True)
                    if h == HEADS - 1:
                        m.then_inc(attn_psum, 1)

                for h in range(4):
                    scores(h)
                pe.wait_ge(gates_ready, 2 * LT)
                for h in range(HEADS):
                    pe.wait_ge(exp_ready, h + 1)
                    if h >= 2:
                        pe.wait_ge(expT_ready, h - 1)
                    for q in range(3):
                        m = pe.transpose(dn[:, 0, (h % 2) * 512 + q * P:(h % 2) * 512 + (q + 1) * P],
                                         expo[:, h % 2, q * P:(q + 1) * P], ident[:])
                    m.then_inc(expT_psum, 1)
                    if h + 4 < HEADS:
                        scores(h + 4)
                    if h:
                        weighted(h - 1)
                weighted(HEADS - 1)
                pe.wait_ge(attn_ready, 1)
                for t in range(TT):
                    for k in range(4):
                        m = pe.transpose(tp[:, t, k * P:(k + 1) * P], attn[:, t, k * P:(k + 1) * P], ident[:])
                    m.then_inc(mixT_psum, 1)
                out_proj(n0 + 20, [4, 5, 6, 7, 0, 1, 2, 3], [MIX0["ab"] + MIX_AB] * 4 + [MIX0["ab"] + 1] * 4)

            def sc(s, n0):
                for t in range(TT):
                    transposed(s, t)
                hT_there(s, 1)
                for q in range(3 * KT):
                    if q >= 8:
                        i, kind = (q - 8) // 3, (q - 8) % 3
                        if kind == 0:
                            pe.wait_ge(sc_gate, i + 1)
                        else:
                            pe.wait_ge(sc_mixed, 2 * i + kind)
                    col_slot(n0 + q, any_bank(q % 8)[:, 0:TOK])
                out_proj(n0 + 3 * KT, range(KT), [MIX0["sc"] + 1] * 4 + [MIX0["sc"] + 2] * 4)

            def dt_slot(n):
                pe.wait_ge(lo_ready, n + 1)
                r = n % RING
                for t in range(TT):
                    for k in range(KT):
                        for q, (h, w) in enumerate(((hT_hi, w_hi), (hT_lo, w_hi), (hT_hi, w_lo))):
                            m = pe.matmul(tp[:, 0, t * NDT:(t + 1) * NDT], h[:, k, t * P:(t + 1) * P],
                                          w[:, r, k * NDT:(k + 1) * NDT],
                                          start=k == 0 and q == 0, stop=k == KT - 1 and q == 2)
                m.then_inc(slot_used, 1)

            def log_decays(turn):
                pe.wait_ge(dta_ready, turn + 1)
                for t in range(TT):
                    for d in range(2):
                        for st in range(TT):
                            m = pe.matmul(tp[:, 1, t * NDT + d * SSD_H:t * NDT + (d + 1) * SSD_H],
                                          tri[:, d, st, t * P:(t + 1) * P], dta[:, st, d * SSD_H:(d + 1) * SSD_H],
                                          start=st == 0, stop=st == 1)
                if turn == 0:
                    for st in range(TT):
                        m = pe.matmul(tp[:, 1, 2 * NDT:3 * NDT], tri[:, 0, 0, P:TOK], dta[:, st, :],
                                      start=st == 0, stop=st == 1)
                else:
                    for d in range(2):
                        for st in range(TT):
                            m = pe.matmul(gu[0:SSD_H, d, 0:TOK], dta[:, st, d * SSD_H:(d + 1) * SSD_H],
                                          tri[:, d, st, :], start=st == 0, stop=st == 1)
                m.then_inc(p_psum, 1)

            def xbc_slots(n, turn, pairs, pair0):
                for p in range(pairs):
                    if turn and p >= 4:
                        pe.wait_ge(xbc_evac, pair0 + p - 3)
                    if turn == 0 and p == 2:
                        pe.wait_ge(x_new, X_NEW_N[CTX[1] - 1])
                    for q in range(2):
                        col_slot(n + 2 * p + q, xbc_bank(turn, p)[:, q * TOK:(q + 1) * TOK])
                    if p == 1:
                        log_decays(turn)

            def turned_tile(o, i, t):
                return pe.transpose(o, xbc[:, i, t * P:(t + 1) * P], ident[:])

            def x_tokens():
                for t in range(TT):
                    for i in range(SSD_W // P):
                        m = turned_tile(x_cols[:, t * SSD_W + i * P:t * SSD_W + (i + 1) * P], XS_T + i, t)
                m.then_inc(tokT_psum, 1)

            def ctx_mix(s, n0):
                for t in range(TT):
                    transposed(s, t)
                hT_there(s, 1)
                dt_slot(n0)
                xbc_slots(n0 + 1, 0, 5, 0)

            def context_x_tokens():
                pe.wait_ge(xbc_evac, 5)
                pe.wait_ge(xbc_ready, 3)
                x_tokens()

            def context_b_tokens():
                pe.wait_ge(xbc_ready, 5)
                for t, bank in enumerate((x_cols[:, TT * SSD_W:], tp[:, 1, :])):
                    for i in range(SSD_G):
                        m = turned_tile(bank[:, i * P:(i + 1) * P], BM_T + i, t)
                m.then_inc(tokT_psum, 1)

            def context_states():
                pe.wait_ge(tok_ready, 2 * TT)
                pe.wait_ge(xdt_ready, 2)
                for d in range(2):
                    for g in range(SSD_G):
                        for t in range(TT):
                            m = pe.matmul(dn[:, d, g * 256:g * 256 + GW], bm_tok[:, t, g * P:(g + 1) * P],
                                          x_dt[d][:, t, g * GW:(g + 1) * GW], start=t == 0, stop=t == 1)
                    m.then_inc(state_psum, 1)
                pe.wait_ge(state_ready, 2)

            def ssd(s, n0):
                for t in range(TT):
                    transposed(s, t)
                hT_there(s, 1)
                dt_slot(n0)
                xbc_slots(n0 + 1, 1, 7, 5)
                pe.wait_ge(p_ready, 2)
                for si in range(4):
                    wide_slot(n0 + 15 + si, si, range(TT), gu)
                for si in range(4):
                    wide_slot(n0 + 19 + si, si, range(TT), tp)
                pe.wait_ge(xbc_evac, 12)
                pe.wait_ge(xbc_ready, 12)
                x_tokens()
                pe.wait_ge(wide_ready, 4)
                for m_ in range(2):
                    for ft in range(2):
                        for st in range(TT):
                            m = pe.matmul(gu[:, m_, ft * TOK:(ft + 1) * TOK], u_tok[:, st, ft * P:(ft + 1) * P],
                                          dft_l[:, m_, st, :], start=st == 0, stop=st == 1)
                m.then_inc(four_psum, 1)
                pe.wait_ge(four_ready, 1)
                for ft in range(2):
                    for m_ in range(2):
                        m = pe.matmul(tp[:, 0, ft * TOK:(ft + 1) * TOK], dft_d[:, m_, :], f_mid[:, m_, ft, :],
                                      start=m_ == 0, stop=m_ == 1)
                m.then_inc(four_psum, 1)
                pe.wait_ge(four_ready, 2)
                for ft in range(2):
                    m = pe.matmul(tp[:, 1, ft * TOK:(ft + 1) * TOK], fourier_bd[:, ft, :], f_T[:, ft, :],
                                  start=True, stop=True)
                m.then_inc(four_psum, 1)
                pe.wait_ge(mix_lo, MIX0["ssd"] + 1)
                for g in range(SSD_G):
                    if g:
                        pe.wait_ge(yoff_used, TT * g)
                    for t in range(TT):
                        for d in range(2):
                            m = pe.matmul(tp[:, t, d * GW:(d + 1) * GW], xbc[:, CM_T + g, t * P:(t + 1) * P],
                                          state0[:, d, g, :], start=True, stop=True)
                    m.then_inc(yoff_psum, 1)
                pe.wait_ge(yoff_used, TT * SSD_G)
                pe.wait_ge(tok_ready, 6)

                def outputs(h):
                    pe.wait_ge(g_ready, h + 1)
                    w, c = decays[h % 3], slice(h * SSD_P, (h + 1) * SSD_P)
                    sums = [[(0, 0, 0), (384, 1, 0), (512, 1, 1)], [(128, 0, 0), (256, 0, 1), (640, 1, 1)]]
                    for t in range(TT):
                        for q, (at, d, st) in enumerate(sums[t]):
                            m = pe.matmul(dn[:, t, c], w[:, at:at + P], x_dt[d][:, st, c], start=q == 0, stop=q == 2)
                    m.then_inc(y_psum, 1)

                pe.wait_ge(xdt_ready, 4)

                def correlations(g):
                    if g >= 2:
                        pe.wait_ge(cb_ready, g - 1)
                    for st in range(TT):
                        m = pe.matmul(tp[:, g % 2, st * TOK:(st + 1) * TOK], xbc[:, BM_T + g, st * P:(st + 1) * P],
                                      xbc[:, CM_T + g, :], start=True, stop=True)
                    m.then_inc(cb_psum, 1)

                def log_rows(h):
                    if h >= 2:
                        pe.wait_ge(arg_ready, h - 1)
                    for q, row in enumerate((row_hi, row_lo)):
                        m = pe.matmul(gu[:, h % 2, :], row_one[:, h:h + 1].broadcast_to([SSD_H, P]),
                                      row.rearrange("p d l -> p (d l)"), start=q == 0, stop=q == 1)
                    m.then_inc(rows_psum, 1)

                pe.wait_ge(row_split, 1)
                log_rows(0)
                correlations(0)
                log_rows(1)
                for h in range(SSD_H):
                    if h % HPG == 0 and h // HPG + 1 < SSD_G:
                        correlations(h // HPG + 1)
                    if h + 2 < SSD_H:
                        log_rows(h + 2)
                    outputs(h)
                pe.wait_ge(y_taken, 1)
                for k in range(2):
                    down_slot(n0 + 23 + k, hT_hi, hT_lo, k, range(TT), k == 0, False)
                for t in range(TT):
                    pe.wait_ge(y_ready, t + 1)
                    for i in range(SSD_W // P):
                        o = tp[:, t, i * P:(i + 1) * P] if i < 4 else gu[:, t, (i - 4) * P:(i - 3) * P]
                        m = pe.transpose(o, y_sum[:, t, i * P:(i + 1) * P], ident[:])
                        if i in (3, 5):
                            m.then_inc(mixT_psum, 1)
                out_proj(n0 + 25, range(2, KT), [MIX0["ssd"] + MIX_SSD] * KT, first=False)

            pe.wait_ge(consts, 16)
            for s, name in enumerate(SUB):
                {"ctx_mix": ctx_mix, "ab": ab, "sc": sc, "ssd": ssd}.get(name, ffn)(s, BASE[name])

        @block.scalar
        def _(act):
            def copy(o, i, done, **kw):
                act.activation(o, i, ACT.Copy, **kw).then_inc(done, 1)

            def upper(n, it=0):
                if n >= NSLOT:
                    return
                slot_landed(act, n, it)
                if n >= RING:
                    act.wait_ge(slot_used, n - RING + 1 + RING * it)
                copy(w_hi[:, n % RING, :], raw[:, n % RING, :], hi_ready)

            def after_slots(n, count, it=0):
                for q in range(count):
                    upper(n + q + RING, it)

            def out_squares(s):
                factor = 0.5 if s in FFNS else 1.0
                for t in range(TT):
                    if t == 0:
                        act.wait_ge(first_tok, FIRST_N["dn", s])
                    else:
                        act.wait_ge(slot_used, LAST[s])
                    act.activation(xn[:, t, :], dn[:, t, :], ACT.Square, scale=1.0 / (factor * D ** 0.5),
                                   accum_out=ssq[:, 2 + t:3 + t]).then_inc(ssq_ready, 1)

            def in_squares(s):
                for t in range(TT):
                    if SOURCE[s] is not None:
                        act.wait_ge(x_new, X_NEW_N[SOURCE[s]] - TT + t + 1)
                    else:
                        act.wait_ge(ctx_loaded if s in CTX else x_loaded, 16)
                    act.activation(xn[:, t, :], stream_of(s)[:, t, :], ACT.Square, scale=1.0 / D ** 0.5,
                                   accum_out=ssq[:, t:t + 1]).then_inc(ssq_ready, 1)

            def in_upper(s, tiles=range(TT)):
                for t in tiles:
                    for half in range(2):
                        act.wait_ge(hT_psum, 2 * (TT * s + t) + half + 1)
                        copy(hT_hi[:, 4 * half:4 * half + 4, t * P:(t + 1) * P],
                             in_bank(s, t, half).rearrange("p (k c) -> p k c", k=4), hT_hi_ready)

            def ada_lower(n, m, r=0):
                act.wait_ge(slot_used, n + RING * r)
                if 0 < m < ADA_FIRST:
                    act.wait_ge(ada_out, m)
                copy(mod_low, ada_bank(m)[LOW:LOW + 2, :], ada_low)

            def ffn(s, n0):
                c0 = FFNS.index(s) * STEPS

                def act_upper(c, it=0, o=actT_hi, bank=tp[:, 0, :]):
                    act.wait_ge(actT_psum, c + 1 + it)
                    copy(o[:, 0:2, :], bank.rearrange("p (k c) -> p k c", k=2), actT_hi_ready)

                def gate(t):
                    act.activation(silu[:, t, :], gu[:, t, 0:FS], ACT.Silu).then_inc(silu_ready, 1)

                def gates(n, r=0):
                    act.wait_ge(slot_used, n + 4 + RING * r)
                    gate(0)
                    gate(1)

                def step(j, it=0):
                    n = n0 + 4 + 6 * (j - 1)
                    act_upper(c0 + j - 1, it)
                    after_slots(n, 3, it)
                    gates(n, it)
                    if s == TAIL and j == 1:
                        context_states()
                    if j == STEPS - 1 and s + 1 in READY:
                        in_upper(s + 1, [0])
                        after_slots(n + 3, 3)
                        act_upper(c0 + STEPS - 1, bank=gu[:, 0, :])
                        in_upper(s + 1, [1])
                    elif j == STEPS - 1:
                        after_slots(n + 3, 2)
                        act_upper(c0 + STEPS - 1, o=last_act(s)[0])
                        after_slots(n + 5, 1)
                    else:
                        after_slots(n + 3, 3, it)

                def steps_with_ada(n, j, it=0):
                    r, i2 = 4 * it, 2 * it
                    act_upper(c0 + j - 1, i2)
                    after_slots(n, 3, r)
                    gates(n, r)
                    after_slots(n + 3, 4, r)
                    ada_lower(n + 8, ADA_FIRST, r)
                    after_slots(n + 7, 3, r)
                    act_upper(c0 + j, i2)
                    after_slots(n + 10, 3, r)
                    gates(n + 10, r)
                    after_slots(n + 13, 4, r)
                    ada_lower(n + 18, ADA_FIRST, r)
                    after_slots(n + 17, 6, r)
                    ada_lower(n + 24, ADA_FIRST, r)
                    after_slots(n + 23, 1, r)

                if s in READY:
                    after_slots(n0, 3)
                    gates(n0)
                else:
                    act.wait_ge(first_tok, FIRST_N["gu", s])
                    gate(0)
                    after_slots(n0, 3)
                    act.wait_ge(slot_used, n0 + 4)
                    gate(1)
                after_slots(n0 + 3, 1)
                if s == TAIL:
                    context_b_tokens()
                if s == 0:
                    act.wait_ge(c_loaded, 16)
                    act.activation(silu_c[:], c_cols[:], ACT.Silu).then_inc(c_ready, 1)
                    for m in range(ADA_FIRST):
                        after_slots(n0 + 4 + 4 * m, 4)
                        ada_lower(n0 + 8 + 4 * m, m)
                    steps_with_ada(n0 + 16, 1)
                    with act.Fori(0, STEPS // 2 - 1) as it:
                        steps_with_ada(n0 + 40, 3, it)
                    act_upper(c0 + STEPS - 1)
                else:
                    step(1)
                    with act.Fori(0, STEPS - 3) as it:
                        step(2, it)
                    if s + 1 in READY:
                        in_squares(s + 1)
                    step(STEPS - 1)

            def lru_gates():
                for g, o in enumerate((rgate, igate)):
                    act.wait_ge(gates_done, g + 1)
                    for i in range(LT):
                        act.activation(o[:, i, :], dn[:, g, i * TOK:(i + 1) * TOK], ACT.Sigmoid,
                                       bias=lru_cols[:, i, 5 + g:6 + g]).then_inc(gates_ready, 1)
                act.wait_ge(lru_c_ready, 1)
                act.wait_ge(gates_ready, LT)
                for i in range(LT):
                    act.activation(th[:, i, :], rgate[:, i, :], ACT.Tanh, scale=lru_tmp[:, 6, i:i + 1]).then_inc(lru_tanh, 1)
                for i in range(LT):
                    act.activation(decay[:, i, :], rgate[:, i, :], ACT.Exp, scale=lru_tmp[:, 7, i:i + 1]).then_inc(lru_decay, 1)

            def ab(s, n0):
                act.wait_ge(late_consts, ALL_LATE)
                act.wait_ge(lam_z, 1)
                act.activation(lru_tmp[:, 1, :], lru_tmp[:, 1, :], ACT.Exp).then_inc(lam_exp, 1)
                for pair in range(2):
                    after_slots(n0 + 2 * pair, 2)
                    act.wait_ge(slot_used, n0 + 2 * pair + 2)
                    copy(lx[:, 2 * pair:2 * pair + 2, LRU_CONV - 1:],
                         dn[:, 0, pair * 512:(pair + 1) * 512].rearrange("p (i c) -> p i c", i=2), ab_evac)
                for pair in range(2):
                    after_slots(n0 + 4 + 2 * pair, 2)
                    act.wait_ge(slot_used, n0 + 4 + 2 * pair + 2)
                    act.activation(gelu[:, 2 * pair:2 * pair + 2, :],
                                   dn[:, 1, pair * 512:(pair + 1) * 512].rearrange("p (i c) -> p i c", i=2),
                                   ACT.Gelu_apprx_tanh).then_inc(ab_evac, 1)
                after_slots(n0 + 8, 4)
                act.wait_ge(slot_used, n0 + 12)
                for t in range(TT):
                    copy(qk[:, t, 0:HEADS, :], gu[:, t, :].rearrange("p (h d) -> p h d", h=HEADS), ab_evac, scale=HD ** -0.5)
                after_slots(n0 + 12, 1)
                lru_gates()
                after_slots(n0 + 13, 3)
                act.wait_ge(slot_used, n0 + 16)
                for t in range(TT):
                    copy(qk[:, t, HEADS:2 * HEADS, :], tp[:, t, :].rearrange("p (h d) -> p h d", h=HEADS), ab_evac)
                act.wait_ge(lru_ratio, 1)
                act.activation(th[:, :, :], th[:, :, :], ACT.Sqrt).then_inc(lru_root, 1)
                after_slots(n0 + 16, 4)
                act.wait_ge(slot_used, n0 + 20)
                for t in range(TT):
                    copy(vtok[:, t, :], gu[:, t, :], ab_evac)
                for which, (o, bank) in enumerate(((qT, tp), (kT, gu))):
                    for half in range(2):
                        act.wait_ge(qkT_psum, 2 * which + half + 1)
                        copy(o[:, 2 * half:2 * half + 2, :], bank[:, half, :].rearrange("p (a c) -> p a c", a=2), qkT_ready)

                def turned(h):
                    act.wait_ge(expT_psum, h + 1)
                    copy(expT[:, h % 2, :], dn[:, 0, (h % 2) * 512:(h % 2) * 512 + 3 * P], expT_ready)

                for h in range(HEADS):
                    act.wait_ge(masked_ready, 3 * h + 3)
                    act.activation(expo[:, h % 2, 0:P], masked[:, h % 2, 0:P], ACT.Exp,
                                   bias=soft[:, 1, h, 0:1], accum_out=soft[:, 2, h, 0:1])
                    act.activation(expo[:, h % 2, P:3 * P], masked[:, h % 2, P:3 * P], ACT.Exp,
                                   bias=soft[:, 1, h, 1:2], accum_out=soft[:, 2, h, 1:2]).then_inc(exp_ready, 1)
                    if h:
                        turned(h - 1)
                turned(HEADS - 1)
                act.wait_ge(rec_ready, 1)
                copy(hT_hi[:, 4:8, :], gelu[:, :, :], mix_hi)
                for t in range(TT):
                    act.wait_ge(mixT_psum, t + 1)
                    copy(hT_hi[:, 0:4, t * P:(t + 1) * P], tp[:, t, :].rearrange("p (k c) -> p k c", k=4), mix_hi)
                after_slots(n0 + 20, 7)

            def sc(s, n0):
                for i in range(KT):
                    act.wait_ge(slot_used, n0 + 3 * i + 1)
                    if i >= 2:
                        act.wait_ge(sc_mixed, 2 * (i - 2) + 1)
                    copy(cgate[:, i % 2, 0:TOK], any_bank(3 * i % 8)[:, 0:TOK], sc_gate)
                    if i < KT - 1:
                        after_slots(n0 + 3 * i, 3)
                    if i == 4 and s + 1 in EARLY:
                        in_squares(s + 1)
                act.wait_ge(slot_used, n0 + 3 * KT)
                for half in range(2):
                    act.wait_ge(sc_mixed, 8 * half + 8)
                    copy(hT_hi[:, 4 * half:4 * half + 4, :], conv_y[:, 4 * half:4 * half + 4, :], mix_hi)
                after_slots(n0 + 3 * KT - 3, 3 + KT - 1)

            def dt_and_conv(turn, n0, pairs, pair0, tile0):
                if turn == 0:
                    act.activation(neg_a[:], ssd_rows[:, NDT:2 * NDT], ACT.Exp).then_inc(a_exp, 1)
                after_slots(n0, 1)
                act.wait_ge(dt_z, turn + 1)
                act.activation(dt_tmp[:, 1, :], dt_tmp[:, 1, :], ACT.Exp).then_inc(dt_exp, 1)

                def convolved(p):
                    act.wait_ge(conv_done, pair0 + p + 1)
                    for q in range(2):
                        i = tile0 + 2 * p + q
                        m = act.activation(xbc[:, i, :], xbc[:, i, :], ACT.Silu, bias=ssd_cols[:, i, 3:4])
                    m.then_inc(xbc_ready, 1)

                for p in range(pairs):
                    n = n0 + 1 + 2 * p
                    after_slots(n, 2)
                    act.wait_ge(slot_used, n + 2)
                    i = tile0 + 2 * p
                    copy(xbc_in[:, i:i + 2, 1:1 + TOK], xbc_bank(turn, p).rearrange("p (i c) -> p i c", i=2), xbc_evac)
                    if turn == 0 and p == pairs - 1:
                        in_upper(TAIL, [0])
                    if p:
                        convolved(p - 1)
                    if p == 2:
                        act.wait_ge(p_psum, turn + 1)
                        if turn == 0:
                            copy(pcol[:, :, :], tp[:, 1, 0:3 * NDT].rearrange("p (t h) -> p t h", t=3), p_ready)
                        else:
                            act.activation(pcol[:, 0:2, :], tp[:, 1, 0:2 * NDT].rearrange("p (t h) -> p t h", t=2), ACT.Copy)
                            copy(prow[:, :, :], gu[0:SSD_H, :, 0:TOK], p_ready)
                    if p == 2 and turn == 0:
                        in_squares(TAIL)
                if turn == 0:
                    act.wait_ge(p_arg, 1)
                    act.activation(exp_p[:, :, :], exp_p[:, :, :], ACT.Exp).then_inc(p_exp, 1)
                    x_tokens(0)
                convolved(pairs - 1)
                if turn == 0:
                    in_upper(TAIL, [1])

            def x_tokens(turn):
                act.wait_ge(tokT_psum, 2 * turn + 1)
                for t in range(TT):
                    copy(xs_tok[:, t, :], x_cols[:, t * SSD_W:(t + 1) * SSD_W], tok_ready)

            def ctx_mix(s, n0):
                dt_and_conv(0, n0, 5, 0, XS_T)

            def context_b_tokens():
                act.wait_ge(tokT_psum, 2)
                for t, bank in enumerate((x_cols[:, TT * SSD_W:], tp[:, 1, :])):
                    copy(bm_tok[:, t, :], bank, tok_ready)

            def context_states():
                for d in range(2):
                    act.wait_ge(state_psum, d + 1)
                    copy(state0[:, d, :, :], dn[:, d, :].rearrange("p (g c) -> p g c", g=SSD_G)[:, :, 0:GW], state_ready)

            def ssd(s, n0):
                dt_and_conv(1, n0, 7, 5, 0)
                act.wait_ge(p_ready, 2)
                act.activation(exp_p[:, :, :], pcol[:, 0:2, :], ACT.Exp).then_inc(p_exp, 1)
                after_slots(n0 + 15, 4)
                act.wait_ge(slot_used, n0 + 19)
                for t in range(TT):
                    act.activation(u_tok[:, t, :], gu[:, t, 0:FOURIER], ACT.Copy)
                for t in range(TT):
                    act.activation(z_tok[:, t, 0:256], gu[:, t, FOURIER:512], ACT.Silu).then_inc(wide_ready, 1)
                after_slots(n0 + 19, 4)
                act.wait_ge(slot_used, n0 + 23)
                for t in range(TT):
                    act.activation(z_tok[:, t, 256:SSD_W], tp[:, t, :], ACT.Silu).then_inc(wide_ready, 1)
                x_tokens(1)
                copy(row_one, ident[0:SSD_H, 0:SSD_H], row_split_hi)
                copy(row_hi, prow[:, :, :], row_split_hi)
                act.wait_ge(four_psum, 1)
                copy(f_mid[:, :, :, :], gu[:, :, :].rearrange("p m (f c) -> p m f c", f=2), four_ready)
                act.wait_ge(four_psum, 2)
                copy(f_T[:, :, :], tp[:, 0, :].rearrange("p (f c) -> p f c", f=2), four_ready)
                act.wait_ge(four_psum, 3)
                copy(hT_hi[:, 0:2, :], tp[:, 1, :].rearrange("p (f c) -> p f c", f=2), mix_hi)
                for h in range(SSD_H):
                    act.wait_ge(arg_ready, h + 1)
                    act.activation(decays[h % 3], decays[h % 3], ACT.Exp).then_inc(dec_ready, 1)
                for t in range(TT):
                    act.wait_ge(y_gated, t + 1)
                    for g in range(SSD_G):
                        c = slice(g * GW, (g + 1) * GW)
                        m = act.activation(y_acc[:, t, c], y_sum[:, t, c], ACT.Square, scale=GW ** -0.5,
                                           accum_out=gstat[:, 0, t * SSD_G + g:t * SSD_G + g + 1])
                    m.then_inc(gsq_ready, 1)
                after_slots(n0 + 23, 2)
                for t in range(TT):
                    c = slice(t * P, (t + 1) * P)
                    act.wait_ge(mixT_psum, 2 + 2 * t + 1)
                    copy(hT_hi[:, 2:6, c], tp[:, t, :].rearrange("p (k c) -> p k c", k=4), mix_hi)
                    act.wait_ge(mixT_psum, 2 + 2 * t + 2)
                    copy(hT_hi[:, 6:8, c], gu[:, t, 0:TOK].rearrange("p (k c) -> p k c", k=2), mix_hi)
                after_slots(n0 + 25, 5)

            act.dma_start(ident[:], small["ident"]).then_inc(consts, 16)
            act.dma_start(c_cols[:], small["c_cols"]).then_inc(c_loaded, 16)
            in_squares(0)
            for n in range(RING):
                upper(n)
            for s, name in enumerate(SUB):
                if s not in READY and s != TAIL:
                    in_upper(s)
                if s:
                    if s in EARLY and s - 1 in WITH_POST:
                        out_squares(s - 1)
                    after_slots(LAST[s - 1] - LEFT[s - 1], LEFT[s - 1])
                {"ctx_mix": ctx_mix, "ab": ab, "sc": sc, "ssd": ssd}.get(name, ffn)(s, BASE[name])
                if s in WITH_POST and s + 1 not in EARLY:
                    out_squares(s)
                    if s + 1 < len(SUB):
                        in_squares(s + 1)

        @block.vector
        def _(dve):
            steps = [0]

            def then(ins):
                steps[0] += 1
                ins.then_inc(dve_step, 1)
                dve.wait_ge(dve_step, steps[0])

            def rest(n, it=0):
                if n >= NSLOT:
                    return
                dve.wait_ge(hi_ready, n + 1 + RING * it)
                r = n % RING
                dve.tensor_tensor(w_lo[:, r, :], raw[:, r, :], w_hi[:, r, :].bitcast(F32),
                                  ALU.subtract).then_inc(lo_ready, 1)

            def after_slots(n, count, it=0):
                for q in range(count):
                    rest(n + q + RING, it)

            def lower(o, i, hi, done):
                dve.tensor_tensor(o, i, hi.bitcast(F32), ALU.subtract).then_inc(done, 1)

            def residual(s, tiles=range(TT)):
                for t in tiles:
                    dve.wait_ge(rstd_ready, NORM_N["post", s, t])
                    if s in MOD:
                        dve.wait_ge(post_mod, POST_MOD_N[s])
                    else:
                        dve.wait_ge(row_post, POST_DMA_N[s])
                    then(dve.scalar_tensor_tensor(xn[:, t, :], dn[:, t, :], rstd[:, 2 + t:3 + t], post_row[:],
                                                  ALU.mult, ALU.mult))
                    xt = stream_of(s)[:, t, :]
                    dve.tensor_tensor(xt, xt, xn[:, t, :], ALU.add).then_inc(x_new, 1)

            def normalised(s):
                for t in range(TT):
                    dve.wait_ge(rstd_ready, NORM_N["pre", s, t])
                    if s in MOD:
                        dve.wait_ge(pre_mod, PRE_MOD_N[s])
                    else:
                        dve.wait_ge(row_pre, PRE_DMA_N[s])
                    m = dve.scalar_tensor_tensor(xn[:, t, :], stream_of(s)[:, t, :], rstd[:, t:t + 1], pre_row[:], ALU.mult, ALU.mult)
                    if s in MOD:
                        then(m)
                        m = dve.tensor_tensor(xn[:, t, :], xn[:, t, :], shift_row[:], ALU.add)
                    m.then_inc(xn_ready, 1)

            def in_lower(s, tiles=range(TT)):
                for t in tiles:
                    for half in range(2):
                        c = (slice(None), slice(4 * half, 4 * half + 4), slice(t * P, (t + 1) * P))
                        dve.wait_ge(hT_hi_ready, 2 * (TT * s + t) + half + 1)
                        lower(hT_lo[c], in_bank(s, t, half).rearrange("p (k c) -> p k c", k=4), hT_hi[c], hT_lo_ready)

            def log1p(tiles):
                u, s1, s2, acc = tiles
                then(dve.tensor_scalar(s1, u, 2.0, None, ALU.add))
                then(dve.reciprocal(s2, s1))
                then(dve.tensor_tensor(s1, u, s2, ALU.mult))
                then(dve.tensor_tensor(s2, s1, s1, ALU.mult))
                then(dve.tensor_scalar(acc, s2, 1.0 / 17, None, ALU.mult))
                for k in range(15, 2, -2):
                    then(dve.scalar_tensor_tensor(acc, acc, 1.0 / k, s2, ALU.add, ALU.mult))
                then(dve.scalar_tensor_tensor(acc, acc, 1.0, s1, ALU.add, ALU.mult))

            def split_c():
                dve.wait_ge(c_ready, 1)
                dve.wait_ge(halves, 2)
                for v in range(2):
                    then(dve.tensor_copy(c_split[:, :, v], silu_c[:, v, :]))
                    m = dve.tensor_tensor(c_split[:, :, LOW + v], silu_c[:, v, :], c_split[:, :, v].bitcast(F32), ALU.subtract)
                m.then_inc(c_split_ready, 1)

            def ada_sum(m, group, it=0):
                dve.wait_ge(ada_low, m + 1 + ADA_FIRST * it)
                if group:
                    dve.wait_ge(ada_biased, group + it)
                at = m % ADA_FIRST * 512
                dve.tensor_tensor(mod_sum[:, at:at + 512], ada_bank(m)[0:2, :], mod_low, ALU.add).then_inc(ada_out, 1)

            def ffn(s, n0):
                c0 = FFNS.index(s) * STEPS

                def act_lower(c, it=0, o=(actT_hi, actT_lo), bank=tp[:, 0, :]):
                    dve.wait_ge(actT_hi_ready, c + 1 + it)
                    lower(o[1][:, 0:2, :], bank.rearrange("p (k c) -> p k c", k=2), o[0][:, 0:2, :], actT_lo_ready)

                def gated(c, t, it=0):
                    dve.wait_ge(silu_ready, TT * c + t + 1 + TT * it)
                    dve.tensor_tensor(act_tok[:, t, :], silu[:, t, :], gu[:, t, FS:512], ALU.mult).then_inc(act_ready, 1)

                def gates(c, it=0):
                    gated(c, 0, it)
                    gated(c, 1, it)

                def step(j, it=0):
                    n = n0 + 4 + 6 * (j - 1)
                    act_lower(c0 + j - 1, it)
                    after_slots(n, 3, it)
                    gates(c0 + j, it)
                    if j == STEPS - 1 and s + 1 in READY:
                        in_lower(s + 1, [0])
                        after_slots(n + 3, 3)
                        act_lower(c0 + STEPS - 1, bank=gu[:, 0, :])
                        in_lower(s + 1, [1])
                    elif j == STEPS - 1:
                        after_slots(n + 3, 2)
                        act_lower(c0 + STEPS - 1, o=last_act(s))
                        after_slots(n + 5, 1)
                    else:
                        after_slots(n + 3, 3, it)

                def steps_with_ada(n, j, m, it=0):
                    r, i2, group = 4 * it, 2 * it, m // ADA_FIRST
                    act_lower(c0 + j - 1, i2)
                    after_slots(n, 3, r)
                    gates(c0 + j, i2)
                    after_slots(n + 3, 4, r)
                    ada_sum(m, group, it)
                    after_slots(n + 7, 3, r)
                    act_lower(c0 + j, i2)
                    after_slots(n + 10, 3, r)
                    gates(c0 + j + 1, i2)
                    after_slots(n + 13, 4, r)
                    ada_sum(m + 1, group, it)
                    after_slots(n + 17, 6, r)
                    ada_sum(m + 2, group, it)
                    after_slots(n + 23, 1, r)

                if s in READY:
                    after_slots(n0, 2)
                    gates(c0)
                    after_slots(n0 + 2, 2)
                else:
                    gated(c0, 0)
                    after_slots(n0, 3)
                    gated(c0, 1)
                    after_slots(n0 + 3, 1)
                if s == TAIL:
                    dve.wait_ge(p_exp, 1)
                    then(dve.tensor_tensor(exp_p[:, :, :], exp_p[:, :, :], dt[:, :, :], ALU.mult))
                    dve.wait_ge(tok_ready, TT)
                    x_times(exp_p)
                if s == 0:
                    split_c()
                    for m in range(ADA_FIRST):
                        after_slots(n0 + 4 + 4 * m, 4)
                        ada_sum(m, 0)
                    steps_with_ada(n0 + 16, 1, ADA_FIRST)
                    with dve.Fori(0, STEPS // 2 - 1) as it:
                        steps_with_ada(n0 + 40, 3, 2 * ADA_FIRST, it)
                    act_lower(c0 + STEPS - 1)
                else:
                    step(1)
                    with dve.Fori(0, STEPS - 3) as it:
                        step(2, it)
                    if s + 1 in READY:
                        normalised(s + 1)
                    step(STEPS - 1)

            def ab(s, n0):
                dve.wait_ge(late_consts, ALL_LATE)
                dve.wait_ge(ada_stored, 16 * (ADA_CH // ADA_FIRST))
                then(dve.memset(lx[:, :, 0:LRU_CONV - 1], 0.0))
                lam = lru_cols[:, :, 7]
                then(dve.tensor_scalar(lru_tmp[:, 0, :], lam, -1.0, None, ALU.mult))
                dve.tensor_tensor(lru_tmp[:, 1, :], lam, lru_tmp[:, 0, :], ALU.min).then_inc(lam_z, 1)
                dve.wait_ge(lam_exp, 1)
                log1p([lru_tmp[:, q, :] for q in (1, 2, 3, 4)])
                then(dve.tensor_scalar(lru_tmp[:, 5, :], lru_tmp[:, 0, :], 0.0, None, ALU.max))
                then(dve.scalar_tensor_tensor(lru_tmp[:, 5, :], lru_tmp[:, 4, :], 2.0, lru_tmp[:, 5, :], ALU.mult, ALU.add))
                dve.tensor_scalar(lru_tmp[:, 6, :], lru_tmp[:, 5, :], LRU_C, None, ALU.mult)
                dve.tensor_scalar(lru_tmp[:, 7, :], lru_tmp[:, 5, :], -LRU_C, None, ALU.mult).then_inc(lru_c_ready, 1)
                after_slots(n0, 4)
                dve.wait_ge(ab_evac, 2)
                for j in range(LRU_CONV):
                    for i in range(LT):
                        src, w = lx[:, i, j:j + TOK], lru_cols[:, i, j:j + 1]
                        if j == 0:
                            m = dve.tensor_scalar(xc[:, i, :], src, w, lru_cols[:, i, 4:5], ALU.mult, ALU.add)
                        else:
                            m = dve.scalar_tensor_tensor(xc[:, i, :], src, w, xc[:, i, :], ALU.mult, ALU.add)
                    if j < LRU_CONV - 1:
                        then(m)
                    else:
                        m.then_inc(xc_ready, 1)
                after_slots(n0 + 4, 9)
                dve.wait_ge(lru_decay, LT)
                then(dve.tensor_tensor(rgate[:, :, :], decay[:, :, :], decay[:, :, :], ALU.mult))
                dve.scalar_tensor_tensor(th[:, :, :], rgate[:, :, :], 1.0, th[:, :, :], ALU.add, ALU.mult).then_inc(lru_ratio, 1)
                after_slots(n0 + 13, 3)
                then(dve.tensor_tensor(igate[:, :, :], igate[:, :, :], xc[:, :, :], ALU.mult))
                dve.wait_ge(ab_evac, 8)
                half = [qk[:, :, :, q * HALF_ROT:(q + 1) * HALF_ROT] for q in range(2)]
                turn = [rope[:, :, q, :].unsqueeze(2).broadcast_to([P, TT, 2 * HEADS, HALF_ROT]) for q in range(2)]
                tmp = [v.rearrange("p (n t h d) -> p n t h d", n=2, t=TT, h=2 * HEADS) for v in (rope_t, rope_u)]
                for q in range(2):
                    for c in range(2):
                        m = dve.tensor_tensor(tmp[q][:, c], half[q], turn[c], ALU.mult)
                then(m)
                dve.tensor_tensor(half[0], tmp[0][:, 0], tmp[1][:, 1], ALU.subtract)
                dve.tensor_tensor(half[1], tmp[1][:, 0], tmp[0][:, 1], ALU.add).then_inc(roped, 1)
                after_slots(n0 + 16, 4)
                dve.wait_ge(lru_root, 1)
                then(dve.tensor_tensor(igate[:, :, :], igate[:, :, :], th[:, :, :], ALU.mult))
                for i in range(LT):
                    m = dve.tensor_tensor_scan(rgate[:, i, :], decay[:, i, :], igate[:, i, :], 0.0, ALU.mult, ALU.add)
                then(m)
                dve.tensor_tensor(gelu[:, :, :], gelu[:, :, :], rgate[:, :, :], ALU.mult).then_inc(rec_ready, 1)
                for h in range(HEADS):
                    bank = (gu, tp)[(h // 2) % 2][:, h % 2, :]
                    dve.wait_ge(scores_done, h + 1)
                    if h >= 2:
                        dve.wait_ge(exp_ready, h - 1)
                    for t, c in enumerate((slice(0, P), slice(P, 3 * P))):
                        dve.tensor_tensor_reduce(masked[:, h % 2, c], bank[:, c], causal[:, c], 1.0, -3.0e38,
                                                 ALU.add, ALU.max, soft[:, 0, h, t:t + 1]).then_inc(masked_ready, 1)
                    dve.wait_ge(masked_ready, 3 * h + 2)
                    dve.tensor_scalar(soft[:, 1, h, :], soft[:, 0, h, :], -1.0, None, ALU.mult).then_inc(masked_ready, 1)
                dve.wait_ge(mix_hi, 1)
                lower(hT_lo[:, 4:8, :], gelu[:, :, :], hT_hi[:, 4:8, :], mix_lo)
                dve.wait_ge(exp_ready, HEADS)
                then(dve.reciprocal(soft[:, 3, :, :], soft[:, 2, :, :]))
                dve.wait_ge(attn_psum, 1)
                for t in range(TT):
                    m = dve.tensor_tensor(attn[:, t, :].rearrange("p (h d) -> p h d", h=HEADS),
                                          dn[:, 1, t * 512:(t + 1) * 512].rearrange("p (h d) -> p h d", h=HEADS),
                                          soft[:, 3, :, t].unsqueeze(2).broadcast_to([P, HEADS, HD]), ALU.mult)
                m.then_inc(attn_ready, 1)
                for t in range(TT):
                    c = (slice(None), slice(0, 4), slice(t * P, (t + 1) * P))
                    dve.wait_ge(mix_hi, 2 + t)
                    lower(hT_lo[c], tp[:, t, :].rearrange("p (k c) -> p k c", k=4), hT_hi[c], mix_lo)
                after_slots(n0 + 20, 7)

            def sc(s, n0):
                then(dve.memset(cx[:, :, 0:SC_CONV - 1], 0.0))
                for i in range(KT):
                    dve.wait_ge(sc_gate, i + 1)
                    dve.wait_ge(slot_used, n0 + 3 * i + 2)
                    dve.tensor_tensor(cx[:, i, SC_CONV - 1:], cgate[:, i % 2, 0:TOK], any_bank((3 * i + 1) % 8)[:, 0:TOK],
                                      ALU.mult).then_inc(sc_mixed, 1)
                    dve.wait_ge(sc_mixed, 2 * i + 1)
                    for j in range(SC_CONV):
                        src, w = cx[:, i, j:j + TOK], sc_cols[:, i, j:j + 1]
                        if j == 0:
                            then(dve.tensor_scalar(conv_y[:, i, :], src, w, None, ALU.mult))
                        else:
                            then(dve.scalar_tensor_tensor(conv_y[:, i, :], src, w, conv_y[:, i, :], ALU.mult, ALU.add))
                    dve.wait_ge(slot_used, n0 + 3 * i + 3)
                    dve.tensor_tensor(conv_y[:, i, :], conv_y[:, i, :], any_bank((3 * i + 2) % 8)[:, 0:TOK],
                                      ALU.mult).then_inc(sc_mixed, 1)
                    if i < KT - 1:
                        after_slots(n0 + 3 * i, 3)
                    if i == 4 and s + 1 in EARLY:
                        normalised(s + 1)
                for half in range(2):
                    c = (slice(None), slice(4 * half, 4 * half + 4))
                    dve.wait_ge(mix_hi, MIX0["sc"] + half + 1)
                    lower(hT_lo[c], conv_y[c], hT_hi[c], mix_lo)
                after_slots(n0 + 3 * KT - 3, 3 + KT - 1)

            def dt_and_conv(turn, n0, pairs, pair0, tile0, after):
                for edge in (0, TOK + 1):
                    m = dve.memset(xbc_in[:, :, edge:edge + 1], 0.0)
                then(m)
                if turn == 0:
                    dve.wait_ge(a_exp, 1)
                    then(dve.tensor_scalar(neg_a[:], neg_a[:], -1.0, None, ALU.mult))
                after_slots(n0, 1)
                z, u, s1, s2, acc, mz = (dt_tmp[:, q, :] for q in range(6))

                def both(v):
                    return v.rearrange("p (t h) -> p t h", t=TT)

                dve.wait_ge(slot_used, n0 + 1)
                then(dve.tensor_tensor(both(z), both(tp[:, 0, 0:TT * NDT]),
                                       ssd_rows[:, 0:NDT].unsqueeze(1).broadcast_to([P, TT, NDT]), ALU.add))
                then(dve.tensor_scalar(u, z, -1.0, None, ALU.mult))
                dve.tensor_tensor(u, z, u, ALU.min).then_inc(dt_z, 1)
                then(dve.tensor_scalar(mz, z, 0.0, None, ALU.max))
                dve.wait_ge(dt_exp, turn + 1)
                log1p([u, s1, s2, acc])
                then(dve.scalar_tensor_tensor(both(dt[:, :, :].rearrange("p t h -> p (t h)")), both(acc), 2.0, both(mz), ALU.mult, ALU.add))
                dve.tensor_tensor(dta[:, :, :], dt[:, :, :], neg_a[:].unsqueeze(1).broadcast_to([P, TT, NDT]),
                                  ALU.mult).then_inc(dta_ready, 1)
                for p in range(pairs):
                    after_slots(n0 + 1 + 2 * p, 2)
                    if turn == 0 and p == pairs - 1:
                        in_lower(TAIL, [0])
                    dve.wait_ge(xbc_evac, pair0 + p + 1)
                    for j in range(3):
                        for q in range(2):
                            i = tile0 + 2 * p + q
                            src, w = xbc_in[:, i, j:j + TOK], ssd_cols[:, i, j:j + 1]
                            if j == 0:
                                m = dve.tensor_scalar(xbc[:, i, :], src, w, None, ALU.mult)
                            else:
                                m = dve.scalar_tensor_tensor(xbc[:, i, :], src, w, xbc[:, i, :], ALU.mult, ALU.add)
                        if j < 2:
                            then(m)
                        else:
                            m.then_inc(conv_done, 1)
                    if p == 3:
                        after()

            def heads_of(v):
                return v.rearrange("p (h d) -> p h d", d=SSD_P)

            def x_times(w):
                for d in range(2):
                    for t in range(TT):
                        m = dve.tensor_tensor(heads_of(x_dt[d][:, t, :]), heads_of(xs_tok[:, t, :]),
                                              w[:, t, d * SSD_H:(d + 1) * SSD_H].unsqueeze(2).broadcast_to([P, SSD_H, SSD_P]), ALU.mult)
                    m.then_inc(xdt_ready, 1)

            def ctx_mix(s, n0):
                def decay_arguments():
                    dve.wait_ge(p_ready, 1)
                    dve.tensor_tensor(exp_p[:, :, :], pcol[:, 2, :].unsqueeze(1).broadcast_to([P, TT, NDT]),
                                      pcol[:, 0:2, :], ALU.subtract).then_inc(p_arg, 1)
                    normalised(TAIL)

                dt_and_conv(0, n0, 5, 0, XS_T, decay_arguments)
                in_lower(TAIL, [1])

            def ssd(s, n0):
                dt_and_conv(1, n0, 7, 5, 0, lambda: None)
                after_slots(n0 + 15, 8)
                dve.wait_ge(tok_ready, 6)
                for t in range(TT):
                    m = dve.tensor_tensor(heads_of(y_acc[:, t, :]), heads_of(xs_tok[:, t, :]),
                                          ssd_rows[:, 2 * NDT:].unsqueeze(2).broadcast_to([P, SSD_H, SSD_P]), ALU.mult)
                then(m)
                x_times(dt)
                dve.wait_ge(row_split_hi, 2)
                lower(row_lo, prow[:, :, :], row_hi, row_split)
                dve.wait_ge(mix_hi, MIX0["ssd"] + 1)
                lower(hT_lo[:, 0:2, :], tp[:, 1, :].rearrange("p (f c) -> p f c", f=2), hT_hi[:, 0:2, :], mix_lo)
                dve.wait_ge(p_exp, 2)
                for g in range(SSD_G):
                    dve.wait_ge(yoff_psum, g + 1)
                    for t in range(TT):
                        w = exp_p[:, t, :].rearrange("p (d h) -> p d h", d=2)[:, :, g * HPG:(g + 1) * HPG]
                        for d in range(2):
                            m = dve.tensor_tensor(heads_of(y_off[:, t, d * GW:(d + 1) * GW]), heads_of(tp[:, t, d * GW:(d + 1) * GW]),
                                                  w[:, d, :].unsqueeze(2).broadcast_to([P, HPG, SSD_P]), ALU.mult)
                        m.then_inc(yoff_used, 1)
                    dve.wait_ge(yoff_used, TT * (g + 1))
                    for d in range(2):
                        for t in range(TT):
                            acc = y_acc[:, t, g * GW:(g + 1) * GW]
                            m = dve.tensor_tensor(acc, acc, y_off[:, t, d * GW:(d + 1) * GW], ALU.add)
                        then(m)

                def masked_cb(g):
                    dve.wait_ge(cb_psum, g + 1)
                    if g:
                        dve.wait_ge(g_ready, HPG * g)
                    cb = tp[:, g % 2, :]
                    dve.tensor_tensor(cb_m[:, 0:256], cb[:, 0:256], tri[:, 0, 0, :], ALU.mult)
                    dve.tensor_tensor(cb_m[:, 256:384], cb[:, 384:512], tri[:, 0, 1, P:], ALU.mult)
                    dve.tensor_tensor(cb_m[:, 384:512], cb[:, 0:128], tri[:, 1, 0, 0:P], ALU.mult)
                    dve.tensor_tensor(cb_m[:, 512:768], cb[:, 256:512], tri[:, 1, 1, :], ALU.mult).then_inc(cb_ready, 1)

                def arguments(h):
                    dve.wait_ge(rows_psum, h + 1)
                    if h >= 3:
                        dve.wait_ge(y_psum, h - 2)
                    w, b = decays[h % 3], gu[:, h % 2, :]
                    for at, c, d, st in ((0, slice(0, 256), 0, 0), (256, slice(128, 256), 0, 1),
                                         (384, slice(256, 384), 1, 0), (512, slice(256, 512), 1, 1)):
                        m = dve.tensor_scalar(w[:, at:at + c.stop - c.start], b[:, c], pcol[:, st, d * SSD_H + h:d * SSD_H + h + 1],
                                              0.0, ALU.subtract, ALU.min)
                    m.then_inc(arg_ready, 1)

                arguments(0)
                for h in range(SSD_H):
                    if h + 1 < SSD_H:
                        arguments(h + 1)
                    if h % HPG == 0:
                        masked_cb(h // HPG)
                    dve.wait_ge(cb_ready, h // HPG + 1)
                    dve.wait_ge(dec_ready, h + 1)
                    dve.tensor_tensor(decays[h % 3], decays[h % 3], cb_m, ALU.mult).then_inc(g_ready, 1)
                dve.wait_ge(y_psum, SSD_H)
                dve.wait_ge(wide_ready, 4)
                for t in range(TT):
                    m = dve.tensor_tensor(y_sum[:, t, :], dn[:, t, 0:SSD_W], y_acc[:, t, :], ALU.add)
                m.then_inc(y_taken, 1)
                dve.wait_ge(y_taken, 1)
                for t in range(TT):
                    dve.tensor_tensor(y_sum[:, t, :], y_sum[:, t, :], z_tok[:, t, :], ALU.mult).then_inc(y_gated, 1)
                for t in range(TT):
                    dve.wait_ge(gr_ready, t + 1)
                    for g in range(SSD_G):
                        c, r = slice(g * GW, (g + 1) * GW), t * SSD_G + g
                        m = dve.scalar_tensor_tensor(y_sum[:, t, c], y_sum[:, t, c], gstat[:, 2, r:r + 1], ssd_norm[:, c],
                                                     ALU.mult, ALU.mult)
                    m.then_inc(y_ready, 1)
                after_slots(n0 + 23, 2)
                for t in range(TT):
                    c = slice(t * P, (t + 1) * P)
                    dve.wait_ge(mix_hi, MIX0["ssd"] + 2 + 2 * t)
                    lower(hT_lo[:, 2:6, c], tp[:, t, :].rearrange("p (k c) -> p k c", k=4), hT_hi[:, 2:6, c], mix_lo)
                    dve.wait_ge(mix_hi, MIX0["ssd"] + 3 + 2 * t)
                    lower(hT_lo[:, 6:8, c], gu[:, t, 0:TOK].rearrange("p (k c) -> p k c", k=2), hT_hi[:, 6:8, c], mix_lo)
                after_slots(n0 + 25, 5)

            dve.memset(neg_half[:], -0.5).then_inc(halves, 1)
            dve.memset(c_split[:].bitcast(F32), 0.0).then_inc(halves, 1)
            rest(0)
            rest(1)
            normalised(0)
            for n in range(2, RING):
                rest(n)
            for s, name in enumerate(SUB):
                if s not in READY and s != TAIL:
                    in_lower(s)
                if s in EARLY and s - 1 in WITH_POST:
                    for t in range(TT):
                        residual(s - 1, [t])
                        if t < LEFT[s - 1]:
                            rest(LAST[s - 1] - LEFT[s - 1] + t + RING)
                elif s:
                    after_slots(LAST[s - 1] - LEFT[s - 1], LEFT[s - 1])
                {"ctx_mix": ctx_mix, "ab": ab, "sc": sc, "ssd": ssd}.get(name, ffn)(s, BASE[name])
                if s in WITH_POST and s + 1 not in EARLY:
                    residual(s)
                    if s + 1 < len(SUB):
                        normalised(s + 1)

        @block.gpsimd
        def _(pool):
            steps = [0]

            def then(ins):
                steps[0] += 1
                ins.then_inc(pool_step, 1)
                pool.wait_ge(pool_step, steps[0])

            def inverse_root(kind, s, t):
                eps = EPS / 0.25 if kind == "post" and s in FFNS else EPS
                c = slice(t + (2 if kind == "post" else 0), t + (2 if kind == "post" else 0) + 1)
                pool.wait_ge(ssq_ready, NORM_N[kind, s, t])
                then(pool.tensor_scalar(ms[:, c], ssq[:, c], eps, None, ALU.add))
                pool.tensor_tensor(rstd[:, c], ms[:, c], neg_half[:, 0:1], ALU.pow).then_inc(rstd_ready, 1)

            def mod_vector(v, q):
                return mod[v, q * D:(q + 1) * D].partition_broadcast(P)

            def rows_in(s):
                pool.dma_start(pre_row[:], pre_rows[s, :].partition_broadcast(P)).then_inc(row_pre, 16)
                if s in MOD:
                    v, shift, scale, _ = MOD[s]
                    pool.dma_start(shift_row[:], mod_vector(v, shift)).then_inc(row_pre, 16)
                    pool.dma_start(mod_row[:], mod_vector(v, scale)).then_inc(row_pre, 16)
                    pool.wait_ge(row_pre, PRE_DMA_N[s])
                    then(pool.tensor_scalar(mod_row[:], mod_row[:], 1.0, None, ALU.add))
                    pool.tensor_tensor(pre_row[:], pre_row[:], mod_row[:], ALU.mult).then_inc(pre_mod, 1)
                    pool.wait_ge(pre_mod, PRE_MOD_N[s])

            def rows_out(s):
                pool.dma_start(post_row[:], post_rows[s, :].partition_broadcast(P)).then_inc(row_post, 16)
                if s in MOD:
                    v, _, _, gate = MOD[s]
                    pool.dma_start(mod_row[:], mod_vector(v, gate)).then_inc(row_post, 16)
                    pool.wait_ge(row_post, POST_DMA_N[s])
                    pool.tensor_tensor(post_row[:], post_row[:], mod_row[:], ALU.mult).then_inc(post_mod, 1)
                    pool.wait_ge(post_mod, POST_MOD_N[s])

            def pre_roots(s):
                for t in range(TT):
                    inverse_root("pre", s, t)

            pool.wait_ge(halves, 1)
            rows_in(0)
            pre_roots(0)
            for s, name in enumerate(SUB):
                if s in EARLY and s - 1 in WITH_POST:
                    pool.wait_ge(x_new, X_NEW_N[s - 1])
                if s in WITH_POST:
                    rows_out(s)
                pool.wait_ge(xn_ready, TT * (s + 1))
                if s == 0:
                    for tile_name, tile in late_tiles.items():
                        source = small[tile_name]
                        if tile_name == "ada_b":
                            source = source[0, :].partition_broadcast(2)
                        pool.dma_start(tile if tile_name in ("ada_b", "gate_bd", "causal") else tile[:], source).then_inc(late_consts, 16)
                    pool.dma_start(ssd_rows[:], small["ssd_rows"][0, :].partition_broadcast(P)).then_inc(late_consts, 16)
                    pool.dma_start(ssd_norm[:], small["ssd_norm"][0, :].partition_broadcast(P)).then_inc(late_consts, 16)
                    pool.wait_ge(late_consts, ALL_LATE)
                    for g in range(ADA_CH // ADA_FIRST):
                        pool.wait_ge(ada_out, ADA_FIRST * (g + 1))
                        if g:
                            pool.wait_ge(ada_stored, 16 * g)
                        cols = slice(g * ADA_FIRST * 512, (g + 1) * ADA_FIRST * 512)
                        pool.tensor_tensor(mod_out, mod_sum, mod_bias[:, cols], ALU.add).then_inc(ada_biased, 1)
                        pool.wait_ge(ada_biased, g + 1)
                        pool.dma_start(mod[:, cols], mod_out).then_inc(ada_stored, 16)
                    pool.wait_ge(ada_stored, 16 * (ADA_CH // ADA_FIRST))
                if s == SOURCE[CTX[0] - 1] + 1:
                    pool.dma_start(ctx_x, ctx_in.rearrange("(t p) d -> p t d", p=P)).then_inc(ctx_loaded, 16)
                if s + 1 < len(SUB):
                    rows_in(s + 1)
                    if s + 1 in EARLY:
                        pre_roots(s + 1)
                if name == "ssd":
                    for t in range(TT):
                        c = slice(t * SSD_G, (t + 1) * SSD_G)
                        pool.wait_ge(gsq_ready, t + 1)
                        then(pool.tensor_scalar(gstat[:, 1, c], gstat[:, 0, c], EPS, None, ALU.add))
                        pool.tensor_tensor(gstat[:, 2, c], gstat[:, 1, c], neg_half[:, 0:SSD_G], ALU.pow).then_inc(gr_ready, 1)
                if s in WITH_POST:
                    for t in range(TT):
                        inverse_root("post", s, t)
                if s + 1 < len(SUB) and s + 1 not in EARLY:
                    pre_roots(s + 1)
            for t in range(TT):
                pool.wait_ge(x_new, TT * (len(WITH_POST) - 1) + t + 1)
                pool.dma_start(out[t * P:(t + 1) * P, :], x[:, t, :]).then_inc(stored, 16)
            pool.wait_ge(stored, 16 * TT)


def wide(w):
    return w.reshape(KT // 2, 2, P, 512).transpose(0, 2, 1, 3).reshape(KT // 2 * P, SLOT)


def columns(w):
    return w.reshape(KT, P, -1, P).transpose(2, 1, 0, 3).reshape(-1, SLOT)


def narrow(w):
    slot = np.zeros((P, SLOT), np.float32)
    slot[:, :KT * NDT] = w.reshape(KT, P, NDT).transpose(1, 0, 2).reshape(P, KT * NDT)
    return slot


def swiglu_slots(w_gate, w_up, w_down):
    slots = []
    for j in range(STEPS):
        c = slice(j * FS, (j + 1) * FS)
        slots.append(wide(np.concatenate([w_gate[:, c], w_up[:, c]], axis=1)))
        if j:
            slots.append(w_down[(j - 1) * FS:j * FS])
    slots.append(w_down[(STEPS - 1) * FS:])
    return slots


def mixed_columns(w, which):
    return np.concatenate([columns(w[:, c:c + P]) for c in which])


def kernel(x, ffn1_w_gate, ffn1_w_up, ffn1_w_down, ffn2_w_gate, ffn2_w_up, ffn2_w_down, norm_pre,
           norm_post, ab_w_in, ab_w_out, lru_conv_w, lru_conv_b, lru_gate_a_w, lru_gate_a_b,
           lru_gate_x_w, lru_gate_x_b, lru_lambda, c_w_in, c_conv_w, c_w_out, c_2, ctx_2, c_ctx_2,
           ada_w_2, ada_b_2, ffn1_norm_pre_2, ffn1_norm_post_2, ffn1_w_gate_2, ffn1_w_up_2,
           ffn1_w_down_2, mix_norm_pre_2, mix_norm_post_2, w_in_2, fourier_w_2, conv_w_2, conv_b_2,
           dt_bias_2, a_log_2, d_skip_2, ssd_norm_2, w_out_2, ffn2_norm_pre_2, ffn2_norm_post_2,
           ffn2_w_gate_2, ffn2_w_up_2, ffn2_w_down_2):
    first = swiglu_slots(ffn1_w_gate_2[0], ffn1_w_up_2[0], ffn1_w_down_2[0])
    w_in, dt_at = w_in_2[0], 4 * 256 + 512 + SSD_W + 512
    ab, c_in = ab_w_in[0], c_w_in[0]
    ada = [wide(ada_w_2[0][:, 512 * i:512 * (i + 1)]) for i in range(ADA_CH)]
    zero = swiglu_slots(ffn1_w_gate[0], ffn1_w_up[0], ffn1_w_down[0])
    among = [zero[0]] + ada[:ADA_FIRST]
    for i in range(STEPS // 2):
        a, b, c = ada[ADA_FIRST * (i + 1):ADA_FIRST * (i + 2)]
        up_a, down_a, up_b, down_b = zero[4 * i + 1:4 * i + 5]
        among += [up_a, a, down_a, up_b, b, down_b, c]
    among.append(zero[-1])
    phases = {
        "ffn_0": among,
        "ab": [columns(ab[:, 1536:2560])] + [wide(ab[:, 512 * i:512 * (i + 1)]) for i in range(3)]
        + [ab_w_out[0][512:], ab_w_out[0][:512]],
        "ffn_1": swiglu_slots(ffn2_w_gate[0], ffn2_w_up[0], ffn2_w_down[0]),
        "ctx_ffn": first,
        "ffn_2": swiglu_slots(ffn1_w_gate[1], ffn1_w_up[1], ffn1_w_down[1]),
        "sc": [mixed_columns(c_in, [k * D + i * P for i in range(KT) for k in (1, 2, 0)]), c_w_out[0]],
        "ctx_mix": [narrow(w_in[:, dt_at:]), columns(w_in[:, 1024 + 512:dt_at])],
        "ffn_3": swiglu_slots(ffn2_w_gate[1], ffn2_w_up[1], ffn2_w_down[1]),
        "ffn_4": first,
        "ssd": [narrow(w_in[:, dt_at:]), columns(w_in[:, 1024:dt_at]), wide(w_in[:, :512]), wide(w_in[:, 512:1024]),
                w_out_2[0]],
        "ffn_5": swiglu_slots(ffn2_w_gate_2[0], ffn2_w_up_2[0], ffn2_w_down_2[0]),
    }
    stream = np.concatenate([w for name, _ in PHASES for w in phases[name]])
    assert stream.shape == (NSLOT * P, SLOT)
    norms = {"ffn_0": (norm_pre[0, 0], norm_post[0, 0]), "ab": (norm_pre[0, 1], norm_post[0, 1]),
             "ffn_1": (norm_pre[0, 2], norm_post[0, 2]), "ctx_ffn": (ffn1_norm_pre_2[0], ffn1_norm_post_2[0]),
             "ffn_2": (norm_pre[1, 0], norm_post[1, 0]), "sc": (norm_pre[1, 1], norm_post[1, 1]),
             "ctx_mix": (mix_norm_pre_2[0], mix_norm_post_2[0]), "ffn_3": (norm_pre[1, 2], norm_post[1, 2]),
             "ffn_4": (ffn1_norm_pre_2[0], ffn1_norm_post_2[0]), "ssd": (mix_norm_pre_2[0], mix_norm_post_2[0]),
             "ffn_5": (ffn2_norm_pre_2[0], ffn2_norm_post_2[0])}
    pre, post = (np.stack([norms[name][q] for name in SUB]) for q in range(2))

    def pairs(w):
        bd = np.zeros((P, len(w) // 2, P), np.float32)
        for h in range(len(w)):
            at = slice(HD * (h % 2), HD * (h % 2) + HD)
            bd[at, h // 2, at] = w[h]
        return bd

    def tiles(v):
        return np.moveaxis(v.reshape(*v.shape[:-1], -1, P), (-1, -2), (0, 1))

    lru_cols = np.concatenate([tiles(lru_conv_w[0])] + [tiles(v.reshape(1, LRU_W)) for v in
                              (lru_conv_b[0], lru_gate_a_b[0], lru_gate_x_b[0], lru_lambda[0])], axis=2)
    i = np.arange(P)
    pos = np.arange(TOK)
    angle = pos[:, None] * 500000.0 ** (-np.arange(0, 2 * HALF_ROT, 2) / (2 * HALF_ROT))[None, :]
    diag = np.where(i[None, :] <= i[:, None], 0.0, -1e30)
    turn_l = 2 * np.pi * (np.outer(pos, pos) % TOK) / TOK
    turn_d = 2 * np.pi * (np.outer(np.arange(HD), np.arange(HD)) % HD) / HD
    by_tile = lambda m: m.reshape(TT, P, TOK).transpose(1, 0, 2)
    small_arrays = {
        "ident": np.eye(P),
        "lru_cols": lru_cols,
        "gate_bd": np.stack([pairs(lru_gate_a_w[0]), pairs(lru_gate_x_w[0])], axis=1),
        "rope": np.stack([np.cos(angle), np.sin(angle)], axis=1).reshape(TT, P, 2, HALF_ROT).transpose(1, 0, 2, 3),
        "causal": np.concatenate([diag, np.zeros((P, P)), diag], axis=1),
        "sc_cols": tiles(c_conv_w[0]),
        "ssd_cols": np.concatenate([tiles(conv_w_2[0]), tiles(conv_b_2)], axis=2),
        "tri": np.stack([by_tile(pos[:, None] <= pos[None, :]), by_tile(pos[:, None] >= pos[None, :])], axis=1),
        "dft_l": np.stack([by_tile(np.cos(turn_l) / 16), by_tile(np.sin(turn_l) / 16)], axis=1),
        "dft_d": np.stack([np.kron(np.eye(2), np.cos(turn_d) / 8), np.kron(np.eye(2), -np.sin(turn_d) / 8)], axis=1),
        "fourier_bd": pairs(fourier_w_2[0]),
        "c_cols": np.concatenate([tiles(c_2), tiles(c_ctx_2[None, :])], axis=2).transpose(0, 2, 1),
        "ssd_rows": np.concatenate([dt_bias_2.reshape(1, NDT), a_log_2.reshape(1, NDT), d_skip_2.reshape(1, SSD_H)], axis=1),
        "ssd_norm": ssd_norm_2,
        "ada_b": ada_b_2,
    }

    import concourse.bacc as bacc
    from concourse.bass_utils import run_bass_kernel_spmd

    nc = bacc.Bacc("TRN2", target_bir_lowering=False, num_devices=1)
    arrays = {"weights": stream, "x_in": x[0], "ctx_in": ctx_2[0], "pre_rows": pre, "post_rows": post}
    arrays.update(small_arrays)
    arrays = {name: np.ascontiguousarray(v, dtype=np.float32) for name, v in arrays.items()}
    aps = {name: nc.dram_tensor("in_" + name, v.shape, F32, kind="ExternalInput").ap() for name, v in arrays.items()}
    mod = nc.dram_tensor("mod", [2, N_MOD * D], F32, kind="Internal").ap()
    out = nc.dram_tensor("out", [TOK, D], F32, kind="ExternalOutput").ap()
    build(nc, aps["weights"], aps["x_in"], aps["ctx_in"], aps["pre_rows"], aps["post_rows"],
          {name: aps[name] for name in small_arrays}, mod, out)
    nc.compile()
    results = run_bass_kernel_spmd(nc, [{"in_" + name: v for name, v in arrays.items()}], core_ids=[0])
    return results.results[0]["out"].reshape(1, TOK, D)
```

```python
from contextlib import ExitStack

import numpy as np

import concourse.bass as bass
from concourse import mybir

F32 = mybir.dt.float32
F32R = mybir.dt.float32r
ACT = mybir.ActivationFunctionType
ALU = mybir.AluOpType
AX = mybir.AxisListType

P = 128
D = 1024
KT = D // P
TOK = 256
TT = TOK // P
WARM = 18
LOW = 32
FF = 2816
FS = 256
STEPS = FF // FS
HEADS, HD = 8, 64
HALF_ROT = HD // 8
LRU_W = 512
LT = LRU_W // P
LRU_CONV = 4
LRU_C = 8.0
SC_CONV = 3
SSD_H, SSD_P = 12, 64
SSD_W = SSD_H * SSD_P
SSD_G = 4
GW = SSD_W // SSD_G
HPG = SSD_H // SSD_G
FOURIER = 256
XBC_T = (512 + SSD_W + 512) // P
CM_T, XS_T, BM_T = 0, 4, 10
NDT = 2 * SSD_H
N_MOD = 9
EPS = 1e-6
SLOT = 1024
RING = 6
SLOTS_FFN = 6 * STEPS
ADA_CH = N_MOD * D // 512

ADA_FIRST = 3
PHASES = [("ffn_0", SLOTS_FFN + 4 * ADA_CH), ("ab", 28), ("ffn_1", SLOTS_FFN),
          ("ctx_ffn", SLOTS_FFN), ("ffn_2", SLOTS_FFN), ("sc", 32), ("ctx_mix", 11), ("ffn_3", SLOTS_FFN),
          ("ffn_4", SLOTS_FFN), ("ssd", 31), ("ffn_5", SLOTS_FFN)]
BASE, NSLOT = {}, 0
for _name, _n in PHASES:
    BASE[_name] = NSLOT
    NSLOT += _n
SUB = [name for name, _ in PHASES]
FFNS = [s for s, name in enumerate(SUB) if "ffn" in name]
CTX = [SUB.index("ctx_ffn"), SUB.index("ctx_mix")]
TAIL = CTX[1] + 1
WITH_POST = [s for s, name in enumerate(SUB) if name != "ctx_mix"]
MOD = {CTX[0]: (1, 0, 1, 2), CTX[1]: (1, 3, 4, None), SUB.index("ffn_4"): (0, 0, 1, 2), SUB.index("ssd"): (0, 3, 4, 5),
       SUB.index("ffn_5"): (0, 6, 7, 8)}
SOURCE = {s: max([q for q in range(s) if (q in CTX) == (s in CTX)], default=None) for s in range(len(SUB))}
EARLY = [s for s in range(1, len(SUB)) if SOURCE[s] != s - 1]
READY = [s for s in EARLY if s in FFNS and s - 1 in FFNS]
LEFT = {s: 2 if s in WITH_POST else 0 for s in range(len(SUB))}
NORMS = [("pre", 0, t) for t in range(TT)]
for _s in range(len(SUB)):
    _posts = [("post", _s, t) for t in range(TT)] if _s in WITH_POST else []
    _pres = [("pre", _s + 1, t) for t in range(TT)] if _s + 1 < len(SUB) else []
    NORMS += _pres + _posts if _s + 1 in EARLY else _posts + _pres
NORM_N = {k: i + 1 for i, k in enumerate(NORMS)}
PRE_DMA_N, POST_DMA_N, PRE_MOD_N, POST_MOD_N = {}, {}, {}, {}
for _s in range(len(SUB)):
    PRE_DMA_N[_s] = PRE_DMA_N.get(_s - 1, 0) + 16 * (3 if _s in MOD else 1)
    PRE_MOD_N[_s] = PRE_MOD_N.get(_s - 1, 0) + (_s in MOD)
    POST_DMA_N[_s] = POST_DMA_N.get(_s - 1, 0) + 16 * ((_s in WITH_POST) + (_s in WITH_POST and _s in MOD))
    POST_MOD_N[_s] = POST_MOD_N.get(_s - 1, 0) + (_s in WITH_POST and _s in MOD)
X_NEW_N = {s: 2 * TT * (i + 1) for i, s in enumerate(WITH_POST)}

FIRST_N = {}
for _s in range(len(SUB)):
    for _k in (["gu"] if _s in FFNS and _s not in READY else []) + (["dn"] if _s in WITH_POST else []):
        FIRST_N[_k, _s] = max(FIRST_N.values(), default=0) + (1 if _k == "gu" else 3)
LAST = [BASE[name] + dict(PHASES)[name] for name in SUB]
APART = ("sc", "ctx_mix")
MIX_AB, MIX_SC, MIX_SSD = 3, 2, 5
MIX0 = {"ab": 0, "sc": MIX_AB, "ssd": MIX_AB + MIX_SC}


def build(nc, weights, x_in, ctx_in, pre_rows, post_rows, small, mod, out):
    with ExitStack() as stack:
        def sb(name, shape, dt=F32):
            return stack.enter_context(nc.sbuf_tensor(name, shape, dt))

        def sem(name):
            return stack.enter_context(nc.semaphore(name))

        raw = sb("raw", [P, RING, SLOT])
        w_hi = sb("w_hi", [P, RING, SLOT], F32R)
        w_lo = sb("w_lo", [P, RING, SLOT], F32R)
        hT_hi = sb("hT_hi", [P, KT, TOK], F32R)
        hT_lo = sb("hT_lo", [P, KT, TOK], F32R)
        actT_hi = sb("actT_hi", [P, 2, TOK], F32R)
        actT_lo = sb("actT_lo", [P, 2, TOK], F32R)
        silu = sb("silu", [P, TT, FS])
        act_tok = sb("act_tok", [P, TT, FS])
        x = sb("x", [P, TT, D])
        xn = sb("xn", [P, TT, D])
        pre_row = sb("pre_row", [P, D])
        shift_row = sb("shift_row", [P, D])
        post_row = sb("post_row", [P, D])
        mod_row = sb("mod_row", [P, D])
        ssq = sb("ssq", [P, 4, 2])
        ms = sb("ms", [P, 4])
        rstd = sb("rstd", [P, 4])
        neg_half = sb("neg_half", [P, 8])
        state0 = sb("state0", [P, 2, SSD_G, GW])
        arena = sb("arena", [P, 13580])

        ident = sb("ident", [P, P])
        lru_cols = sb("lru_cols", [P, LT, 8])
        rope = sb("rope", [P, TT, 2, HALF_ROT])
        sc_cols = sb("sc_cols", [P, KT, SC_CONV])
        ssd_cols = sb("ssd_cols", [P, XBC_T, 4])
        ssd_rows = sb("ssd_rows", [P, 2 * NDT + SSD_H])
        ssd_norm = sb("ssd_norm", [P, SSD_W])
        tri = sb("tri", [P, 2, TT, TOK])
        dft_l = sb("dft_l", [P, 2, TT, TOK])
        dft_d = sb("dft_d", [P, 2, P])
        fourier_bd = sb("fourier_bd", [P, 2, P])
        c_cols = sb("c_cols", [P, 2, KT])
        silu_c = sb("silu_c", [P, 2, KT])
        c_split = sb("c_split", [P, KT, 64], F32R)
        dt_tmp = sb("dt_tmp", [P, 6, TT * NDT])
        dt = sb("dt", [P, TT, NDT])
        dta = sb("dta", [P, TT, NDT])
        neg_a = sb("neg_a", [P, NDT])
        pcol = sb("pcol", [P, TT + 1, NDT])
        exp_p = sb("exp_p", [P, TT, NDT])
        prow = sb("prow", [SSD_H, 2, TOK])
        gstat = sb("gstat", [P, 3, TT * SSD_G])

        dn = stack.enter_context(nc.psum_tensor("dn", [P, TT, D], F32))
        gu = stack.enter_context(nc.psum_tensor("gu", [P, TT, 512], F32))
        tp = stack.enter_context(nc.psum_tensor("tp", [P, TT, 512], F32))

        def part(at, *shape):
            n = int(np.prod(shape))
            v = arena[:, at:at + n]
            if len(shape) == 2:
                v = v.rearrange("p (a b) -> p a b", a=shape[0])
            elif len(shape) == 3:
                v = v.rearrange("p (a b c) -> p a b c", a=shape[0], b=shape[1])
            return v

        mod_bias = arena[0:2, 0:N_MOD * D]
        mod_sum = arena[0:2, N_MOD * D:N_MOD * D + 1536]
        mod_out = arena[0:2, N_MOD * D + 1536:N_MOD * D + 3072]
        mod_low = mod_row[0:2, 480:992]

        ctx_x = arena[:, 11532:11532 + TT * D].rearrange("p (t d) -> p t d", t=TT)

        lx = part(0, LT, TOK + LRU_CONV - 1)
        xc = part(1036, LT, TOK)
        gelu = part(2060, LT, TOK)
        rgate = part(3084, LT, TOK)
        igate = part(4108, LT, TOK)
        th = part(5132, LT, TOK)
        decay = part(6156, LT, TOK)
        vtok = part(7180, TT, HEADS * HD)
        masked = part(10252, 2, 3 * P)
        expo = part(11020, 2, 3 * P)
        expT = part(11788, 2, 3 * P)
        attn = part(12556, TT, HEADS * HD)
        qk = xn[:, :, :].rearrange("p t (h d) -> p t h d", h=2 * HEADS)
        rope_t = silu[:, :, :].rearrange("p a b -> p (a b)")
        rope_u = act_tok[:, :, :].rearrange("p a b -> p (a b)")

        causal = mod_row[:, 0:3 * P]
        lru_tmp = mod_row[:, 384:416].rearrange("p (q i) -> p q i", q=8)
        soft = mod_row[:, 416:480].rearrange("p (q h t) -> p q h t", q=4, h=HEADS)
        gate_bd = shift_row[:].rearrange("p (g i c) -> p g i c", g=2, i=LT)

        cgate = part(0, 2, 2 * TOK)
        cx = part(1024, KT, TOK + SC_CONV - 1)
        conv_y = part(1024 + 2064, KT, TOK)

        row_one = hT_hi[0:SSD_H, 5, 0:SSD_H]
        row_hi, row_lo = (v[0:SSD_H, 6:8, :] for v in (hT_hi, hT_lo))
        xbc_in = part(0, XBC_T, TOK + 2)
        xbc = part(3612, XBC_T, TOK)
        y_acc = part(0, TT, SSD_W)
        y_sum = part(1536, TT, SSD_W)
        bm_tok = part(1536, TT, 512)
        f_mid = part(2304, 2, 2, TOK)
        f_T = silu
        decays = [part(at, 3 * TOK) for at in (1536, 3612 + 1024, 3612 + 1792)]
        xs_tok = part(7196, TT, SSD_W)
        x_dt = [part(8732, TT, SSD_W), part(10268, TT, SSD_W)]
        cb_m = part(11804, 3 * TOK)
        y_off = part(12572, 2, 3 * 2 * SSD_P)
        u_tok = xn[:, :, 0:FOURIER]
        z_tok = xn[:, :, FOURIER:D]

        landed = [sem(f"landed_{r}") for r in range(RING)]
        hi_ready, lo_ready, slot_used = sem("hi_ready"), sem("lo_ready"), sem("slot_used")
        consts, late_consts, c_loaded, ctx_loaded, x_loaded, stored = sem("consts"), sem("late_consts"), sem("c_loaded"), sem("ctx_loaded"), sem("x_loaded"), sem("stored")
        row_pre, row_post, pre_mod, post_mod = sem("row_pre"), sem("row_post"), sem("pre_mod"), sem("post_mod")
        halves = sem("halves")
        ssq_ready, rstd_ready, x_new, xn_ready = sem("ssq_ready"), sem("rstd_ready"), sem("x_new"), sem("xn_ready")
        hT_psum, hT_hi_ready, hT_lo_ready = sem("hT_psum"), sem("hT_hi_ready"), sem("hT_lo_ready")
        first_tok = sem("first_tok")
        silu_ready, act_ready = sem("silu_ready"), sem("act_ready")
        actT_psum, actT_hi_ready, actT_lo_ready = sem("actT_psum"), sem("actT_hi_ready"), sem("actT_lo_ready")
        dve_step, pool_step = sem("dve_step"), sem("pool_step")
        c_ready, c_split_ready = sem("c_ready"), sem("c_split_ready")
        ada_low, ada_out, ada_biased, ada_stored = sem("ada_low"), sem("ada_out"), sem("ada_biased"), sem("ada_stored")
        mixT_psum, mix_hi, mix_lo = sem("mixT_psum"), sem("mix_hi"), sem("mix_lo")
        ab_evac, xc_ready, gates_done, gates_ready = sem("ab_evac"), sem("xc_ready"), sem("gates_done"), sem("gates_ready")
        lam_z, lam_exp, lru_c_ready = sem("lam_z"), sem("lam_exp"), sem("lru_c_ready")
        lru_tanh, lru_decay, lru_ratio, lru_root, rec_ready = sem("lru_tanh"), sem("lru_decay"), sem("lru_ratio"), sem("lru_root"), sem("rec_ready")
        roped, qkT_psum, qkT_hi, qkT_lo = sem("roped"), sem("qkT_psum"), sem("qkT_hi"), sem("qkT_lo")
        scores_done, masked_ready, exp_ready = sem("scores_done"), sem("masked_ready"), sem("exp_ready")
        expT_psum, expT_ready, attn_psum, attn_ready = sem("expT_psum"), sem("expT_ready"), sem("attn_psum"), sem("attn_ready")
        sc_gate, sc_mixed = sem("sc_gate"), sem("sc_mixed")
        dt_z, dt_exp, dta_ready, a_exp = sem("dt_z"), sem("dt_exp"), sem("dta_ready"), sem("a_exp")
        p_psum, p_ready, p_arg, p_exp = sem("p_psum"), sem("p_ready"), sem("p_arg"), sem("p_exp")
        pads, xbc_evac, conv_done, xbc_ready = sem("pads"), sem("xbc_evac"), sem("conv_done"), sem("xbc_ready")
        tokT_psum, tok_ready, xdt_ready = sem("tokT_psum"), sem("tok_ready"), sem("xdt_ready")
        state_psum, state_ready, wide_ready = sem("state_psum"), sem("state_ready"), sem("wide_ready")
        four_psum, four_ready = sem("four_psum"), sem("four_ready")
        yoff_psum, yoff_used, cb_psum, cb_ready = sem("yoff_psum"), sem("yoff_used"), sem("cb_psum"), sem("cb_ready")
        rows_psum, arg_ready, dec_ready, g_ready = sem("rows_psum"), sem("arg_ready"), sem("dec_ready"), sem("g_ready")
        row_split_hi, row_split, y_taken, y_gated = sem("row_split_hi"), sem("row_split"), sem("y_taken"), sem("y_gated")
        y_psum, gsq_ready, gr_ready, y_ready = sem("y_psum"), sem("gsq_ready"), sem("gr_ready"), sem("y_ready")

        late_tiles = {"ada_b": mod_bias, "lru_cols": lru_cols, "rope": rope, "causal": causal, "sc_cols": sc_cols, "ssd_cols": ssd_cols,
                      "tri": tri, "dft_l": dft_l, "dft_d": dft_d, "fourier_bd": fourier_bd, "gate_bd": gate_bd}
        ALL_LATE = 16 * (len(late_tiles) + 2)

        def stream_of(s):
            return ctx_x if s in CTX else x

        def dn_bank(b):
            return dn[:, b // 2, (b % 2) * 512:(b % 2) * 512 + 512]

        def any_bank(b):
            return dn_bank(b) if b < 4 else gu[:, b - 4, :] if b < 6 else tp[:, b - 6, :]

        def ada_bank(m):
            return dn_bank(m) if m < ADA_FIRST else tp[:, 1, :]

        def last_act(s):
            return (actT_hi, actT_lo) if s == 0 or s + 1 in READY else (hT_hi, hT_lo)

        def xbc_bank(turn, p):
            return dn_bank(p % 4) if turn else any_bank([4, 5, 0, 1, 2][p])

        def in_bank(s, t, half):
            return gu[:, half, :] if t and SUB[s] in APART else tp[:, half, :]

        def half_of(half):
            return slice(half * D // 2, (half + 1) * D // 2)

        x_cols = dn[:, :, :].rearrange("p t d -> p (t d)")

        block = stack.enter_context(nc.Block())

        @block.sync
        def _(sp):
            def load(n_first, r, it):
                n = n_first + r
                if n >= RING:
                    sp.wait_ge(lo_ready, n - RING + 1 + RING * it)
                sp.dma_start(raw[:, r, :], weights[bass.ts(n + RING * it, P), :]).then_inc(landed[r], 16)

            sp.dma_start(x[:], x_in.rearrange("(t p) d -> p t d", p=P)).then_inc(x_loaded, 16)
            for r in range(RING):
                load(0, r, 0)
            with sp.Fori(0, NSLOT // RING - 1) as it:
                for r in range(RING):
                    load(RING, r, it)
            for t in range(TT):
                sp.wait_ge(x_new, X_NEW_N[len(SUB) - 1] - 2 * TT + 2 * t + 2)
                sp.dma_start(out[t * P:(t + 1) * P, :], x[:, t, :]).then_inc(stored, 16)
            sp.wait_ge(stored, 16 * TT)

        def slot_landed(eng, n, it=0):
            eng.wait_ge(landed[n % RING], 16 * (n // RING + 1) + 16 * it)

        @block.tensor
        def _(pe):
            def transposed(s, t):
                if t and SUB[s] not in APART:
                    pe.wait_ge(hT_lo_ready, 2 * (TT * s + t))
                for half in range(2):
                    pe.wait_ge(xn_ready, 2 * (TT * s + t) + half + 1)
                    for q in range(4):
                        k = 4 * half + q
                        m = pe.transpose(in_bank(s, t, half)[:, q * P:(q + 1) * P], xn[:, t, k * P:(k + 1) * P], ident[:])
                    m.then_inc(hT_psum, 1)

            def hT_there(s, t):
                pe.wait_ge(hT_lo_ready, 2 * (TT * s + t) + 2)

            def half_there(s, t):
                pe.wait_ge(hT_lo_ready, 2 * (TT * s + t) + 1)

            def wide_slot(n, si, tiles, bank, it=0, used=True):
                pe.wait_ge(lo_ready, n + 1 + RING * it)
                r = n % RING
                for kk in range(2):
                    k = 2 * si + kk
                    for t in tiles:
                        for q, (h, w) in enumerate(((hT_hi, w_hi), (hT_lo, w_hi), (hT_hi, w_lo))):
                            m = pe.matmul(bank[:, t, :], h[:, k, t * P:(t + 1) * P],
                                          w[:, r, kk * 512:(kk + 1) * 512],
                                          start=k == 0 and q == 0, stop=k == KT - 1 and q == 2)
                if used:
                    m.then_inc(slot_used, 1)
                return m

            def col_slot(n, o):
                pe.wait_ge(lo_ready, n + 1)
                r = n % RING
                for k in range(KT):
                    for q, (h, w) in enumerate(((hT_hi, w_hi), (hT_lo, w_hi), (hT_hi, w_lo))):
                        m = pe.matmul(o, w[:, r, k * P:(k + 1) * P], h[:, k, :],
                                      start=k == 0 and q == 0, stop=k == KT - 1 and q == 2)
                m.then_inc(slot_used, 1)

            def down_slot(n, a_hi, a_lo, k, tiles, start, stop, it=0, used=True):
                pe.wait_ge(lo_ready, n + 1 + RING * it)
                r = n % RING
                for t in tiles:
                    for half in range(2):
                        c = slice(512 * half, 512 * (half + 1))
                        for q, (a, w) in enumerate(((a_hi, w_hi), (a_lo, w_hi), (a_hi, w_lo))):
                            m = pe.matmul(dn[:, t, c], a[:, k, t * P:(t + 1) * P], w[:, r, c],
                                          start=start and q == 0, stop=stop and q == 2)
                        if stop and (half == 0 or not used):
                            m.then_inc(first_tok, 1)
                if used:
                    m.then_inc(slot_used, 1)

            def out_proj(n, order, parts, first=True):
                for i, k in enumerate(order[:-2]):
                    pe.wait_ge(mix_lo, parts[k])
                    down_slot(n + i, hT_hi, hT_lo, k, range(TT), first and i == 0, False)
                for t in range(TT):
                    for i, k in enumerate(order[-2:]):
                        pe.wait_ge(mix_lo, parts[k])
                        down_slot(n + len(order) - 2 + i, hT_hi, hT_lo, k, [t], False, i == 1, used=t == 1)

            def ada_chunk(n, m, it=0, r=0):
                if m >= ADA_FIRST:
                    pe.wait_ge(ada_out, m + ADA_FIRST * it)
                for si in range(4):
                    pe.wait_ge(lo_ready, n + si + 1 + RING * r)
                    for kk in range(2):
                        k = 2 * si + kk
                        for q, w in enumerate((w_hi, w_lo)):
                            mm = pe.matmul(ada_bank(m)[0:64, :], c_split[:, k, :],
                                           w[:, (n + si) % RING, kk * 512:(kk + 1) * 512],
                                           start=k == 0 and q == 0, stop=k == KT - 1 and q == 1)
                    mm.then_inc(slot_used, 1)

            def keep_warm(count, o=tp[:, 1, :]):
                for _ in range(count):
                    pe.matmul(o, hT_hi[:, 2, 0:P], hT_hi[:, 2:4, :].rearrange("p k c -> p (k c)")[:, 0:o.shape[1]], start=True, stop=True)

            def first_slots(s, n0, between=None):
                transposed(s, 0)
                if between:
                    between()
                half_there(s, 0)
                wide_slot(n0, 0, [0], gu, used=False)
                wide_slot(n0 + 1, 1, [0], gu, used=False)
                hT_there(s, 0)
                transposed(s, 1)
                wide_slot(n0 + 2, 2, [0], gu, used=False)
                m = wide_slot(n0 + 3, 3, [0], gu, used=False)
                if s in FFNS:
                    m.then_inc(first_tok, 1)
                hT_there(s, 1)
                for si in range(4):
                    wide_slot(n0 + si, si, [1], gu)

            def ffn(s, n0):
                c0 = FFNS.index(s) * STEPS
                end = LAST[s] - 2

                def act_transposed(c, it=0, bank=tp[:, 0, :]):
                    pe.wait_ge(act_ready, TT * (c + 1) + TT * it)
                    for t in range(TT):
                        for kk in range(2):
                            m = pe.transpose(bank[:, kk * TOK + t * P:kk * TOK + (t + 1) * P],
                                             act_tok[:, t, kk * P:(kk + 1) * P], ident[:])
                    m.then_inc(actT_psum, 1)

                def gate_up(n, r=0):
                    for si in range(4):
                        wide_slot(n + si, si, range(TT), gu, it=r)

                def down(n, c, first=False, r=0, it=0):
                    pe.wait_ge(actT_lo_ready, c + 1 + it)
                    for kk in range(2):
                        down_slot(n + kk, actT_hi, actT_lo, kk, range(TT), first and kk == 0, False, it=r)

                def step(j, it=0):
                    n = n0 + 4 + 6 * (j - 1)
                    act_transposed(c0 + j - 1, it)
                    gate_up(n, it)
                    if j == 1:
                        if s == TAIL:
                            context_states()
                        if s in EARLY:
                            pe.wait_ge(x_new, X_NEW_N[max(WITH_POST[:WITH_POST.index(s)])])
                    down(n + 4, c0 + j - 1, j == 1, it, it)

                def steps_with_ada(n, j, m, first=False, it=0):
                    r, i2 = 4 * it, 2 * it
                    gate_up(n, r)
                    ada_chunk(n + 4, m, it, r)
                    down(n + 8, c0 + j - 1, first, r, i2)
                    act_transposed(c0 + j, i2)
                    gate_up(n + 10, r)
                    ada_chunk(n + 14, m + 1, it, r)
                    down(n + 18, c0 + j, False, r, i2)
                    act_transposed(c0 + j + 1, i2)
                    ada_chunk(n + 20, m + 2, it, r)

                if s in READY:
                    gate_up(n0)
                else:
                    first_slots(s, n0, context_x_tokens if s == TAIL else None)
                    if s == TAIL:
                        context_b_tokens()
                if s == 0:
                    pe.wait_ge(c_split_ready, 1)
                    for m in range(ADA_FIRST):
                        if m == ADA_FIRST - 1:
                            act_transposed(c0)
                        ada_chunk(n0 + 4 + 4 * m, m)
                    steps_with_ada(n0 + 16, 1, ADA_FIRST, first=True)
                    with pe.Fori(0, STEPS // 2 - 1) as it:
                        steps_with_ada(n0 + 40, 3, 2 * ADA_FIRST, it=it)
                else:
                    step(1)
                    with pe.Fori(0, STEPS - 3) as it:
                        step(2, it)
                    act_transposed(c0 + STEPS - 2)
                    gate_up(end - 6)
                    pe.wait_ge(actT_lo_ready, c0 + STEPS - 1)
                    if s + 1 in READY:
                        transposed(s + 1, 0)
                        down(end - 2, c0 + STEPS - 2)
                        act_transposed(c0 + STEPS - 1, bank=gu[:, 0, :])
                        transposed(s + 1, 1)
                    else:
                        down_slot(end - 2, actT_hi, actT_lo, 0, range(TT), False, False)
                        act_transposed(c0 + STEPS - 1)
                        down_slot(end - 1, actT_hi, actT_lo, 1, range(TT), False, False)
                pe.wait_ge(actT_lo_ready, c0 + STEPS)
                a_hi, a_lo = last_act(s)
                down_slot(end, a_hi, a_lo, 0, [0], False, False, used=False)
                down_slot(end + 1, a_hi, a_lo, 1, [0], False, True, used=False)
                down_slot(end, a_hi, a_lo, 0, [1], False, False)
                down_slot(end + 1, a_hi, a_lo, 1, [1], False, True)
                if s + 1 in READY:
                    hT_there(s + 1, 1)

            def ab(s, n0):
                pe.wait_ge(late_consts, ALL_LATE)
                first_slots(s, n0)
                for i in range(LT):
                    col_slot(n0 + 4 + i, dn[:, 0, i * TOK:(i + 1) * TOK])
                for i in range(LT):
                    col_slot(n0 + 4 + LT + i, dn[:, 1, i * TOK:(i + 1) * TOK])
                pe.wait_ge(xc_ready, 1)
                pe.wait_ge(ab_evac, 6)
                for gate in range(2):
                    for i in range(LT):
                        m = pe.matmul(dn[:, gate, i * TOK:(i + 1) * TOK], gate_bd[:, gate, i, :], xc[:, i, :],
                                      start=True, stop=True)
                    m.then_inc(gates_done, 1)
                for si in range(4):
                    wide_slot(n0 + 12 + si, si, range(TT), tp)
                pe.wait_ge(ab_evac, 2)
                for si in range(4):
                    wide_slot(n0 + 16 + si, si, range(TT), gu)
                pe.wait_ge(roped, 1)
                for which, bank in ((0, tp), (1, gu)):
                    if which:
                        pe.wait_ge(ab_evac, 10)
                    for half in range(2):
                        for pair in range(2):
                            for t in range(TT):
                                h = 8 * which + 2 * (2 * half + pair)
                                m = pe.transpose(bank[:, half, pair * TOK + t * P:pair * TOK + (t + 1) * P],
                                                 qk[:, t, h:h + 2, :].rearrange("p h d -> p (h d)"), ident[:])
                        m.then_inc(qkT_psum, 1)

                def scores(h):
                    bank = (gu, tp)[(h // 2) % 2][:, h % 2, :]
                    rows = slice(HD * (h % 2), HD * (h % 2) + HD)
                    pe.wait_ge(masked_ready, 3 * (h - 4) + 2) if h >= 4 else pe.wait_ge(qkT_lo, 4)
                    for o, queries, keys in ((bank[:, 0:P], slice(0, P), slice(0, P)),
                                             (bank[:, P:3 * P], slice(P, TOK), slice(0, TOK))):
                        for q, (a, b) in enumerate(((hT_hi, hT_hi), (hT_lo, hT_hi), (hT_hi, hT_lo))):
                            m = pe.matmul(o, a[rows, h // 2, queries], b[rows, HEADS // 2 + h // 2, keys],
                                          start=q == 0, stop=q == 2)
                    m.then_inc(scores_done, 1)

                def weighted(h):
                    pe.wait_ge(expT_ready, h + 1)
                    eT, v = expT[:, h % 2, :], slice(h * HD, (h + 1) * HD)
                    pe.matmul(dn[:, 1, v], eT[:, 0:P], vtok[:, 0, v], start=True, stop=True)
                    pe.matmul(dn[:, 1, 512 + h * HD:512 + (h + 1) * HD], eT[:, P:2 * P], vtok[:, 0, v],
                              start=True, stop=False)
                    m = pe.matmul(dn[:, 1, 512 + h * HD:512 + (h + 1) * HD], eT[:, 2 * P:3 * P], vtok[:, 1, v],
                                  start=False, stop=True)
                    if h == HEADS - 1:
                        m.then_inc(attn_psum, 1)

                for h in range(4):
                    scores(h)
                pe.wait_ge(gates_ready, 2 * LT)
                for h in range(HEADS):
                    pe.wait_ge(exp_ready, h + 1)
                    if h >= 2:
                        pe.wait_ge(expT_ready, h - 1)
                    for q in range(3):
                        m = pe.transpose(dn[:, 0, (h % 2) * 512 + q * P:(h % 2) * 512 + (q + 1) * P],
                                         expo[:, h % 2, q * P:(q + 1) * P], ident[:])
                    m.then_inc(expT_psum, 1)
                    if h + 4 < HEADS:
                        scores(h + 4)
                    if h:
                        weighted(h - 1)
                weighted(HEADS - 1)
                pe.wait_ge(attn_ready, 1)
                for t in range(TT):
                    for k in range(4):
                        m = pe.transpose(tp[:, t, k * P:(k + 1) * P], attn[:, t, k * P:(k + 1) * P], ident[:])
                    m.then_inc(mixT_psum, 1)
                out_proj(n0 + 20, [4, 5, 6, 7, 0, 1, 2, 3], [MIX0["ab"] + MIX_AB] * 4 + [MIX0["ab"] + 1] * 4)

            def sc(s, n0):
                for t in range(TT):
                    transposed(s, t)
                hT_there(s, 1)
                for q in range(3 * KT):
                    if q >= 8:
                        i, kind = (q - 8) // 3, (q - 8) % 3
                        if kind == 0:
                            pe.wait_ge(sc_gate, i + 1)
                        else:
                            pe.wait_ge(sc_mixed, 2 * i + kind)
                    col_slot(n0 + q, any_bank(q % 8)[:, 0:TOK])
                out_proj(n0 + 3 * KT, range(KT), [MIX0["sc"] + 1] * 4 + [MIX0["sc"] + 2] * 4)

            def dt_slot(n):
                pe.wait_ge(lo_ready, n + 1)
                r = n % RING
                for t in range(TT):
                    for k in range(KT):
                        for q, (h, w) in enumerate(((hT_hi, w_hi), (hT_lo, w_hi), (hT_hi, w_lo))):
                            m = pe.matmul(tp[:, 0, t * NDT:(t + 1) * NDT], h[:, k, t * P:(t + 1) * P],
                                          w[:, r, k * NDT:(k + 1) * NDT],
                                          start=k == 0 and q == 0, stop=k == KT - 1 and q == 2)
                m.then_inc(slot_used, 1)

            def log_decays(turn):
                pe.wait_ge(dta_ready, turn + 1)
                for t in range(TT):
                    for d in range(2):
                        for st in range(TT):
                            m = pe.matmul(tp[:, 1, t * NDT + d * SSD_H:t * NDT + (d + 1) * SSD_H],
                                          tri[:, d, st, t * P:(t + 1) * P], dta[:, st, d * SSD_H:(d + 1) * SSD_H],
                                          start=st == 0, stop=st == 1)
                if turn == 0:
                    for st in range(TT):
                        m = pe.matmul(tp[:, 1, 2 * NDT:3 * NDT], tri[:, 0, 0, P:TOK], dta[:, st, :],
                                      start=st == 0, stop=st == 1)
                else:
                    for d in range(2):
                        for st in range(TT):
                            m = pe.matmul(gu[0:SSD_H, d, 0:TOK], dta[:, st, d * SSD_H:(d + 1) * SSD_H],
                                          tri[:, d, st, :], start=st == 0, stop=st == 1)
                m.then_inc(p_psum, 1)

            def xbc_slots(n, turn, pairs, pair0):
                for p in range(pairs):
                    if turn and p >= 4:
                        pe.wait_ge(xbc_evac, pair0 + p - 3)
                    if turn == 0 and p == 2:
                        pe.wait_ge(x_new, X_NEW_N[CTX[1] - 1])
                    for q in range(2):
                        col_slot(n + 2 * p + q, xbc_bank(turn, p)[:, q * TOK:(q + 1) * TOK])
                    if p == 1:
                        if turn:
                            pe.wait_ge(wide_ready, 2)
                        log_decays(turn)

            def turned_tile(o, i, t):
                return pe.transpose(o, xbc[:, i, t * P:(t + 1) * P], ident[:])

            def x_tokens():
                for t in range(TT):
                    for i in range(SSD_W // P):
                        m = turned_tile(x_cols[:, t * SSD_W + i * P:t * SSD_W + (i + 1) * P], XS_T + i, t)
                m.then_inc(tokT_psum, 1)

            def ctx_mix(s, n0):
                for t in range(TT):
                    transposed(s, t)
                hT_there(s, 1)
                dt_slot(n0)
                xbc_slots(n0 + 1, 0, 5, 0)

            def context_x_tokens():
                pe.wait_ge(xbc_evac, 5)
                pe.wait_ge(xbc_ready, 3)
                x_tokens()

            def context_b_tokens():
                pe.wait_ge(xbc_ready, 5)
                for t, bank in enumerate((x_cols[:, TT * SSD_W:], tp[:, 1, :])):
                    for i in range(SSD_G):
                        m = turned_tile(bank[:, i * P:(i + 1) * P], BM_T + i, t)
                m.then_inc(tokT_psum, 1)

            def context_states():
                pe.wait_ge(tok_ready, 2 * TT)
                pe.wait_ge(xdt_ready, 2)
                for d in range(2):
                    for g in range(SSD_G):
                        for t in range(TT):
                            m = pe.matmul(dn[:, d, g * 256:g * 256 + GW], bm_tok[:, t, g * P:(g + 1) * P],
                                          x_dt[d][:, t, g * GW:(g + 1) * GW], start=t == 0, stop=t == 1)
                    m.then_inc(state_psum, 1)
                pe.wait_ge(state_ready, 2)

            def ssd(s, n0):
                first_slots(s, n0)
                dt_slot(n0 + 4)
                xbc_slots(n0 + 5, 1, 7, 5)
                pe.wait_ge(p_ready, 2)
                for m_ in range(2):
                    for ft in range(2):
                        for st in range(TT):
                            m = pe.matmul(gu[:, m_, ft * TOK:(ft + 1) * TOK], u_tok[:, st, ft * P:(ft + 1) * P],
                                          dft_l[:, m_, st, :], start=st == 0, stop=st == 1)
                m.then_inc(four_psum, 1)
                for si in range(4):
                    wide_slot(n0 + 19 + si, si, range(TT), tp)
                pe.wait_ge(xbc_evac, 12)
                pe.wait_ge(xbc_ready, 12)
                x_tokens()

                def context_part(g):
                    if g >= 2:
                        pe.wait_ge(yoff_used, TT * (g - 1))
                    for t in range(TT):
                        for d in range(2):
                            m = pe.matmul((tp, gu)[g % 2][:, t, d * GW:(d + 1) * GW], xbc[:, CM_T + g, t * P:(t + 1) * P],
                                          state0[:, d, g, :], start=True, stop=True)
                    m.then_inc(yoff_psum, 1)

                pe.wait_ge(four_ready, 1)
                for ft in range(2):
                    for m_ in range(2):
                        m = pe.matmul(gu[:, 0, ft * TOK:(ft + 1) * TOK], dft_d[:, m_, :], f_mid[:, m_, ft, :],
                                      start=m_ == 0, stop=m_ == 1)
                m.then_inc(four_psum, 1)
                pe.wait_ge(wide_ready, 4)
                context_part(0)
                pe.wait_ge(four_ready, 2)
                for ft in range(2):
                    m = pe.matmul(gu[:, 1, ft * TOK:(ft + 1) * TOK], fourier_bd[:, ft, :], f_T[:, ft, :],
                                  start=True, stop=True)
                m.then_inc(four_psum, 1)
                pe.wait_ge(mix_lo, MIX0["ssd"] + 1)
                for g in range(1, SSD_G):
                    context_part(g)
                pe.wait_ge(yoff_used, TT * SSD_G)
                pe.wait_ge(tok_ready, 6)

                def outputs(h):
                    pe.wait_ge(g_ready, h + 1)
                    w, c = decays[h % 3], slice(h * SSD_P, (h + 1) * SSD_P)
                    sums = [[(0, 0), (512, 1)], [(128, 0), (256, 1)]]
                    for t in range(TT):
                        for q, (at, st) in enumerate(sums[t]):
                            m = pe.matmul(dn[:, t, c], w[:, at:at + P], xs_tok[:, st, c], start=q == 0, stop=q == 1)
                    m.then_inc(y_psum, 1)


                def correlations(g):
                    if g >= 2:
                        pe.wait_ge(cb_ready, g - 1)
                    for st in range(TT):
                        m = pe.matmul(tp[:, g % 2, st * TOK:(st + 1) * TOK], xbc[:, BM_T + g, st * P:(st + 1) * P],
                                      xbc[:, CM_T + g, :], start=True, stop=True)
                    m.then_inc(cb_psum, 1)

                def log_rows(h):
                    if h >= 2:
                        pe.wait_ge(arg_ready, h - 1)
                    for q, row in enumerate((row_hi, row_lo)):
                        m = pe.matmul(gu[:, h % 2, :], row_one[:, h:h + 1].broadcast_to([SSD_H, P]),
                                      row.rearrange("p d l -> p (d l)"), start=q == 0, stop=q == 1)
                    m.then_inc(rows_psum, 1)

                pe.wait_ge(row_split, 1)
                log_rows(0)
                correlations(0)
                log_rows(1)
                for h in range(SSD_H):
                    if h % HPG == 0 and h // HPG + 1 < SSD_G:
                        correlations(h // HPG + 1)
                    if h + 2 < SSD_H:
                        log_rows(h + 2)
                    outputs(h)
                pe.wait_ge(y_taken, 1)
                for k in range(2):
                    down_slot(n0 + 23 + k, hT_hi, hT_lo, k, range(TT), k == 0, False)
                for t in range(TT):
                    pe.wait_ge(y_ready, t + 1)
                    for i in range(SSD_W // P):
                        o = tp[:, t, i * P:(i + 1) * P] if i < 4 else gu[:, t, (i - 4) * P:(i - 3) * P]
                        m = pe.transpose(o, y_sum[:, t, i * P:(i + 1) * P], ident[:])
                        if i in (3, 5):
                            m.then_inc(mixT_psum, 1)
                out_proj(n0 + 25, range(2, KT), [MIX0["ssd"] + MIX_SSD] * KT, first=False)

            pe.wait_ge(consts, 16)
            for s, name in enumerate(SUB):
                if s and s not in EARLY:
                    if s == 1:
                        pe.wait_ge(ada_out, ADA_CH)
                    keep_warm(WARM)
                {"ctx_mix": ctx_mix, "ab": ab, "sc": sc, "ssd": ssd}.get(name, ffn)(s, BASE[name])

        @block.scalar
        def _(act):
            def copy(o, i, done, **kw):
                act.activation(o, i, ACT.Copy, **kw).then_inc(done, 1)

            def upper(n, it=0):
                if n >= NSLOT:
                    return
                slot_landed(act, n, it)
                if n >= RING:
                    act.wait_ge(slot_used, n - RING + 1 + RING * it)
                copy(w_hi[:, n % RING, :], raw[:, n % RING, :], hi_ready)

            def after_slots(n, count, it=0):
                for q in range(count):
                    upper(n + q + RING, it)

            def out_squares(s):
                factor = 0.5 if s in FFNS else 1.0
                for t in range(TT):
                    for half in range(2):
                        if t == 0 or half == 0:
                            act.wait_ge(first_tok, FIRST_N["dn", s] - 2 + 2 * t + half)
                        else:
                            act.wait_ge(slot_used, LAST[s])
                        c = half_of(half)
                        act.activation(xn[:, t, c], dn[:, t, c], ACT.Square, scale=1.0 / (factor * D ** 0.5),
                                       accum_out=ssq[:, 2 + t, half:half + 1]).then_inc(ssq_ready, 1)

            def in_squares(s, tiles=range(TT)):
                for t in tiles:
                    for half in range(2):
                        if SOURCE[s] is not None:
                            act.wait_ge(x_new, X_NEW_N[SOURCE[s]] - 2 * TT + 2 * t + half + 1)
                        else:
                            act.wait_ge(ctx_loaded if s in CTX else x_loaded, 16)
                        c = half_of(half)
                        act.activation(xn[:, t, c], stream_of(s)[:, t, c], ACT.Square, scale=1.0 / D ** 0.5,
                                       accum_out=ssq[:, t, half:half + 1]).then_inc(ssq_ready, 1)

            def in_upper(s, tiles=range(TT)):
                for t in tiles:
                    for half in range(2):
                        act.wait_ge(hT_psum, 2 * (TT * s + t) + half + 1)
                        copy(hT_hi[:, 4 * half:4 * half + 4, t * P:(t + 1) * P],
                             in_bank(s, t, half).rearrange("p (k c) -> p k c", k=4), hT_hi_ready)

            def ada_lower(n, m, r=0):
                act.wait_ge(slot_used, n + RING * r)
                if 0 < m < ADA_FIRST:
                    act.wait_ge(ada_out, m)
                copy(mod_low, ada_bank(m)[LOW:LOW + 2, :], ada_low)

            def ffn(s, n0):
                c0 = FFNS.index(s) * STEPS

                def act_upper(c, it=0, o=actT_hi, bank=tp[:, 0, :]):
                    act.wait_ge(actT_psum, c + 1 + it)
                    copy(o[:, 0:2, :], bank.rearrange("p (k c) -> p k c", k=2), actT_hi_ready)

                def gate(t):
                    act.activation(silu[:, t, :], gu[:, t, 0:FS], ACT.Silu).then_inc(silu_ready, 1)

                def gates(n, r=0):
                    act.wait_ge(slot_used, n + 4 + RING * r)
                    gate(0)
                    gate(1)

                def step(j, it=0):
                    n = n0 + 4 + 6 * (j - 1)
                    act_upper(c0 + j - 1, it)
                    after_slots(n, 3, it)
                    gates(n, it)
                    if s == TAIL and j == 1:
                        context_states()
                    if j == STEPS - 1 and s + 1 in READY:
                        in_upper(s + 1, [0])
                        after_slots(n + 3, 3)
                        act_upper(c0 + STEPS - 1, bank=gu[:, 0, :])
                        in_upper(s + 1, [1])
                    elif j == STEPS - 1:
                        after_slots(n + 3, 2)
                        act_upper(c0 + STEPS - 1, o=last_act(s)[0])
                        after_slots(n + 5, 1)
                    else:
                        after_slots(n + 3, 3, it)

                def steps_with_ada(n, j, it=0):
                    r, i2 = 4 * it, 2 * it
                    after_slots(n, 3, r)
                    gates(n, r)
                    after_slots(n + 3, 4, r)
                    ada_lower(n + 8, ADA_FIRST, r)
                    after_slots(n + 7, 3, r)
                    act_upper(c0 + j, i2)
                    after_slots(n + 10, 3, r)
                    gates(n + 10, r)
                    after_slots(n + 13, 4, r)
                    ada_lower(n + 18, ADA_FIRST, r)
                    after_slots(n + 17, 3, r)
                    act_upper(c0 + j + 1, i2)
                    after_slots(n + 20, 3, r)
                    ada_lower(n + 24, ADA_FIRST, r)
                    after_slots(n + 23, 1, r)

                if s in READY:
                    after_slots(n0, 3)
                    gates(n0)
                else:
                    act.wait_ge(first_tok, FIRST_N["gu", s])
                    gate(0)
                    after_slots(n0, 3)
                    act.wait_ge(slot_used, n0 + 4)
                    gate(1)
                after_slots(n0 + 3, 1)
                if s == TAIL:
                    context_b_tokens()
                if s == 0:
                    for m in range(ADA_FIRST):
                        if m == ADA_FIRST - 1:
                            act_upper(c0)
                        after_slots(n0 + 4 + 4 * m, 4)
                        ada_lower(n0 + 8 + 4 * m, m)
                    steps_with_ada(n0 + 16, 1)
                    with act.Fori(0, STEPS // 2 - 1) as it:
                        steps_with_ada(n0 + 40, 3, it)
                else:
                    step(1)
                    with act.Fori(0, STEPS - 3) as it:
                        step(2, it)
                    if s + 1 in READY:
                        in_squares(s + 1)
                    step(STEPS - 1)

            def lru_gates():
                for g, o in enumerate((rgate, igate)):
                    act.wait_ge(gates_done, g + 1)
                    for i in range(LT):
                        act.activation(o[:, i, :], dn[:, g, i * TOK:(i + 1) * TOK], ACT.Sigmoid,
                                       bias=lru_cols[:, i, 5 + g:6 + g]).then_inc(gates_ready, 1)
                act.wait_ge(lru_c_ready, 1)
                act.wait_ge(gates_ready, LT)
                for i in range(LT):
                    act.activation(th[:, i, :], rgate[:, i, :], ACT.Tanh, scale=lru_tmp[:, 6, i:i + 1]).then_inc(lru_tanh, 1)
                for i in range(LT):
                    act.activation(decay[:, i, :], rgate[:, i, :], ACT.Exp, scale=lru_tmp[:, 7, i:i + 1]).then_inc(lru_decay, 1)

            def ab(s, n0):
                act.wait_ge(late_consts, ALL_LATE)
                act.wait_ge(lam_z, 1)
                act.activation(lru_tmp[:, 1, :], lru_tmp[:, 1, :], ACT.Exp).then_inc(lam_exp, 1)
                after_slots(n0, 4)
                act.wait_ge(slot_used, n0 + 4)
                for t in range(TT):
                    copy(qk[:, t, 0:HEADS, :], gu[:, t, :].rearrange("p (h d) -> p h d", h=HEADS), ab_evac, scale=HD ** -0.5)
                act.wait_ge(ada_stored, 16 * (ADA_CH // ADA_FIRST))
                for pair in range(2):
                    after_slots(n0 + 4 + 2 * pair, 2)
                    act.wait_ge(slot_used, n0 + 4 + 2 * pair + 2)
                    copy(lx[:, 2 * pair:2 * pair + 2, LRU_CONV - 1:],
                         dn[:, 0, pair * 512:(pair + 1) * 512].rearrange("p (i c) -> p i c", i=2), ab_evac)
                for pair in range(2):
                    after_slots(n0 + 8 + 2 * pair, 2)
                    act.wait_ge(slot_used, n0 + 8 + 2 * pair + 2)
                    act.activation(gelu[:, 2 * pair:2 * pair + 2, :],
                                   dn[:, 1, pair * 512:(pair + 1) * 512].rearrange("p (i c) -> p i c", i=2),
                                   ACT.Gelu_apprx_tanh).then_inc(ab_evac, 1)
                after_slots(n0 + 12, 1)
                lru_gates()
                after_slots(n0 + 13, 3)
                act.wait_ge(slot_used, n0 + 16)
                for t in range(TT):
                    copy(qk[:, t, HEADS:2 * HEADS, :], tp[:, t, :].rearrange("p (h d) -> p h d", h=HEADS), ab_evac)
                after_slots(n0 + 16, 4)
                act.wait_ge(slot_used, n0 + 20)
                for t in range(TT):
                    copy(vtok[:, t, :], gu[:, t, :], ab_evac)
                for which, bank in enumerate((tp, gu)):
                    for half in range(2):
                        act.wait_ge(qkT_psum, 2 * which + half + 1)
                        k = HEADS // 2 * which + 2 * half
                        copy(hT_hi[:, k:k + 2, :], bank[:, half, :].rearrange("p (a c) -> p a c", a=2), qkT_hi)
                act.wait_ge(lru_ratio, 1)
                act.activation(th[:, :, :], th[:, :, :], ACT.Sqrt).then_inc(lru_root, 1)

                def turned(h):
                    act.wait_ge(expT_psum, h + 1)
                    copy(expT[:, h % 2, :], dn[:, 0, (h % 2) * 512:(h % 2) * 512 + 3 * P], expT_ready)

                for h in range(HEADS):
                    act.wait_ge(masked_ready, 3 * h + 3)
                    act.activation(expo[:, h % 2, 0:P], masked[:, h % 2, 0:P], ACT.Exp,
                                   bias=soft[:, 1, h, 0:1], accum_out=soft[:, 2, h, 0:1])
                    act.activation(expo[:, h % 2, P:3 * P], masked[:, h % 2, P:3 * P], ACT.Exp,
                                   bias=soft[:, 1, h, 1:2], accum_out=soft[:, 2, h, 1:2]).then_inc(exp_ready, 1)
                    if h:
                        turned(h - 1)
                turned(HEADS - 1)
                act.wait_ge(rec_ready, 1)
                copy(hT_hi[:, 4:8, :], gelu[:, :, :], mix_hi)
                for t in range(TT):
                    act.wait_ge(mixT_psum, t + 1)
                    copy(hT_hi[:, 0:4, t * P:(t + 1) * P], tp[:, t, :].rearrange("p (k c) -> p k c", k=4), mix_hi)
                after_slots(n0 + 20, 6)

            def sc(s, n0):
                for i in range(KT):
                    act.wait_ge(slot_used, n0 + 3 * i + 1)
                    if i >= 2:
                        act.wait_ge(sc_mixed, 2 * (i - 2) + 1)
                    copy(cgate[:, i % 2, 0:TOK], any_bank(3 * i % 8)[:, 0:TOK], sc_gate)
                    if i < KT - 1:
                        after_slots(n0 + 3 * i, 3)
                    if i == 4 and s + 1 in EARLY:
                        in_squares(s + 1)
                act.wait_ge(slot_used, n0 + 3 * KT)
                for half in range(2):
                    act.wait_ge(sc_mixed, 8 * half + 8)
                    copy(hT_hi[:, 4 * half:4 * half + 4, :], conv_y[:, 4 * half:4 * half + 4, :], mix_hi)
                after_slots(n0 + 3 * KT - 3, 3 + KT - 2)

            def dt_and_conv(turn, n0, pairs, pair0, tile0):
                if turn == 0:
                    act.activation(neg_a[:], ssd_rows[:, NDT:2 * NDT], ACT.Exp).then_inc(a_exp, 1)
                after_slots(n0, 1)
                act.wait_ge(dt_z, turn + 1)
                act.activation(dt_tmp[:, 1, :], dt_tmp[:, 1, :], ACT.Exp).then_inc(dt_exp, 1)

                def convolved(p):
                    act.wait_ge(conv_done, pair0 + p + 1)
                    for q in range(2):
                        i = tile0 + 2 * p + q
                        m = act.activation(xbc[:, i, :], xbc[:, i, :], ACT.Silu, bias=ssd_cols[:, i, 3:4])
                    m.then_inc(xbc_ready, 1)

                for p in range(pairs):
                    n = n0 + 1 + 2 * p
                    after_slots(n, 2)
                    act.wait_ge(slot_used, n + 2)
                    i = tile0 + 2 * p
                    copy(xbc_in[:, i:i + 2, 1:1 + TOK], xbc_bank(turn, p).rearrange("p (i c) -> p i c", i=2), xbc_evac)
                    if turn == 0 and p == pairs - 1:
                        in_upper(TAIL, [0])
                    if p:
                        convolved(p - 1)
                    if p == 2:
                        act.wait_ge(p_psum, turn + 1)
                        if turn == 0:
                            copy(pcol[:, :, :], tp[:, 1, 0:3 * NDT].rearrange("p (t h) -> p t h", t=3), p_ready)
                        else:
                            act.activation(pcol[:, 0:2, :], tp[:, 1, 0:2 * NDT].rearrange("p (t h) -> p t h", t=2), ACT.Copy)
                            copy(prow[:, :, :], gu[0:SSD_H, :, 0:TOK], p_ready)
                    if p == 2 and turn == 0:
                        in_squares(TAIL)
                if turn == 0:
                    act.wait_ge(p_arg, 1)
                    act.activation(exp_p[:, :, :], exp_p[:, :, :], ACT.Exp).then_inc(p_exp, 1)
                    x_tokens(0)
                convolved(pairs - 1)
                if turn == 0:
                    in_upper(TAIL, [1])

            def x_tokens(turn):
                act.wait_ge(tokT_psum, 2 * turn + 1)
                for t in range(TT):
                    copy(xs_tok[:, t, :], x_cols[:, t * SSD_W:(t + 1) * SSD_W], tok_ready)

            def ctx_mix(s, n0):
                dt_and_conv(0, n0, 5, 0, XS_T)

            def context_b_tokens():
                act.wait_ge(tokT_psum, 2)
                for t, bank in enumerate((x_cols[:, TT * SSD_W:], tp[:, 1, :])):
                    copy(bm_tok[:, t, :], bank, tok_ready)

            def context_states():
                for d in range(2):
                    act.wait_ge(state_psum, d + 1)
                    copy(state0[:, d, :, :], dn[:, d, :].rearrange("p (g c) -> p g c", g=SSD_G)[:, :, 0:GW], state_ready)

            def ssd(s, n0):
                after_slots(n0, 4)
                act.wait_ge(slot_used, n0 + 4)
                for t in range(TT):
                    act.activation(u_tok[:, t, :], gu[:, t, 0:FOURIER], ACT.Copy)
                    act.activation(z_tok[:, t, 0:256], gu[:, t, FOURIER:512], ACT.Silu).then_inc(wide_ready, 1)
                dt_and_conv(1, n0 + 4, 7, 5, 0)
                act.wait_ge(p_ready, 2)
                act.activation(exp_p[:, :, :], pcol[:, 0:2, :], ACT.Exp).then_inc(p_exp, 1)
                act.wait_ge(four_psum, 1)
                copy(f_mid[:, :, :, :], gu[:, :, :].rearrange("p m (f c) -> p m f c", f=2), four_ready)
                after_slots(n0 + 19, 4)
                act.wait_ge(slot_used, n0 + 23)
                for t in range(TT):
                    act.activation(z_tok[:, t, 256:SSD_W], tp[:, t, :], ACT.Silu).then_inc(wide_ready, 1)
                x_tokens(1)
                copy(row_one, ident[0:SSD_H, 0:SSD_H], row_split_hi)
                copy(row_hi, prow[:, :, :], row_split_hi)
                act.wait_ge(four_psum, 2)
                copy(f_T[:, :, :], gu[:, 0, :].rearrange("p (f c) -> p f c", f=2), four_ready)
                act.wait_ge(four_psum, 3)
                copy(hT_hi[:, 0:2, :], gu[:, 1, :].rearrange("p (f c) -> p f c", f=2), mix_hi)
                def arguments(h):
                    act.wait_ge(rows_psum, h + 1)
                    if h >= 3:
                        act.wait_ge(y_psum, h - 2)
                    w, b = decays[h % 3], gu[:, h % 2, :]
                    for at, c, d, st in ((0, slice(0, 256), 0, 0), (256, slice(128, 256), 0, 1),
                                         (384, slice(256, 384), 1, 0), (512, slice(256, 512), 1, 1)):
                        m = act.activation(w[:, at:at + c.stop - c.start], b[:, c], ACT.Relu,
                                           bias=pcol[:, st, d * SSD_H + h:d * SSD_H + h + 1], scale=-1.0)
                    m.then_inc(arg_ready, 1)

                arguments(0)
                for h in range(SSD_H):
                    act.wait_ge(arg_ready, h + 1)
                    act.activation(decays[h % 3], decays[h % 3], ACT.Exp, scale=-1.0).then_inc(dec_ready, 1)
                    if h + 1 < SSD_H:
                        arguments(h + 1)
                for t in range(TT):
                    act.wait_ge(y_gated, t + 1)
                    for g in range(SSD_G):
                        c = slice(g * GW, (g + 1) * GW)
                        m = act.activation(y_acc[:, t, c], y_sum[:, t, c], ACT.Square, scale=GW ** -0.5,
                                           accum_out=gstat[:, 0, t * SSD_G + g:t * SSD_G + g + 1])
                    m.then_inc(gsq_ready, 1)
                for t in range(TT):
                    c = slice(t * P, (t + 1) * P)
                    act.wait_ge(mixT_psum, 2 + 2 * t + 1)
                    copy(hT_hi[:, 2:6, c], tp[:, t, :].rearrange("p (k c) -> p k c", k=4), mix_hi)
                    act.wait_ge(mixT_psum, 2 + 2 * t + 2)
                    copy(hT_hi[:, 6:8, c], gu[:, t, 0:TOK].rearrange("p (k c) -> p k c", k=2), mix_hi)
                after_slots(n0 + 23, 6)

            act.dma_start(ident[:], small["ident"]).then_inc(consts, 16)
            act.dma_start(c_cols[:], small["c_cols"]).then_inc(c_loaded, 16)
            in_squares(0)
            act.wait_ge(c_loaded, 16)
            act.activation(silu_c[:], c_cols[:], ACT.Silu).then_inc(c_ready, 1)
            upper(0)
            in_upper(0, [0])
            upper(1)
            upper(2)
            in_upper(0, [1])
            for n in range(3, RING):
                upper(n)
            for s, name in enumerate(SUB):
                if s in EARLY and s not in READY and s != TAIL:
                    in_upper(s)
                if s:
                    if s in EARLY and s - 1 in WITH_POST:
                        out_squares(s - 1)
                    after_slots(LAST[s - 1] - LEFT[s - 1], LEFT[s - 1])
                {"ctx_mix": ctx_mix, "ab": ab, "sc": sc, "ssd": ssd}.get(name, ffn)(s, BASE[name])
                if s in WITH_POST and s + 1 not in EARLY:
                    out_squares(s)
                    if s + 1 < len(SUB):
                        for t in range(TT):
                            in_squares(s + 1, [t])
                            in_upper(s + 1, [t])

        @block.vector
        def _(dve):
            steps = [0]

            def then(ins):
                steps[0] += 1
                ins.then_inc(dve_step, 1)
                dve.wait_ge(dve_step, steps[0])

            def rest(n, it=0):
                if n >= NSLOT:
                    return
                dve.wait_ge(hi_ready, n + 1 + RING * it)
                r = n % RING
                dve.tensor_tensor(w_lo[:, r, :], raw[:, r, :], w_hi[:, r, :].bitcast(F32),
                                  ALU.subtract).then_inc(lo_ready, 1)

            def after_slots(n, count, it=0):
                for q in range(count):
                    rest(n + q + RING, it)

            def lower(o, i, hi, done):
                dve.tensor_tensor(o, i, hi.bitcast(F32), ALU.subtract).then_inc(done, 1)

            def post_normalised(s, t, half):
                dve.wait_ge(rstd_ready, NORM_N["post", s, t])
                if s in MOD:
                    dve.wait_ge(post_mod, POST_MOD_N[s])
                else:
                    dve.wait_ge(row_post, POST_DMA_N[s])
                c = half_of(half)
                then(dve.scalar_tensor_tensor(xn[:, t, c], dn[:, t, c], rstd[:, 2 + t:3 + t], post_row[:, c],
                                              ALU.mult, ALU.mult))

            def added(s, t, half):
                xt = stream_of(s)[:, t, half_of(half)]
                dve.tensor_tensor(xt, xt, xn[:, t, half_of(half)], ALU.add).then_inc(x_new, 1)

            def residual(s, tiles=range(TT)):
                for t in tiles:
                    for half in range(2):
                        post_normalised(s, t, half)
                        added(s, t, half)

            def to_next(s):
                residual(s, [0])
                for half in range(2):
                    post_normalised(s, 1, half)
                normalised(s + 1, [0])
                for half in range(2):
                    added(s, 1, half)
                in_lower(s + 1, [0])
                normalised(s + 1, [1])
                in_lower(s + 1, [1])

            def normalised(s, tiles=range(TT)):
                for t in tiles:
                    dve.wait_ge(rstd_ready, NORM_N["pre", s, t])
                    if s in MOD:
                        dve.wait_ge(pre_mod, PRE_MOD_N[s])
                    else:
                        dve.wait_ge(row_pre, PRE_DMA_N[s])
                    for half in range(2):
                        c = half_of(half)
                        m = dve.scalar_tensor_tensor(xn[:, t, c], stream_of(s)[:, t, c], rstd[:, t:t + 1], pre_row[:, c],
                                                     ALU.mult, ALU.mult)
                        if s in MOD:
                            then(m)
                            m = dve.tensor_tensor(xn[:, t, c], xn[:, t, c], shift_row[:, c], ALU.add)
                        m.then_inc(xn_ready, 1)

            def in_lower(s, tiles=range(TT)):
                for t in tiles:
                    for half in range(2):
                        c = (slice(None), slice(4 * half, 4 * half + 4), slice(t * P, (t + 1) * P))
                        dve.wait_ge(hT_hi_ready, 2 * (TT * s + t) + half + 1)
                        lower(hT_lo[c], in_bank(s, t, half).rearrange("p (k c) -> p k c", k=4), hT_hi[c], hT_lo_ready)

            def log1p(tiles):
                u, s1, s2, acc = tiles
                then(dve.tensor_scalar(s1, u, 2.0, None, ALU.add))
                then(dve.reciprocal(s2, s1))
                then(dve.tensor_tensor(s1, u, s2, ALU.mult))
                then(dve.tensor_tensor(s2, s1, s1, ALU.mult))
                then(dve.tensor_scalar(acc, s2, 1.0 / 17, None, ALU.mult))
                for k in range(15, 2, -2):
                    then(dve.scalar_tensor_tensor(acc, acc, 1.0 / k, s2, ALU.add, ALU.mult))
                then(dve.scalar_tensor_tensor(acc, acc, 1.0, s1, ALU.add, ALU.mult))

            def split_c():
                dve.wait_ge(c_ready, 1)
                dve.wait_ge(halves, 2)
                for v in range(2):
                    then(dve.tensor_copy(c_split[:, :, v], silu_c[:, v, :]))
                    m = dve.tensor_tensor(c_split[:, :, LOW + v], silu_c[:, v, :], c_split[:, :, v].bitcast(F32), ALU.subtract)
                m.then_inc(c_split_ready, 1)

            def ada_sum(m, group, it=0):
                dve.wait_ge(ada_low, m + 1 + ADA_FIRST * it)
                if group:
                    dve.wait_ge(ada_biased, group + it)
                at = m % ADA_FIRST * 512
                dve.tensor_tensor(mod_sum[:, at:at + 512], ada_bank(m)[0:2, :], mod_low, ALU.add).then_inc(ada_out, 1)

            def ffn(s, n0):
                c0 = FFNS.index(s) * STEPS

                def act_lower(c, it=0, o=(actT_hi, actT_lo), bank=tp[:, 0, :]):
                    dve.wait_ge(actT_hi_ready, c + 1 + it)
                    lower(o[1][:, 0:2, :], bank.rearrange("p (k c) -> p k c", k=2), o[0][:, 0:2, :], actT_lo_ready)

                def gated(c, t, it=0):
                    dve.wait_ge(silu_ready, TT * c + t + 1 + TT * it)
                    dve.tensor_tensor(act_tok[:, t, :], silu[:, t, :], gu[:, t, FS:512], ALU.mult).then_inc(act_ready, 1)

                def gates(c, it=0):
                    gated(c, 0, it)
                    gated(c, 1, it)

                def step(j, it=0):
                    n = n0 + 4 + 6 * (j - 1)
                    act_lower(c0 + j - 1, it)
                    after_slots(n, 3, it)
                    gates(c0 + j, it)
                    if j == STEPS - 1 and s + 1 in READY:
                        in_lower(s + 1, [0])
                        after_slots(n + 3, 3)
                        act_lower(c0 + STEPS - 1, bank=gu[:, 0, :])
                        in_lower(s + 1, [1])
                    elif j == STEPS - 1:
                        after_slots(n + 3, 2)
                        act_lower(c0 + STEPS - 1, o=last_act(s))
                        after_slots(n + 5, 1)
                    else:
                        after_slots(n + 3, 3, it)

                def steps_with_ada(n, j, m, it=0):
                    r, i2, group = 4 * it, 2 * it, m // ADA_FIRST
                    after_slots(n, 3, r)
                    gates(c0 + j, i2)
                    after_slots(n + 3, 4, r)
                    ada_sum(m, group, it)
                    after_slots(n + 7, 3, r)
                    act_lower(c0 + j, i2)
                    after_slots(n + 10, 3, r)
                    gates(c0 + j + 1, i2)
                    after_slots(n + 13, 4, r)
                    ada_sum(m + 1, group, it)
                    after_slots(n + 17, 3, r)
                    act_lower(c0 + j + 1, i2)
                    after_slots(n + 20, 3, r)
                    ada_sum(m + 2, group, it)
                    after_slots(n + 23, 1, r)

                if s in READY:
                    after_slots(n0, 2)
                    gates(c0)
                    after_slots(n0 + 2, 2)
                else:
                    gated(c0, 0)
                    after_slots(n0, 3)
                    gated(c0, 1)
                    after_slots(n0 + 3, 1)
                if s == TAIL:
                    dve.wait_ge(p_exp, 1)
                    then(dve.tensor_tensor(exp_p[:, :, :], exp_p[:, :, :], dt[:, :, :], ALU.mult))
                    dve.wait_ge(tok_ready, TT)
                    x_times(exp_p)
                if s == 0:
                    for m in range(ADA_FIRST):
                        if m == ADA_FIRST - 1:
                            act_lower(c0)
                        after_slots(n0 + 4 + 4 * m, 4)
                        ada_sum(m, 0)
                    steps_with_ada(n0 + 16, 1, ADA_FIRST)
                    with dve.Fori(0, STEPS // 2 - 1) as it:
                        steps_with_ada(n0 + 40, 3, 2 * ADA_FIRST, it)
                else:
                    step(1)
                    with dve.Fori(0, STEPS - 3) as it:
                        step(2, it)
                    if s + 1 in READY:
                        normalised(s + 1)
                    step(STEPS - 1)

            def ab(s, n0):
                dve.wait_ge(late_consts, ALL_LATE)
                lam = lru_cols[:, :, 7]
                then(dve.tensor_scalar(lru_tmp[:, 0, :], lam, -1.0, None, ALU.mult))
                dve.tensor_tensor(lru_tmp[:, 1, :], lam, lru_tmp[:, 0, :], ALU.min).then_inc(lam_z, 1)
                dve.wait_ge(lam_exp, 1)
                log1p([lru_tmp[:, q, :] for q in (1, 2, 3, 4)])
                then(dve.tensor_scalar(lru_tmp[:, 5, :], lru_tmp[:, 0, :], 0.0, None, ALU.max))
                then(dve.scalar_tensor_tensor(lru_tmp[:, 5, :], lru_tmp[:, 4, :], 2.0, lru_tmp[:, 5, :], ALU.mult, ALU.add))
                dve.tensor_scalar(lru_tmp[:, 6, :], lru_tmp[:, 5, :], LRU_C, None, ALU.mult)
                dve.tensor_scalar(lru_tmp[:, 7, :], lru_tmp[:, 5, :], -LRU_C, None, ALU.mult).then_inc(lru_c_ready, 1)
                after_slots(n0, 4)
                dve.wait_ge(ada_stored, 16 * (ADA_CH // ADA_FIRST))
                then(dve.memset(lx[:, :, 0:LRU_CONV - 1], 0.0))
                after_slots(n0 + 4, 4)
                dve.wait_ge(ab_evac, 4)
                for j in range(LRU_CONV):
                    for i in range(LT):
                        src, w = lx[:, i, j:j + TOK], lru_cols[:, i, j:j + 1]
                        if j == 0:
                            m = dve.tensor_scalar(xc[:, i, :], src, w, lru_cols[:, i, 4:5], ALU.mult, ALU.add)
                        else:
                            m = dve.scalar_tensor_tensor(xc[:, i, :], src, w, xc[:, i, :], ALU.mult, ALU.add)
                    if j < LRU_CONV - 1:
                        then(m)
                    else:
                        m.then_inc(xc_ready, 1)
                after_slots(n0 + 8, 5)
                dve.wait_ge(lru_decay, LT)
                then(dve.tensor_tensor(rgate[:, :, :], decay[:, :, :], decay[:, :, :], ALU.mult))
                dve.scalar_tensor_tensor(th[:, :, :], rgate[:, :, :], 1.0, th[:, :, :], ALU.add, ALU.mult).then_inc(lru_ratio, 1)
                after_slots(n0 + 13, 3)
                then(dve.tensor_tensor(igate[:, :, :], igate[:, :, :], xc[:, :, :], ALU.mult))
                dve.wait_ge(ab_evac, 8)
                half = [qk[:, :, :, q * HALF_ROT:(q + 1) * HALF_ROT] for q in range(2)]
                turn = [rope[:, :, q, :].unsqueeze(2).broadcast_to([P, TT, 2 * HEADS, HALF_ROT]) for q in range(2)]
                tmp = [v.rearrange("p (n t h d) -> p n t h d", n=2, t=TT, h=2 * HEADS) for v in (rope_t, rope_u)]
                for q in range(2):
                    for c in range(2):
                        m = dve.tensor_tensor(tmp[q][:, c], half[q], turn[c], ALU.mult)
                then(m)
                dve.tensor_tensor(half[0], tmp[0][:, 0], tmp[1][:, 1], ALU.subtract)
                dve.tensor_tensor(half[1], tmp[1][:, 0], tmp[0][:, 1], ALU.add).then_inc(roped, 1)
                for which, bank in enumerate((tp, gu)):
                    for half in range(2):
                        k = HEADS // 2 * which + 2 * half
                        dve.wait_ge(qkT_hi, 2 * which + half + 1)
                        lower(hT_lo[:, k:k + 2, :], bank[:, half, :].rearrange("p (a c) -> p a c", a=2), hT_hi[:, k:k + 2, :], qkT_lo)

                def recurrence():
                    dve.wait_ge(lru_root, 1)
                    then(dve.tensor_tensor(igate[:, :, :], igate[:, :, :], th[:, :, :], ALU.mult))
                    for i in range(LT):
                        m = dve.tensor_tensor_scan(rgate[:, i, :], decay[:, i, :], igate[:, i, :], 0.0, ALU.mult, ALU.add)
                    then(m)
                    dve.tensor_tensor(gelu[:, :, :], gelu[:, :, :], rgate[:, :, :], ALU.mult).then_inc(rec_ready, 1)

                for h in range(HEADS):
                    if h == 4:
                        recurrence()
                    bank = (gu, tp)[(h // 2) % 2][:, h % 2, :]
                    dve.wait_ge(scores_done, h + 1)
                    if h >= 2:
                        dve.wait_ge(exp_ready, h - 1)
                    for t, c in enumerate((slice(0, P), slice(P, 3 * P))):
                        dve.tensor_tensor_reduce(masked[:, h % 2, c], bank[:, c], causal[:, c], 1.0, -3.0e38,
                                                 ALU.add, ALU.max, soft[:, 0, h, t:t + 1]).then_inc(masked_ready, 1)
                    dve.wait_ge(masked_ready, 3 * h + 2)
                    dve.tensor_scalar(soft[:, 1, h, :], soft[:, 0, h, :], -1.0, None, ALU.mult).then_inc(masked_ready, 1)
                    if h < 4:
                        after_slots(n0 + 16 + h, 1)
                dve.wait_ge(mix_hi, 1)
                lower(hT_lo[:, 4:8, :], gelu[:, :, :], hT_hi[:, 4:8, :], mix_lo)
                dve.wait_ge(exp_ready, HEADS)
                then(dve.reciprocal(soft[:, 3, :, :], soft[:, 2, :, :]))
                dve.wait_ge(attn_psum, 1)
                for t in range(TT):
                    m = dve.tensor_tensor(attn[:, t, :].rearrange("p (h d) -> p h d", h=HEADS),
                                          dn[:, 1, t * 512:(t + 1) * 512].rearrange("p (h d) -> p h d", h=HEADS),
                                          soft[:, 3, :, t].unsqueeze(2).broadcast_to([P, HEADS, HD]), ALU.mult)
                m.then_inc(attn_ready, 1)
                for t in range(TT):
                    c = (slice(None), slice(0, 4), slice(t * P, (t + 1) * P))
                    dve.wait_ge(mix_hi, 2 + t)
                    lower(hT_lo[c], tp[:, t, :].rearrange("p (k c) -> p k c", k=4), hT_hi[c], mix_lo)
                after_slots(n0 + 20, 6)

            def sc(s, n0):
                then(dve.memset(cx[:, :, 0:SC_CONV - 1], 0.0))
                for i in range(KT):
                    dve.wait_ge(sc_gate, i + 1)
                    dve.wait_ge(slot_used, n0 + 3 * i + 2)
                    dve.tensor_tensor(cx[:, i, SC_CONV - 1:], cgate[:, i % 2, 0:TOK], any_bank((3 * i + 1) % 8)[:, 0:TOK],
                                      ALU.mult).then_inc(sc_mixed, 1)
                    dve.wait_ge(sc_mixed, 2 * i + 1)
                    for j in range(SC_CONV):
                        src, w = cx[:, i, j:j + TOK], sc_cols[:, i, j:j + 1]
                        if j == 0:
                            then(dve.tensor_scalar(conv_y[:, i, :], src, w, None, ALU.mult))
                        else:
                            then(dve.scalar_tensor_tensor(conv_y[:, i, :], src, w, conv_y[:, i, :], ALU.mult, ALU.add))
                    dve.wait_ge(slot_used, n0 + 3 * i + 3)
                    dve.tensor_tensor(conv_y[:, i, :], conv_y[:, i, :], any_bank((3 * i + 2) % 8)[:, 0:TOK],
                                      ALU.mult).then_inc(sc_mixed, 1)
                    if i < KT - 1:
                        after_slots(n0 + 3 * i, 3)
                    if i == 4 and s + 1 in EARLY:
                        normalised(s + 1)
                for half in range(2):
                    c = (slice(None), slice(4 * half, 4 * half + 4))
                    dve.wait_ge(mix_hi, MIX0["sc"] + half + 1)
                    lower(hT_lo[c], conv_y[c], hT_hi[c], mix_lo)
                after_slots(n0 + 3 * KT - 3, 3 + KT - 2)

            def dt_and_conv(turn, n0, pairs, pair0, tile0, after):
                for edge in (0, TOK + 1):
                    m = dve.memset(xbc_in[:, :, edge:edge + 1], 0.0)
                then(m)
                if turn == 0:
                    dve.wait_ge(a_exp, 1)
                    then(dve.tensor_scalar(neg_a[:], neg_a[:], -1.0, None, ALU.mult))
                after_slots(n0, 1)
                z, u, s1, s2, acc, mz = (dt_tmp[:, q, :] for q in range(6))

                def both(v):
                    return v.rearrange("p (t h) -> p t h", t=TT)

                dve.wait_ge(slot_used, n0 + 1)
                then(dve.tensor_tensor(both(z), both(tp[:, 0, 0:TT * NDT]),
                                       ssd_rows[:, 0:NDT].unsqueeze(1).broadcast_to([P, TT, NDT]), ALU.add))
                then(dve.tensor_scalar(u, z, -1.0, None, ALU.mult))
                dve.tensor_tensor(u, z, u, ALU.min).then_inc(dt_z, 1)
                then(dve.tensor_scalar(mz, z, 0.0, None, ALU.max))
                dve.wait_ge(dt_exp, turn + 1)
                log1p([u, s1, s2, acc])
                then(dve.scalar_tensor_tensor(both(dt[:, :, :].rearrange("p t h -> p (t h)")), both(acc), 2.0, both(mz), ALU.mult, ALU.add))
                dve.tensor_tensor(dta[:, :, :], dt[:, :, :], neg_a[:].unsqueeze(1).broadcast_to([P, TT, NDT]),
                                  ALU.mult).then_inc(dta_ready, 1)
                for p in range(pairs):
                    after_slots(n0 + 1 + 2 * p, 2)
                    if turn == 0 and p == pairs - 1:
                        in_lower(TAIL, [0])
                    dve.wait_ge(xbc_evac, pair0 + p + 1)
                    for j in range(3):
                        for q in range(2):
                            i = tile0 + 2 * p + q
                            src, w = xbc_in[:, i, j:j + TOK], ssd_cols[:, i, j:j + 1]
                            if j == 0:
                                m = dve.tensor_scalar(xbc[:, i, :], src, w, None, ALU.mult)
                            else:
                                m = dve.scalar_tensor_tensor(xbc[:, i, :], src, w, xbc[:, i, :], ALU.mult, ALU.add)
                        if j < 2:
                            then(m)
                        else:
                            m.then_inc(conv_done, 1)
                    if p == 3:
                        after()

            def heads_of(v):
                return v.rearrange("p (h d) -> p h d", d=SSD_P)

            def x_times(w):
                for d in range(2):
                    for t in range(TT):
                        m = dve.tensor_tensor(heads_of(x_dt[d][:, t, :]), heads_of(xs_tok[:, t, :]),
                                              w[:, t, d * SSD_H:(d + 1) * SSD_H].unsqueeze(2).broadcast_to([P, SSD_H, SSD_P]), ALU.mult)
                    m.then_inc(xdt_ready, 1)

            def ctx_mix(s, n0):
                def decay_arguments():
                    dve.wait_ge(p_ready, 1)
                    dve.tensor_tensor(exp_p[:, :, :], pcol[:, 2, :].unsqueeze(1).broadcast_to([P, TT, NDT]),
                                      pcol[:, 0:2, :], ALU.subtract).then_inc(p_arg, 1)
                    normalised(TAIL)

                dt_and_conv(0, n0, 5, 0, XS_T, decay_arguments)
                in_lower(TAIL, [1])

            def ssd(s, n0):
                after_slots(n0, 4)
                dt_and_conv(1, n0 + 4, 7, 5, 0, lambda: None)
                after_slots(n0 + 19, 4)
                dve.wait_ge(tok_ready, 6)
                for t in range(TT):
                    m = dve.tensor_tensor(heads_of(y_acc[:, t, :]), heads_of(xs_tok[:, t, :]),
                                          ssd_rows[:, 2 * NDT:].unsqueeze(2).broadcast_to([P, SSD_H, SSD_P]), ALU.mult)
                then(m)
                dve.wait_ge(row_split_hi, 2)
                lower(row_lo, prow[:, :, :], row_hi, row_split)
                dve.wait_ge(p_exp, 2)
                for g in range(SSD_G):
                    dve.wait_ge(yoff_psum, g + 1)
                    for t in range(TT):
                        w = exp_p[:, t, :].rearrange("p (d h) -> p d h", d=2)[:, :, g * HPG:(g + 1) * HPG]
                        bank, o = ((v[:, t, 0:2 * GW].rearrange("p (d h c) -> p d h c", d=2, h=HPG)) for v in ((tp, gu)[g % 2], y_off))
                        dve.tensor_tensor(o, bank, w.unsqueeze(3).broadcast_to([P, 2, HPG, SSD_P]), ALU.mult).then_inc(yoff_used, 1)
                    if g == 0:
                        dve.wait_ge(mix_hi, MIX0["ssd"] + 1)
                        lower(hT_lo[:, 0:2, :], gu[:, 1, :].rearrange("p (f c) -> p f c", f=2), hT_hi[:, 0:2, :], mix_lo)
                    dve.wait_ge(yoff_used, TT * (g + 1))
                    for d in range(2):
                        for t in range(TT):
                            acc = y_acc[:, t, g * GW:(g + 1) * GW]
                            m = dve.tensor_tensor(acc, acc, y_off[:, t, d * GW:(d + 1) * GW], ALU.add)
                        then(m)

                def masked_cb(g):
                    dve.wait_ge(cb_psum, g + 1)
                    if g:
                        dve.wait_ge(g_ready, HPG * g)
                    cb = tp[:, g % 2, :]
                    dve.tensor_tensor(cb_m[:, 0:256], cb[:, 0:256], tri[:, 0, 0, :], ALU.mult)
                    dve.tensor_tensor(cb_m[:, 256:384], cb[:, 384:512], tri[:, 0, 1, P:], ALU.mult)
                    dve.tensor_tensor(cb_m[:, 384:512], cb[:, 0:128], tri[:, 1, 0, 0:P], ALU.mult)
                    dve.tensor_tensor(cb_m[:, 512:768], cb[:, 256:512], tri[:, 1, 1, :], ALU.mult).then_inc(cb_ready, 1)

                for h in range(SSD_H):
                    if h % HPG == 0:
                        masked_cb(h // HPG)
                    dve.wait_ge(cb_ready, h // HPG + 1)
                    dve.wait_ge(dec_ready, h + 1)
                    w = decays[h % 3]
                    for at, width, d, st in ((0, 256, 0, 0), (256, 128, 0, 1), (384, 128, 1, 0), (512, 256, 1, 1)):
                        c = slice(at, at + width)
                        m = dve.scalar_tensor_tensor(w[:, c], w[:, c], dt[:, st, d * SSD_H + h:d * SSD_H + h + 1], cb_m[:, c],
                                                     ALU.mult, ALU.mult)
                    then(m)
                    forward, backward = (w.rearrange("p (b c) -> p b c", c=P)[:, q:q + 3:2, :] for q in (0, 3))
                    dve.tensor_tensor(forward, forward, backward, ALU.add).then_inc(g_ready, 1)
                dve.wait_ge(y_psum, SSD_H)
                dve.wait_ge(wide_ready, 4)
                for t in range(TT):
                    m = dve.tensor_tensor(y_sum[:, t, :], dn[:, t, 0:SSD_W], y_acc[:, t, :], ALU.add)
                m.then_inc(y_taken, 1)
                dve.wait_ge(y_taken, 1)
                for t in range(TT):
                    dve.tensor_tensor(y_sum[:, t, :], y_sum[:, t, :], z_tok[:, t, :], ALU.mult).then_inc(y_gated, 1)
                for t in range(TT):
                    dve.wait_ge(gr_ready, t + 1)
                    for g in range(SSD_G):
                        c, r = slice(g * GW, (g + 1) * GW), t * SSD_G + g
                        m = dve.scalar_tensor_tensor(y_sum[:, t, c], y_sum[:, t, c], gstat[:, 2, r:r + 1], ssd_norm[:, c],
                                                     ALU.mult, ALU.mult)
                    m.then_inc(y_ready, 1)
                for t in range(TT):
                    c = slice(t * P, (t + 1) * P)
                    dve.wait_ge(mix_hi, MIX0["ssd"] + 2 + 2 * t)
                    lower(hT_lo[:, 2:6, c], tp[:, t, :].rearrange("p (k c) -> p k c", k=4), hT_hi[:, 2:6, c], mix_lo)
                    dve.wait_ge(mix_hi, MIX0["ssd"] + 3 + 2 * t)
                    lower(hT_lo[:, 6:8, c], gu[:, t, 0:TOK].rearrange("p (k c) -> p k c", k=2), hT_hi[:, 6:8, c], mix_lo)
                after_slots(n0 + 23, 6)

            dve.memset(neg_half[:], -0.5).then_inc(halves, 1)
            dve.memset(c_split[:].bitcast(F32), 0.0).then_inc(halves, 1)
            normalised(0)
            split_c()
            rest(0)
            in_lower(0, [0])
            rest(1)
            rest(2)
            in_lower(0, [1])
            for n in range(3, RING):
                rest(n)
            for s, name in enumerate(SUB):
                if s in EARLY and s not in READY and s != TAIL:
                    in_lower(s)
                if s in EARLY and s - 1 in WITH_POST:
                    for t in range(TT):
                        residual(s - 1, [t])
                        if t < LEFT[s - 1]:
                            rest(LAST[s - 1] - LEFT[s - 1] + t + RING)
                elif s:
                    after_slots(LAST[s - 1] - LEFT[s - 1], LEFT[s - 1])
                {"ctx_mix": ctx_mix, "ab": ab, "sc": sc, "ssd": ssd}.get(name, ffn)(s, BASE[name])
                if s + 1 == len(SUB):
                    residual(s)
                elif s in WITH_POST and s + 1 not in EARLY:
                    to_next(s)

        @block.gpsimd
        def _(pool):
            steps = [0]

            def then(ins):
                steps[0] += 1
                ins.then_inc(pool_step, 1)
                pool.wait_ge(pool_step, steps[0])

            def inverse_root(kind, s, t):
                eps = EPS / 0.25 if kind == "post" and s in FFNS else EPS
                c = slice(t + (2 if kind == "post" else 0), t + (2 if kind == "post" else 0) + 1)
                pool.wait_ge(ssq_ready, 2 * NORM_N[kind, s, t] - 1)
                pool.tensor_scalar(ms[:, c], ssq[:, c, 0], eps, None, ALU.add).then_inc(pool_step, 1)
                pool.wait_ge(ssq_ready, 2 * NORM_N[kind, s, t])
                steps[0] += 1
                pool.wait_ge(pool_step, steps[0])
                then(pool.tensor_tensor(ms[:, c], ms[:, c], ssq[:, c, 1], ALU.add))
                pool.tensor_tensor(rstd[:, c], ms[:, c], neg_half[:, 0:1], ALU.pow).then_inc(rstd_ready, 1)

            def mod_vector(v, q):
                return mod[v, q * D:(q + 1) * D].partition_broadcast(P)

            def rows_in(s):
                pool.dma_start(pre_row[:], pre_rows[s, :].partition_broadcast(P)).then_inc(row_pre, 16)
                if s in MOD:
                    v, shift, scale, _ = MOD[s]
                    pool.dma_start(shift_row[:], mod_vector(v, shift)).then_inc(row_pre, 16)
                    pool.dma_start(mod_row[:], mod_vector(v, scale)).then_inc(row_pre, 16)
                    pool.wait_ge(row_pre, PRE_DMA_N[s])
                    then(pool.tensor_scalar(mod_row[:], mod_row[:], 1.0, None, ALU.add))
                    pool.tensor_tensor(pre_row[:], pre_row[:], mod_row[:], ALU.mult).then_inc(pre_mod, 1)
                    pool.wait_ge(pre_mod, PRE_MOD_N[s])

            def rows_out(s):
                pool.dma_start(post_row[:], post_rows[s, :].partition_broadcast(P)).then_inc(row_post, 16)
                if s in MOD:
                    v, _, _, gate = MOD[s]
                    pool.dma_start(mod_row[:], mod_vector(v, gate)).then_inc(row_post, 16)
                    pool.wait_ge(row_post, POST_DMA_N[s])
                    pool.tensor_tensor(post_row[:], post_row[:], mod_row[:], ALU.mult).then_inc(post_mod, 1)
                    pool.wait_ge(post_mod, POST_MOD_N[s])

            def pre_roots(s):
                for t in range(TT):
                    inverse_root("pre", s, t)

            def ada_group(g):
                pool.wait_ge(ada_out, ADA_FIRST * (g + 1))
                if g:
                    pool.wait_ge(ada_stored, 16 * g)
                cols = slice(g * ADA_FIRST * 512, (g + 1) * ADA_FIRST * 512)
                pool.tensor_tensor(mod_out, mod_sum, mod_bias[:, cols], ALU.add).then_inc(ada_biased, 1)
                pool.wait_ge(ada_biased, g + 1)
                pool.dma_start(mod[:, cols], mod_out).then_inc(ada_stored, 16)

            pool.wait_ge(halves, 1)
            rows_in(0)
            pre_roots(0)
            for s, name in enumerate(SUB):
                if s in EARLY and s - 1 in WITH_POST:
                    pool.wait_ge(x_new, X_NEW_N[s - 1])
                if s in WITH_POST:
                    rows_out(s)
                pool.wait_ge(xn_ready, 2 * TT * (s + 1))
                if s == 0:
                    for tile_name, tile in late_tiles.items():
                        source = small[tile_name]
                        if tile_name == "ada_b":
                            source = source[0, :].partition_broadcast(2)
                        pool.dma_start(tile if tile_name in ("ada_b", "gate_bd", "causal") else tile[:], source).then_inc(late_consts, 16)
                    pool.dma_start(ssd_rows[:], small["ssd_rows"][0, :].partition_broadcast(P)).then_inc(late_consts, 16)
                    pool.dma_start(ssd_norm[:], small["ssd_norm"][0, :].partition_broadcast(P)).then_inc(late_consts, 16)
                    pool.wait_ge(late_consts, ALL_LATE)
                    rows_in(1)
                    for g in range(ADA_CH // ADA_FIRST - 1):
                        ada_group(g)
                if s == SOURCE[CTX[0] - 1] + 1:
                    pool.dma_start(ctx_x, ctx_in.rearrange("(t p) d -> p t d", p=P)).then_inc(ctx_loaded, 16)
                if 0 < s < len(SUB) - 1:
                    rows_in(s + 1)
                    if s + 1 in EARLY:
                        pre_roots(s + 1)
                if name == "ssd":
                    for t in range(TT):
                        c = slice(t * SSD_G, (t + 1) * SSD_G)
                        pool.wait_ge(gsq_ready, t + 1)
                        then(pool.tensor_scalar(gstat[:, 1, c], gstat[:, 0, c], EPS, None, ALU.add))
                        pool.tensor_tensor(gstat[:, 2, c], gstat[:, 1, c], neg_half[:, 0:SSD_G], ALU.pow).then_inc(gr_ready, 1)
                if s in WITH_POST:
                    for t in range(TT):
                        inverse_root("post", s, t)
                if s + 1 < len(SUB) and s + 1 not in EARLY:
                    pre_roots(s + 1)
                if s == 0:
                    ada_group(ADA_CH // ADA_FIRST - 1)
                    pool.wait_ge(ada_stored, 16 * (ADA_CH // ADA_FIRST))


def wide(w):
    return w.reshape(KT // 2, 2, P, 512).transpose(0, 2, 1, 3).reshape(KT // 2 * P, SLOT)


def columns(w):
    return w.reshape(KT, P, -1, P).transpose(2, 1, 0, 3).reshape(-1, SLOT)


def narrow(w):
    slot = np.zeros((P, SLOT), np.float32)
    slot[:, :KT * NDT] = w.reshape(KT, P, NDT).transpose(1, 0, 2).reshape(P, KT * NDT)
    return slot


def swiglu_slots(w_gate, w_up, w_down):
    slots = []
    for j in range(STEPS):
        c = slice(j * FS, (j + 1) * FS)
        slots.append(wide(np.concatenate([w_gate[:, c], w_up[:, c]], axis=1)))
        if j:
            slots.append(w_down[(j - 1) * FS:j * FS])
    slots.append(w_down[(STEPS - 1) * FS:])
    return slots


def mixed_columns(w, which):
    return np.concatenate([columns(w[:, c:c + P]) for c in which])


def kernel(x, ffn1_w_gate, ffn1_w_up, ffn1_w_down, ffn2_w_gate, ffn2_w_up, ffn2_w_down, norm_pre,
           norm_post, ab_w_in, ab_w_out, lru_conv_w, lru_conv_b, lru_gate_a_w, lru_gate_a_b,
           lru_gate_x_w, lru_gate_x_b, lru_lambda, c_w_in, c_conv_w, c_w_out, c_2, ctx_2, c_ctx_2,
           ada_w_2, ada_b_2, ffn1_norm_pre_2, ffn1_norm_post_2, ffn1_w_gate_2, ffn1_w_up_2,
           ffn1_w_down_2, mix_norm_pre_2, mix_norm_post_2, w_in_2, fourier_w_2, conv_w_2, conv_b_2,
           dt_bias_2, a_log_2, d_skip_2, ssd_norm_2, w_out_2, ffn2_norm_pre_2, ffn2_norm_post_2,
           ffn2_w_gate_2, ffn2_w_up_2, ffn2_w_down_2):
    first = swiglu_slots(ffn1_w_gate_2[0], ffn1_w_up_2[0], ffn1_w_down_2[0])
    w_in, dt_at = w_in_2[0], 4 * 256 + 512 + SSD_W + 512
    ab, c_in = ab_w_in[0], c_w_in[0]
    ada = [wide(ada_w_2[0][:, 512 * i:512 * (i + 1)]) for i in range(ADA_CH)]
    zero = swiglu_slots(ffn1_w_gate[0], ffn1_w_up[0], ffn1_w_down[0])
    among = [zero[0]] + ada[:ADA_FIRST]
    for i in range(STEPS // 2):
        a, b, c = ada[ADA_FIRST * (i + 1):ADA_FIRST * (i + 2)]
        up_a, down_a, up_b, down_b = zero[4 * i + 1:4 * i + 5]
        among += [up_a, a, down_a, up_b, b, down_b, c]
    among.append(zero[-1])
    phases = {
        "ffn_0": among,
        "ab": [wide(ab[:, 0:512]), columns(ab[:, 1536:2560]), wide(ab[:, 512:1024]), wide(ab[:, 1024:1536])]
        + [ab_w_out[0][512:], ab_w_out[0][:512]],
        "ffn_1": swiglu_slots(ffn2_w_gate[0], ffn2_w_up[0], ffn2_w_down[0]),
        "ctx_ffn": first,
        "ffn_2": swiglu_slots(ffn1_w_gate[1], ffn1_w_up[1], ffn1_w_down[1]),
        "sc": [mixed_columns(c_in, [k * D + i * P for i in range(KT) for k in (1, 2, 0)]), c_w_out[0]],
        "ctx_mix": [narrow(w_in[:, dt_at:]), columns(w_in[:, 1024 + 512:dt_at])],
        "ffn_3": swiglu_slots(ffn2_w_gate[1], ffn2_w_up[1], ffn2_w_down[1]),
        "ffn_4": first,
        "ssd": [wide(w_in[:, :512]), narrow(w_in[:, dt_at:]), columns(w_in[:, 1024:dt_at]), wide(w_in[:, 512:1024]),
                w_out_2[0]],
        "ffn_5": swiglu_slots(ffn2_w_gate_2[0], ffn2_w_up_2[0], ffn2_w_down_2[0]),
    }
    stream = np.concatenate([w for name, _ in PHASES for w in phases[name]])
    assert stream.shape == (NSLOT * P, SLOT)
    norms = {"ffn_0": (norm_pre[0, 0], norm_post[0, 0]), "ab": (norm_pre[0, 1], norm_post[0, 1]),
             "ffn_1": (norm_pre[0, 2], norm_post[0, 2]), "ctx_ffn": (ffn1_norm_pre_2[0], ffn1_norm_post_2[0]),
             "ffn_2": (norm_pre[1, 0], norm_post[1, 0]), "sc": (norm_pre[1, 1], norm_post[1, 1]),
             "ctx_mix": (mix_norm_pre_2[0], mix_norm_post_2[0]), "ffn_3": (norm_pre[1, 2], norm_post[1, 2]),
             "ffn_4": (ffn1_norm_pre_2[0], ffn1_norm_post_2[0]), "ssd": (mix_norm_pre_2[0], mix_norm_post_2[0]),
             "ffn_5": (ffn2_norm_pre_2[0], ffn2_norm_post_2[0])}
    pre, post = (np.stack([norms[name][q] for name in SUB]) for q in range(2))

    def pairs(w):
        bd = np.zeros((P, len(w) // 2, P), np.float32)
        for h in range(len(w)):
            at = slice(HD * (h % 2), HD * (h % 2) + HD)
            bd[at, h // 2, at] = w[h]
        return bd

    def tiles(v):
        return np.moveaxis(v.reshape(*v.shape[:-1], -1, P), (-1, -2), (0, 1))

    lru_cols = np.concatenate([tiles(lru_conv_w[0])] + [tiles(v.reshape(1, LRU_W)) for v in
                              (lru_conv_b[0], lru_gate_a_b[0], lru_gate_x_b[0], lru_lambda[0])], axis=2)
    i = np.arange(P)
    pos = np.arange(TOK)
    angle = pos[:, None] * 500000.0 ** (-np.arange(0, 2 * HALF_ROT, 2) / (2 * HALF_ROT))[None, :]
    diag = np.where(i[None, :] <= i[:, None], 0.0, -1e30)
    turn_l = 2 * np.pi * (np.outer(pos, pos) % TOK) / TOK
    turn_d = 2 * np.pi * (np.outer(np.arange(HD), np.arange(HD)) % HD) / HD
    by_tile = lambda m: m.reshape(TT, P, TOK).transpose(1, 0, 2)
    small_arrays = {
        "ident": np.eye(P),
        "lru_cols": lru_cols,
        "gate_bd": np.stack([pairs(lru_gate_a_w[0]), pairs(lru_gate_x_w[0])], axis=1),
        "rope": np.stack([np.cos(angle), np.sin(angle)], axis=1).reshape(TT, P, 2, HALF_ROT).transpose(1, 0, 2, 3),
        "causal": np.concatenate([diag, np.zeros((P, P)), diag], axis=1),
        "sc_cols": tiles(c_conv_w[0]),
        "ssd_cols": np.concatenate([tiles(conv_w_2[0]), tiles(conv_b_2)], axis=2),
        "tri": np.stack([by_tile(pos[:, None] <= pos[None, :]), by_tile(pos[:, None] >= pos[None, :])], axis=1),
        "dft_l": np.stack([by_tile(np.cos(turn_l) / 16), by_tile(np.sin(turn_l) / 16)], axis=1),
        "dft_d": np.stack([np.kron(np.eye(2), np.cos(turn_d) / 8), np.kron(np.eye(2), -np.sin(turn_d) / 8)], axis=1),
        "fourier_bd": pairs(fourier_w_2[0]),
        "c_cols": np.concatenate([tiles(c_2), tiles(c_ctx_2[None, :])], axis=2).transpose(0, 2, 1),
        "ssd_rows": np.concatenate([dt_bias_2.reshape(1, NDT), a_log_2.reshape(1, NDT), d_skip_2.reshape(1, SSD_H)], axis=1),
        "ssd_norm": ssd_norm_2,
        "ada_b": ada_b_2,
    }

    import concourse.bacc as bacc
    from concourse.bass_utils import run_bass_kernel_spmd

    nc = bacc.Bacc("TRN2", target_bir_lowering=False, num_devices=1)
    arrays = {"weights": stream, "x_in": x[0], "ctx_in": ctx_2[0], "pre_rows": pre, "post_rows": post}
    arrays.update(small_arrays)
    arrays = {name: np.ascontiguousarray(v, dtype=np.float32) for name, v in arrays.items()}
    aps = {name: nc.dram_tensor("in_" + name, v.shape, F32, kind="ExternalInput").ap() for name, v in arrays.items()}
    mod = nc.dram_tensor("mod", [2, N_MOD * D], F32, kind="Internal").ap()
    out = nc.dram_tensor("out", [TOK, D], F32, kind="ExternalOutput").ap()
    build(nc, aps["weights"], aps["x_in"], aps["ctx_in"], aps["pre_rows"], aps["post_rows"],
          {name: aps[name] for name in small_arrays}, mod, out)
    nc.compile()
    results = run_bass_kernel_spmd(nc, [{"in_" + name: v for name, v in arrays.items()}], core_ids=[0])
    return results.results[0]["out"].reshape(1, TOK, D)
```
